# Optimizing a Trainium2 kernel written in Bass

```python
import jax, jax.numpy as jnp
from jax import lax
import numpy as np
import math

D_MODEL = 1024
BATCH = 1
SEQ = 512
DEPTH = 2

N_AB_LAYERS = (DEPTH + 1) // 2
N_C_LAYERS = DEPTH // 2

M_HEADS = 4
M_QK_DIM = 64
M_V_DIM = 128
M_CHUNK = 64
GATE_SOFTCAP = 15.0
G_HEADS = 4
G_K_DIM = 128
G_V_DIM = 128
G_CHUNK = 64
SHORT_CONV = 4
C_HEADS = 8
C_K_DIM = D_MODEL // C_HEADS
C_V_DIM = D_MODEL // C_HEADS
C_CHUNK = 32
D_FF = 2816
FFN_CONV = 3
EPS = 1e-6

M_QK = M_HEADS * M_QK_DIM
M_V = M_HEADS * M_V_DIM
G_QK = G_HEADS * G_K_DIM
G_V = G_HEADS * G_V_DIM
AB_SPLITS = (M_QK, M_QK, M_V, M_V, M_HEADS, M_HEADS, G_QK, G_QK, G_V, G_V, G_HEADS, G_HEADS)
AB_SPLIT_IDX = tuple(int(s) for s in np.cumsum(AB_SPLITS)[:-1])
AB_IN = sum(AB_SPLITS)
AB_MIX = M_V + G_V
C_K_TOTAL = C_HEADS * C_K_DIM
C_MIX = C_HEADS * C_V_DIM
C_IN = 2 * C_K_TOTAL + 2 * C_MIX


def rms_norm(x, gain):
    xf = x.astype(jnp.float32)
    y = xf * lax.rsqrt(jnp.mean(jnp.square(xf), -1, keepdims=True) + EPS)
    return (y * gain.astype(jnp.float32)).astype(x.dtype)

def head_rms_norm(x, gain):
    B, S, H, d = x.shape
    y = x * lax.rsqrt(jnp.mean(jnp.square(x), -1, keepdims=True) + EPS)
    return y.reshape(B, S, H * d) * gain.astype(jnp.float32)

def l2_norm(x):
    return x * lax.rsqrt(jnp.sum(jnp.square(x), -1, keepdims=True) + EPS)

def softcap(x, cap):
    return cap * jnp.tanh(x / cap)

def causal_dwconv(x, w):
    K, C = w.shape
    return lax.conv_general_dilated(
        x, w[:, None, :].astype(x.dtype), window_strides=(1,), padding=[(K - 1, 0)],
        dimension_numbers=("NWC", "WIO", "NWC"), feature_group_count=C)

def to_heads(t, n_heads):
    B, S, C = t.shape
    return t.reshape(B, S, n_heads, C // n_heads)

def to_chunks(t, L):
    B, S, H = t.shape[:3]
    t = t.reshape((B, S // L, L, H) + t.shape[3:])
    return jnp.moveaxis(t, (1, 3), (0, 2))

def from_chunks(t):
    N, B, H, L = t.shape[:4]
    t = jnp.moveaxis(t, (0, 2), (1, 3))
    return t.reshape((B, N * L, H) + t.shape[4:])

def mlstm_chunkwise(q, k, v, i_pre, f_pre):
    B, S, H, DK = q.shape
    DV = v.shape[-1]
    L = M_CHUNK
    q = q * DK ** -0.5
    qc, kc, vc = to_chunks(q, L), to_chunks(k, L), to_chunks(v, L)
    lfc = to_chunks(jax.nn.log_sigmoid(f_pre), L)
    igc = to_chunks(i_pre, L)
    causal = jnp.tril(jnp.ones((L, L), bool))

    def step(carry, inp):
        C, n, m = carry
        q_, k_, v_, lf_, ig_ = inp
        b = jnp.cumsum(lf_, -1)
        log_d = jnp.where(causal, b[..., :, None] - b[..., None, :] + ig_[..., None, :], -jnp.inf)
        log_inter = b + m[..., None]
        m_t = jnp.maximum(jnp.max(log_d, -1), log_inter)
        d = jnp.exp(log_d - m_t[..., None])
        w_inter = jnp.exp(log_inter - m_t)
        s = jnp.einsum("bhld,bhsd->bhls", q_, k_) * d
        num = jnp.einsum("bhls,bhsv->bhlv", s, v_) + w_inter[..., None] * jnp.einsum("bhld,bhdv->bhlv", q_, C)
        den = jnp.sum(s, -1) + w_inter * jnp.einsum("bhld,bhd->bhl", q_, n)
        h = num / jnp.maximum(jnp.abs(den), jnp.exp(-m_t))[..., None]
        b_last = b[..., -1]
        log_w = b_last[..., None] - b + ig_
        m_new = jnp.maximum(b_last + m, jnp.max(log_w, -1))
        wk = jnp.exp(log_w - m_new[..., None])
        carry_decay = jnp.exp(b_last + m - m_new)
        C = carry_decay[..., None, None] * C + jnp.einsum("bhl,bhld,bhlv->bhdv", wk, k_, v_)
        n = carry_decay[..., None] * n + jnp.einsum("bhl,bhld->bhd", wk, k_)
        return (C, n, m_new), h

    init = (jnp.zeros((B, H, DK, DV), jnp.float32), jnp.zeros((B, H, DK), jnp.float32),
            jnp.zeros((B, H), jnp.float32))
    _, h = lax.scan(step, init, (qc, kc, vc, lfc, igc))
    return from_chunks(h)

def gated_delta_chunkwise(q, k, v, g, beta):
    B, S, H, DK = q.shape
    DV = v.shape[-1]
    L = G_CHUNK
    q = q * DK ** -0.5
    qc, kc, vc = to_chunks(q, L), to_chunks(k, L), to_chunks(v, L)
    bc = to_chunks(beta, L)
    G = jnp.cumsum(to_chunks(g, L), -1)
    incl = jnp.tril(jnp.ones((L, L), bool))
    strict = jnp.tril(jnp.ones((L, L), bool), -1)
    diff = G[..., :, None] - G[..., None, :]
    decay = jnp.where(incl, jnp.exp(jnp.where(incl, diff, 0.0)), 0.0)
    kk = jnp.einsum("nbhld,nbhsd->nbhls", kc, kc)
    a_mat = jnp.where(strict, bc[..., :, None] * kk * decay, 0.0) + jnp.eye(L, dtype=jnp.float32)
    rhs = jnp.concatenate([vc * bc[..., None], kc * (bc * jnp.exp(G))[..., None]], -1)
    sol = lax.linalg.triangular_solve(a_mat, rhs, left_side=True, lower=True, unit_diagonal=True)
    u, w = sol[..., :DV], sol[..., DV:]
    attn = jnp.einsum("nbhld,nbhsd->nbhls", qc, kc) * decay
    q_dec = qc * jnp.exp(G)[..., None]
    k_dec = kc * jnp.exp(G[..., -1:] - G)[..., None]
    g_last = jnp.exp(G[..., -1])

    def step(state, inp):
        u_, w_, attn_, qd_, kd_, gl_ = inp
        v_new = u_ - jnp.einsum("bhld,bhdv->bhlv", w_, state)
        o = jnp.einsum("bhld,bhdv->bhlv", qd_, state) + jnp.einsum("bhls,bhsv->bhlv", attn_, v_new)
        state = gl_[..., None, None] * state + jnp.einsum("bhld,bhlv->bhdv", kd_, v_new)
        return state, o

    _, o = lax.scan(step, jnp.zeros((B, H, DK, DV), jnp.float32), (u, w, attn, q_dec, k_dec, g_last))
    return from_chunks(o)

def hgrn2_chunkwise(q, k, v, log_f):
    B, S, H, DK = q.shape
    DV = v.shape[-1]
    L = C_CHUNK
    q = q * DK ** -0.5
    qc, kc, vc = to_chunks(q, L), to_chunks(k, L), to_chunks(v, L)
    G = jnp.cumsum(to_chunks(log_f, L), -2)
    q_dec = qc * jnp.exp(G)
    k_dec = kc * jnp.exp(G[..., -1:, :] - G)
    g_last = jnp.exp(G[..., -1, :])
    incl = jnp.tril(jnp.ones((L, L), bool))[:, :, None]

    def step(state, inp):
        q_, k_, v_, G_, qd_, kd_, gl_ = inp
        diff = G_[..., :, None, :] - G_[..., None, :, :]
        pair_decay = jnp.exp(jnp.where(incl, diff, -jnp.inf))
        attn = jnp.einsum("bhld,bhlsd,bhsd->bhls", q_, pair_decay, k_)
        o = jnp.einsum("bhld,bhdv->bhlv", qd_, state) + jnp.einsum("bhls,bhsv->bhlv", attn, v_)
        state = gl_[..., :, None] * state + jnp.einsum("bhld,bhlv->bhdv", kd_, v_)
        return state, o

    _, o = lax.scan(step, jnp.zeros((B, H, DK, DV), jnp.float32), (qc, kc, vc, G, q_dec, k_dec, g_last))
    return from_chunks(o)

def hgrn_lower_bounds(lb_logits):
    p = jax.nn.softmax(lb_logits.astype(jnp.float32), axis=0)
    return jnp.cumsum(p, axis=0) - p[0]

def ab_mixer(u, w_in, conv_m, m_gate_bias, m_norm, conv_g, g_a_log, g_dt_bias, g_norm, w_out):
    f32 = jnp.float32
    proj = u @ w_in
    m_q, m_k, m_v, m_o, m_i, m_f, g_q, g_k, g_v, g_gate, g_a, g_b = jnp.split(proj, AB_SPLIT_IDX, axis=-1)
    m_qk = jax.nn.silu(causal_dwconv(jnp.concatenate([m_q, m_k], -1), conv_m))
    m_q, m_k = jnp.split(m_qk, 2, axis=-1)
    gb = m_gate_bias.astype(f32)
    i_pre = softcap(m_i.astype(f32) + gb[0], GATE_SOFTCAP)
    f_pre = softcap(m_f.astype(f32) + gb[1], GATE_SOFTCAP)
    h_m = mlstm_chunkwise(to_heads(m_q, M_HEADS).astype(f32), to_heads(m_k, M_HEADS).astype(f32),
                          to_heads(m_v, M_HEADS).astype(f32), i_pre, f_pre)
    y_m = jax.nn.sigmoid(m_o.astype(f32)) * head_rms_norm(h_m, m_norm)
    g_qkv = jax.nn.silu(causal_dwconv(jnp.concatenate([g_q, g_k, g_v], -1), conv_g))
    g_q, g_k, g_v = jnp.split(g_qkv, 3, axis=-1)
    log_decay = -jnp.exp(g_a_log.astype(f32)) * jax.nn.softplus(g_a.astype(f32) + g_dt_bias.astype(f32))
    beta = jax.nn.sigmoid(g_b.astype(f32))
    h_g = gated_delta_chunkwise(l2_norm(to_heads(g_q, G_HEADS).astype(f32)),
                                l2_norm(to_heads(g_k, G_HEADS).astype(f32)),
                                to_heads(g_v, G_HEADS).astype(f32), log_decay, beta)
    y_g = head_rms_norm(h_g, g_norm) * jax.nn.silu(g_gate.astype(f32))
    y = jnp.concatenate([y_m, y_g], -1).astype(u.dtype)
    return y @ w_out

def hgrn2_mixer(u, w_in, lower_bound, norm_gain, w_out):
    f32 = jnp.float32
    q, f, i, gate = jnp.split(u @ w_in, [C_K_TOTAL, 2 * C_K_TOTAL, 2 * C_K_TOTAL + C_MIX], axis=-1)
    lb = lower_bound.astype(f32)
    ff = f.astype(f32)
    log_f = jnp.logaddexp(jnp.log(lb), jnp.log1p(-lb) + jax.nn.log_sigmoid(ff))
    k = (1.0 - lb) * jax.nn.sigmoid(-ff)
    o = hgrn2_chunkwise(to_heads(jax.nn.silu(q.astype(f32)), C_HEADS), to_heads(k, C_HEADS),
                        to_heads(i.astype(f32), C_HEADS), to_heads(log_f, C_HEADS))
    y = head_rms_norm(o, norm_gain) * jax.nn.silu(gate.astype(f32))
    return y.astype(u.dtype) @ w_out

def conv_ffn(u, w_up, conv_w, conv_b, w_down):
    hdn = causal_dwconv(u @ w_up, conv_w) + conv_b
    gate, val = jnp.split(hdn, 2, axis=-1)
    return (jax.nn.silu(gate) * val) @ w_down

def first_inputs(seed: int = 0) -> dict:
    key = jax.random.key(seed)
    ks = jax.random.split(key, 24)
    f32 = jnp.float32

    def nrm(k, shape, scale):
        return jax.random.normal(k, shape, f32) * scale

    dt = jnp.exp(jax.random.uniform(ks[9], (N_AB_LAYERS, G_HEADS), f32, np.log(1e-3), np.log(1e-1)))
    return {
        "x": nrm(ks[0], (BATCH, SEQ, D_MODEL), 1.0),
        "norm_gains": 1.0 + nrm(ks[1], (DEPTH, 4, D_MODEL), 0.05),
        "ab_w_in": nrm(ks[2], (N_AB_LAYERS, D_MODEL, AB_IN), D_MODEL ** -0.5),
        "ab_conv_m": nrm(ks[3], (N_AB_LAYERS, SHORT_CONV, 2 * M_QK), SHORT_CONV ** -0.5),
        "ab_m_gate_bias": jnp.stack([nrm(ks[4], (N_AB_LAYERS, M_HEADS), 0.1),
                                     jnp.linspace(3.0, 6.0, M_HEADS, dtype=f32) + nrm(ks[5], (N_AB_LAYERS, M_HEADS), 0.1)], axis=1),
        "ab_m_norm": 1.0 + nrm(ks[6], (N_AB_LAYERS, M_V), 0.05),
        "ab_conv_g": nrm(ks[7], (N_AB_LAYERS, SHORT_CONV, 2 * G_QK + G_V), SHORT_CONV ** -0.5),
        "ab_g_a_log": jnp.log(jax.random.uniform(ks[8], (N_AB_LAYERS, G_HEADS), f32, 1.0, 16.0)),
        "ab_g_dt_bias": dt + jnp.log(-jnp.expm1(-dt)),
        "ab_g_norm": 1.0 + nrm(ks[10], (N_AB_LAYERS, G_V), 0.05),
        "ab_w_out": nrm(ks[11], (N_AB_LAYERS, AB_MIX, D_MODEL), AB_MIX ** -0.5),
        "c_w_in": nrm(ks[12], (N_C_LAYERS, D_MODEL, C_IN), D_MODEL ** -0.5),
        "c_lb_logits": nrm(ks[13], (DEPTH, C_K_TOTAL), 0.5),
        "c_norm": 1.0 + nrm(ks[14], (N_C_LAYERS, C_MIX), 0.05),
        "c_w_out": nrm(ks[15], (N_C_LAYERS, C_MIX, D_MODEL), C_MIX ** -0.5),
        "ffn_w_up": nrm(ks[16], (DEPTH, D_MODEL, 2 * D_FF), D_MODEL ** -0.5),
        "ffn_conv_w": nrm(ks[17], (DEPTH, FFN_CONV, 2 * D_FF), FFN_CONV ** -0.5),
        "ffn_conv_b": nrm(ks[18], (DEPTH, 2 * D_FF), 0.02),
        "ffn_w_down": nrm(ks[19], (DEPTH, D_FF, D_MODEL), D_FF ** -0.5),
    }

def first_block(x, norm_gains, ab_w_in, ab_conv_m, ab_m_gate_bias, ab_m_norm, ab_conv_g, ab_g_a_log,
              ab_g_dt_bias, ab_g_norm, ab_w_out, c_w_in, c_lb_logits, c_norm, c_w_out,
              ffn_w_up, ffn_conv_w, ffn_conv_b, ffn_w_down):
    lower_bounds = hgrn_lower_bounds(c_lb_logits)
    for layer in range(DEPTH):
        j = layer // 2
        u = rms_norm(x, norm_gains[layer, 0])
        if layer % 2 == 0:
            mix = ab_mixer(u, ab_w_in[j], ab_conv_m[j], ab_m_gate_bias[j], ab_m_norm[j], ab_conv_g[j],
                           ab_g_a_log[j], ab_g_dt_bias[j], ab_g_norm[j], ab_w_out[j])
        else:
            mix = hgrn2_mixer(u, c_w_in[j], lower_bounds[layer], c_norm[j], c_w_out[j])
        x = x + rms_norm(mix, norm_gains[layer, 1])
        u = rms_norm(x, norm_gains[layer, 2])
        ff = conv_ffn(u, ffn_w_up[layer], ffn_conv_w[layer], ffn_conv_b[layer], ffn_w_down[layer])
        x = x + rms_norm(ff, norm_gains[layer, 3])
    return x


DEPTH_2 = 1

CHUNK = 64
HEAD_DIM = 64
POOL_WINDOWS = (2, 4, 8, 16)
POOL_WIDTH = D_MODEL // 4
POOL_GROUP = POOL_WIDTH // len(POOL_WINDOWS)
DSA_WIDTH = 3 * D_MODEL // 8
DSA_HEADS = DSA_WIDTH // HEAD_DIM
FOX_WIDTH = 3 * D_MODEL // 8
FOX_HEADS = FOX_WIDTH // HEAD_DIM
MIX_WIDTH = POOL_WIDTH + DSA_WIDTH + FOX_WIDTH
IDX_HEADS = 8
IDX_DIM = 32
DSA_TOPK_MAX = 256
DSA_QBLOCK = 32
FOX_QBLOCK = 128
RMS_EPS = 1e-6
IN_SIZES = (
    POOL_WIDTH, POOL_WIDTH,
    DSA_WIDTH, DSA_WIDTH, DSA_WIDTH, DSA_WIDTH,
    IDX_HEADS * IDX_DIM, IDX_DIM, IDX_HEADS,
    FOX_WIDTH, FOX_WIDTH, FOX_WIDTH, FOX_WIDTH,
    FOX_HEADS,
)
IN_COLS = 2 * POOL_WIDTH + 4 * DSA_WIDTH + IDX_HEADS * IDX_DIM + IDX_DIM + IDX_HEADS + 4 * FOX_WIDTH + FOX_HEADS


def rmsnorm(x, g):
    xf = x.astype(jnp.float32)
    y = xf * lax.rsqrt(jnp.mean(xf * xf, axis=-1, keepdims=True) + RMS_EPS)
    return (y * g.astype(jnp.float32)).astype(x.dtype)

def split_columns(z):
    parts = []
    off = 0
    for n in IN_SIZES:
        parts.append(z[..., off:off + n])
        off += n
    return parts

def pool_mixer(v, w_grp, scale):
    B, L, _ = v.shape
    vf = v.astype(jnp.float32)
    cs = jnp.pad(jnp.cumsum(vf, axis=1), ((0, 0), (1, 0), (0, 0)))
    t = jnp.arange(L)
    outs = []
    for gi, w in enumerate(POOL_WINDOWS):
        sl = slice(gi * POOL_GROUP, (gi + 1) * POOL_GROUP)
        c = cs[:, :, sl]
        lo = jnp.maximum(t + 1 - w, 0)
        win_sum = c[:, t + 1] - c[:, lo]
        cnt = (t + 1 - lo).astype(jnp.float32)[None, :, None]
        outs.append(win_sum / cnt - vf[:, :, sl])
    p = jnp.stack(outs, axis=2).astype(v.dtype)
    y = jnp.einsum('blgc,gcd->blgd', p, w_grp).reshape(B, L, POOL_WIDTH)
    return y * scale

def dsa_mixer(q, k, v, iq, ik, iw, topk):
    B, L, H, dh = q.shape
    n_blocks = L // DSA_QBLOCK
    key_pos = jnp.arange(L)
    sm_scale = 1.0 / math.sqrt(dh)
    gather = jax.vmap(lambda arr, idx: arr[idx])

    def block(bi):
        start = bi * DSA_QBLOCK
        qb = lax.dynamic_slice_in_dim(q, start, DSA_QBLOCK, axis=1)
        iqb = lax.dynamic_slice_in_dim(iq, start, DSA_QBLOCK, axis=1)
        iwb = lax.dynamic_slice_in_dim(iw, start, DSA_QBLOCK, axis=1)
        qpos = start + jnp.arange(DSA_QBLOCK)
        limit = (qpos // CHUNK + 1) * CHUNK
        dots = jnp.einsum('bqhd,bsd->bqhs', iqb, ik).astype(jnp.float32)
        score = jnp.einsum('bqh,bqhs->bqs', iwb.astype(jnp.float32), jax.nn.relu(dots))
        admissible = key_pos[None, None, :] < limit[None, :, None]
        score = jnp.where(admissible, score, -jnp.inf)
        _, sel = lax.top_k(score, topk)
        valid = sel < limit[None, :, None]
        kg = gather(k, sel)
        vg = gather(v, sel)
        s = jnp.einsum('bqhd,bqkhd->bqhk', qb, kg).astype(jnp.float32) * sm_scale
        s = jnp.where(valid[:, :, None, :], s, -jnp.inf)
        p = jax.nn.softmax(s, axis=-1).astype(v.dtype)
        return jnp.einsum('bqhk,bqkhd->bqhd', p, vg)

    o = lax.map(block, jnp.arange(n_blocks))
    return jnp.transpose(o, (1, 0, 2, 3, 4)).reshape(B, L, H, dh)

def fox_mixer(q, k, v, log_f):
    B, L, H, dh = q.shape
    sm_scale = 1.0 / math.sqrt(dh)
    F = jnp.transpose(jnp.cumsum(log_f, axis=1), (0, 2, 1))
    outs = []
    for bi in range(L // FOX_QBLOCK):
        s0 = bi * FOX_QBLOCK
        e = s0 + FOX_QBLOCK
        s = jnp.einsum('bqhd,bkhd->bhqk', q[:, s0:e], k[:, :e]).astype(jnp.float32) * sm_scale
        s = s + F[:, :, s0:e, None] - F[:, :, None, :e]
        mask = jnp.arange(s0, e)[:, None] >= jnp.arange(e)[None, :]
        s = jnp.where(mask[None, None], s, -jnp.inf)
        p = jax.nn.softmax(s, axis=-1).astype(v.dtype)
        outs.append(jnp.einsum('bhqk,bkhd->bqhd', p, v[:, :e]))
    return jnp.concatenate(outs, axis=1)

def second_inputs(seed: int = 0) -> dict:
    key = jax.random.key(seed)
    ks = jax.random.split(key, 9)
    x = jax.random.normal(ks[0], (BATCH, SEQ, D_MODEL), jnp.float32)
    w_in = jax.random.normal(ks[1], (DEPTH_2, D_MODEL, IN_COLS), jnp.float32) * D_MODEL ** -0.5
    norm_g = 1.0 + 0.02 * jax.random.normal(ks[2], (DEPTH_2, D_MODEL), jnp.float32)
    pool_w = jax.random.normal(ks[3], (DEPTH_2, len(POOL_WINDOWS), POOL_GROUP, POOL_GROUP), jnp.float32) * POOL_GROUP ** -0.5
    pool_scale = 1.0 + 0.1 * jax.random.normal(ks[4], (DEPTH_2, POOL_WIDTH), jnp.float32)
    fox_bf = 3.0 + 0.5 * jax.random.normal(ks[5], (DEPTH_2, FOX_HEADS), jnp.float32)
    w_out = jax.random.normal(ks[6], (DEPTH_2, MIX_WIDTH, D_MODEL), jnp.float32) * MIX_WIDTH ** -0.5
    final_g = 1.0 + 0.02 * jax.random.normal(ks[7], (D_MODEL,), jnp.float32)
    return {'x': x, 'w_in': w_in, 'norm_g': norm_g, 'pool_w': pool_w, 'pool_scale': pool_scale,
            'fox_bf': fox_bf, 'w_out': w_out, 'final_g': final_g}

def second_block(x, w_in, norm_g, pool_w, pool_scale, fox_bf, w_out, final_g):
    B, L, _ = x.shape
    topk = min(DSA_TOPK_MAX, L // 4)
    idx_w_scale = IDX_HEADS ** -0.5
    for layer in range(DEPTH_2):
        h = rmsnorm(x, norm_g[layer])
        z = jnp.einsum('bld,dc->blc', h, w_in[layer])
        (pv, pg, dq, dk, dv, dg, iq, ik, iw, fq, fk, fv, fg, ff) = split_columns(z)
        a_out = pool_mixer(pv, pool_w[layer], pool_scale[layer]) * jax.nn.silu(pg)
        b_o = dsa_mixer(dq.reshape(B, L, DSA_HEADS, HEAD_DIM), dk.reshape(B, L, DSA_HEADS, HEAD_DIM),
                        dv.reshape(B, L, DSA_HEADS, HEAD_DIM), iq.reshape(B, L, IDX_HEADS, IDX_DIM),
                        ik, iw * idx_w_scale, topk)
        b_out = b_o.reshape(B, L, DSA_WIDTH) * jax.nn.silu(dg)
        log_f = jax.nn.log_sigmoid(ff.astype(jnp.float32) + fox_bf[layer].astype(jnp.float32))
        c_o = fox_mixer(fq.reshape(B, L, FOX_HEADS, HEAD_DIM), fk.reshape(B, L, FOX_HEADS, HEAD_DIM),
                        fv.reshape(B, L, FOX_HEADS, HEAD_DIM), log_f)
        c_out = c_o.reshape(B, L, FOX_WIDTH) * jax.nn.silu(fg)
        mixed = jnp.concatenate([a_out, b_out, c_out], axis=-1)
        x = x + jnp.einsum('blc,cd->bld', mixed, w_out[layer])
    return rmsnorm(x, final_g)


def setup_inputs(seed=0):
    out = dict(first_inputs(seed))
    for name, value in second_inputs(seed + 1).items():
        if name != "x":
            out[name + "_2"] = value
    return out


def reference(
    x, norm_gains, ab_w_in, ab_conv_m, ab_m_gate_bias, ab_m_norm, ab_conv_g, ab_g_a_log,
    ab_g_dt_bias, ab_g_norm, ab_w_out, c_w_in, c_lb_logits, c_norm, c_w_out, ffn_w_up,
    ffn_conv_w, ffn_conv_b, ffn_w_down, w_in_2, norm_g_2, pool_w_2, pool_scale_2, fox_bf_2,
    w_out_2, final_g_2,
):
    x = first_block(
        x, norm_gains, ab_w_in, ab_conv_m, ab_m_gate_bias, ab_m_norm, ab_conv_g, ab_g_a_log,
        ab_g_dt_bias, ab_g_norm, ab_w_out, c_w_in, c_lb_logits, c_norm, c_w_out, ffn_w_up,
        ffn_conv_w, ffn_conv_b, ffn_w_down,
    )
    return second_block(
        x, w_in_2, norm_g_2, pool_w_2, pool_scale_2, fox_bf_2, w_out_2, final_g_2,
    )


_drawn_inputs = setup_inputs


def setup_inputs(seed=0):
    import zlib

    import numpy as np

    out = dict(_drawn_inputs(seed))
    spreads = {}
    factors = {'norm_g_2': 8.0, 'pool_scale_2': 4.994, 'fox_bf_2': 3.394, 'final_g_2': 2.8}
    for name, (base, spread) in spreads.items():
        noise = np.random.default_rng([zlib.crc32(name.encode()), seed]).standard_normal(out[name].shape)
        drawn = base * np.exp(spread * noise) if base else spread * noise
        out[name] = __import__('jax').numpy.asarray(drawn.astype(out[name].dtype))
    for name, factor in factors.items():
        out[name] = (out[name] * factor).astype(out[name].dtype)
    return out
```

```python
from contextlib import ExitStack

import numpy as np
import concourse.bass as bass
from concourse import mybir
from concourse.alu_op_type import AluOpType as ALU

F32 = mybir.dt.float32
U32 = mybir.dt.uint32
ACT = mybir.ActivationFunctionType
AX = mybir.AxisListType.X

P = 128
T = 512
NT = T // P
D = 1024
KD = D // P
FF = 2816
KF = FF // P
EPS = 1e-6
BIG = 1e30

LEVELS = [1 << n for n in range(7)]
_CST = [("ident", P), ("ones", P), ("upper", P), ("causal", P), ("chunkdiag", P), ("levels", P * len(LEVELS)),
        ("reset", T), ("rcount", 2 * T), ("sel", 6 * P)]
CST = {}
_at = 0
for _n, _w in _CST:
    CST[_n] = (_at, _w)
    _at += _w
NCST = _at

_COLS = [("gains", 8 * KD), ("norm2", KD), ("final2", KD), ("ffn", 2 * 2 * KF * 4), ("mconv", 4 * 4), ("gconv", 4 * 3 * 4),
         ("mnorm", 4), ("gnorm", 4), ("cnorm", 8), ("lb", 2 * 8), ("pscale", 2), ("gbias", 2), ("adt", 2), ("foxb", 1)]
COL = {}
_at = 0
for _n, _w in _COLS:
    COL[_n] = (_at, _w)
    _at += _w
NCOL = _at


class Chain:

    def __init__(self, eng, sem):
        self.eng, self.sem, self.base, self.n = eng, sem, 0, 0

    def link(self, ins):
        self.n += 1
        ins.then_inc(self.sem, 1)
        self.eng.wait_ge(self.sem, self.base + self.n)

    def loop(self, per_step, i):
        self.base, self.enter, self.n = self.base + self.n + i * per_step, (self.base + self.n, per_step), 0

    def end(self, steps):
        before, per_step = self.enter
        assert self.n == per_step, (self.n, per_step)
        self.base, self.n = before + per_step * steps, 0


def phase(f):
    def run(k, *args):
        with ExitStack() as k.stack:
            f(k, *args)
    return run


class Core:

    def __init__(self, nc, a):
        self.nc, self.a, self.sems = nc, a, []
        sb = nc.alloc_sbuf_tensor
        self.x = sb("x_res", [P, KD, T], F32)
        self.u = sb("u_in", [P, KD, T], F32)
        self.y = sb("y_mix", [P, KD, T], F32)
        self.w = sb("w_ring", [P, 4, D], F32)
        self.sq = sb("sq", [P, 2, T], F32)
        self.rstd = sb("rstd", [P, T], F32)
        self.cst = sb("cst_sb", [P, NCST], F32)
        self.col = sb("col_sb", [P, NCOL], F32)
        self.epsc = sb("eps_col", [P, 1], F32)
        self.lb = sb("lb_cols", [P, 2, KD], F32)
        self.ps = [nc.alloc_psum_tensor(f"bank{i}", [P, T], F32) for i in range(8)]

    def sb(self, name, shape, dtype=F32):
        return self.stack.enter_context(self.nc.sbuf_tensor(name, shape, dtype))

    def sem(self, name):
        self.sems.append(self.nc.alloc_semaphore(name))
        return self.sems[-1]

    def clear_semaphores(self):
        self.nc.clear_and_free_semaphores(self.sems)
        self.nc.all_engine_barrier()
        self.sems = []

    def c(self, name, lo=0, hi=None):
        at, w = CST[name]
        return self.cst[:, at + lo:at + (w if hi is None else hi)]

    def p(self, name, i, n=1):
        at, _ = COL[name]
        return self.col[:, bass.ds(at + i, n)]


@phase
def load_inputs(k):
    nc, a = k.nc, k.a
    loaded = k.sem("inputs_loaded")
    with nc.Block() as block:
        @block.sync
        def _(sp):
            sp.dma_start(k.x[:, :, :], a["x"].rearrange("(k p) t -> p k t", p=P)).then_inc(loaded, 16)
            sp.dma_start(k.cst[:, :], a["cst"]).then_inc(loaded, 16)
            sp.dma_start(k.col[:, :], a["col"]).then_inc(loaded, 16)
            sp.wait_ge(loaded, 49)

        @block.vector
        def _(dve):
            nc.vector.memset(k.epsc[:, :], EPS).then_inc(loaded, 1)


@phase
def norm_in(k, tag, gain):
    nc = k.nc
    squared, summed, rooted, chained = (k.sem(f"{s}_{tag}") for s in
                                        ("squared", "summed", "rooted", "chained"))
    with nc.Block() as block:
        @block.scalar
        def _(act):
            for m in range(KD):
                if m >= 2:
                    act.wait_ge(summed, m - 1)
                nc.scalar.activation(k.sq[:, m % 2, :], k.x[:, m, :], ACT.Square).then_inc(squared, 1)
            act.wait_ge(summed, KD)
            nc.scalar.activation(k.rstd[:, :], k.ps[0][:, :], ACT.Sqrt, bias=k.epsc[:, 0:1], scale=1.0 / D).then_inc(rooted, 1)

        @block.tensor
        def _(pe):
            for m in range(KD):
                pe.wait_ge(squared, m + 1)
                nc.tensor.matmul(k.ps[0][:, :], k.c("ones"), k.sq[:, m % 2, :], start=m == 0, stop=m == KD - 1).then_inc(summed, 1)

        @block.vector
        def _(dve):
            ch = Chain(dve, chained)
            dve.wait_ge(rooted, 1)
            ch.link(nc.vector.reciprocal(k.rstd[:, :], k.rstd[:, :]))
            for m in range(KD):
                ins = nc.vector.scalar_tensor_tensor(k.u[:, m, :], k.x[:, m, :], gain(m), k.rstd[:, :], ALU.mult, ALU.mult)
            ch.link(ins)


@phase
def out_proj(k, tag, src, tiles, weights, gain_post, gain_next):
    nc = k.nc
    w_loaded = [k.sem(f"w_loaded{s}_{tag}") for s in range(2)]
    w_used = [k.sem(f"w_used{s}_{tag}") for s in range(2)]
    names = ("mixed", "moved", "squared", "summed", "rooted", "added", "squared2", "summed2", "rooted2", "chained")
    mixed, moved, squared, summed, rooted, added, squared2, summed2, rooted2, chained = (
        k.sem(f"{s}_{tag}") for s in names)
    pairs = tiles // 2
    with nc.Block() as block:
        @block.sync
        def _(sp):
            for s in range(2):
                sp.dma_start(k.w[:, s, :], weights[s * P:(s + 1) * P, :]).then_inc(w_loaded[s], 16)
            with sp.Fori(1, pairs) as i:
                for s in range(2):
                    sp.wait_ge(w_used[s], i)
                    sp.dma_start(k.w[:, s, :], weights[bass.ds((2 * i + s) * P, P), :]).then_inc(w_loaded[s], 16)

        @block.tensor
        def _(pe):
            def step(i, s, start, stop):
                pe.wait_ge(w_loaded[s], 16 * i + 16)
                for m in range(KD):
                    ins = nc.tensor.matmul(k.ps[m][:, :], k.w[:, s, m * P:(m + 1) * P],
                                           src[:, bass.ds(2 * i + s, 1), :].rearrange("p a t -> p (a t)"), start=start, stop=stop)
                    if stop:
                        ins.then_inc(mixed, 1)
                if not stop:
                    ins.then_inc(w_used[s], 1)
            step(0, 0, True, False)
            step(0, 1, False, False)
            with pe.Fori(1, pairs - 1) as i:
                step(i, 0, False, False)
                step(i, 1, False, False)
            step(pairs - 1, 0, False, False)
            step(pairs - 1, 1, False, True)
            if gain_post:
                pe.wait_ge(moved, 1)
                for m in range(KD):
                    pe.wait_ge(squared, m + 1)
                    nc.tensor.matmul(k.ps[0][:, :], k.c("ones"), k.sq[:, m % 2, :], start=m == 0, stop=m == KD - 1).then_inc(summed, 1)
            for m in range(KD):
                if m == 0:
                    pe.wait_ge(moved if gain_post else added, 2)
                pe.wait_ge(squared2, m + 1)
                nc.tensor.matmul(k.ps[1][:, :], k.c("ones"), k.sq[:, m % 2, :], start=m == 0, stop=m == KD - 1).then_inc(summed2, 1)

        @block.scalar
        def _(act):
            if gain_post:
                for m in range(KD):
                    act.wait_ge(moved, m + 1)
                    if m >= 2:
                        act.wait_ge(summed, m - 1)
                    nc.scalar.activation(k.sq[:, m % 2, :], k.u[:, m, :], ACT.Square).then_inc(squared, 1)
                act.wait_ge(summed, KD)
                nc.scalar.activation(k.rstd[:, :], k.ps[0][:, :], ACT.Sqrt, bias=k.epsc[:, 0:1], scale=1.0 / D).then_inc(rooted, 1)
            for m in range(KD):
                act.wait_ge(added, m + 1)
                if m >= 2:
                    act.wait_ge(summed2, m - 1)
                nc.scalar.activation(k.sq[:, m % 2, :], k.x[:, m, :], ACT.Square).then_inc(squared2, 1)
            act.wait_ge(summed2, KD)
            nc.scalar.activation(k.rstd[:, :], k.ps[1][:, :], ACT.Sqrt, bias=k.epsc[:, 0:1], scale=1.0 / D).then_inc(rooted2, 1)

        @block.vector
        def _(dve):
            ch = Chain(dve, chained)
            if gain_post:
                for m in range(KD):
                    dve.wait_ge(mixed, m + 1)
                    nc.vector.tensor_copy(k.u[:, m, :], k.ps[m][:, :]).then_inc(moved, 1)
                dve.wait_ge(moved, KD)
                dve.wait_ge(rooted, 1)
                ch.link(nc.vector.reciprocal(k.rstd[:, :], k.rstd[:, :]))
                ins = None
                for m in range(KD):
                    nxt = nc.vector.scalar_tensor_tensor(k.u[:, m, :], k.u[:, m, :], gain_post(m), k.rstd[:, :], ALU.mult, ALU.mult)
                    if m < KD - 1:
                        nxt.then_inc(chained, 1)
                        ch.n += 1
                    else:
                        ch.link(nxt)
                for m in range(KD):
                    nc.vector.tensor_tensor(k.x[:, m, :], k.x[:, m, :], k.u[:, m, :], ALU.add).then_inc(added, 1)
            else:
                for m in range(KD):
                    dve.wait_ge(mixed, m + 1)
                    ins = nc.vector.tensor_tensor(k.x[:, m, :], k.x[:, m, :], k.ps[m][:, :], ALU.add)
                    ins.then_inc(added, 1)
                dve.wait_ge(added, KD)
            dve.wait_ge(rooted2, 1)
            ch.link(nc.vector.reciprocal(k.rstd[:, :], k.rstd[:, :]))
            for m in range(KD):
                ins = nc.vector.scalar_tensor_tensor(k.u[:, m, :], k.x[:, m, :], gain_next(m), k.rstd[:, :], ALU.mult, ALU.mult)
            ch.link(ins)


@phase
def ffn_up(k, tag, layer, weights, h):
    nc = k.nc
    sem = k.sem
    w_loaded = [sem(f"w_loaded{s}_{tag}") for s in range(4)]
    up_done, tap_done, conv_done, silu_done, mul_done = (sem(f"{s}_{tag}") for s in
                                                        ("up_done", "tap_done", "conv_done", "silu_done", "mul_done"))
    chained = sem(f"chained_{tag}")
    cg = k.sb(f"conv_{tag}", [P, 4, T])
    n = KF // 2

    def coef(tile, j):
        return k.p("ffn", (layer * 2 * KF + tile) * 4 + j)

    with nc.Block() as block:
        @block.sync
        def _(sp):
            for s in range(4):
                sp.dma_start(k.w[:, s, :], weights[s, :, :]).then_inc(w_loaded[s], 16)
            with sp.Fori(1, n) as i:
                for s in range(4):
                    sp.wait_ge(up_done, 4 * i - 3 + s)
                    sp.dma_start(k.w[:, s:s + 1, :], weights[bass.ds(4 * i + s, 1), :, :].rearrange("a p d -> p a d")).then_inc(w_loaded[s], 16)

        @block.tensor
        def _(pe):
            def step(i, first):
                for s in range(4):
                    pe.wait_ge(w_loaded[s], 16 * i + 16)
                    if not first:
                        pe.wait_ge(conv_done, 4 * i - 3 + s)
                    for m in range(KD):
                        ins = nc.tensor.matmul(k.ps[s][:, :], k.w[:, s, m * P:(m + 1) * P], k.u[:, m, :], start=m == 0, stop=m == KD - 1)
                    ins.then_inc(up_done, 1)
            step(0, True)
            with pe.Fori(1, n) as i:
                step(i, False)

        @block.scalar
        def _(act):
            def step(i, first):
                for s in range(4):
                    act.wait_ge(up_done, 4 * i + s + 1)
                    if not first:
                        act.wait_ge(mul_done, 2 * i - 1 + s // 2)
                    nc.scalar.activation(cg[:, s, :], k.ps[s][:, :], ACT.Identity, bias=coef(4 * i + s, 3), scale=coef(4 * i + s, 2)).then_inc(tap_done, 1)
                    if s % 2:
                        act.wait_ge(conv_done, 4 * i + s)
                        nc.scalar.activation(cg[:, s - 1, :], cg[:, s - 1, :], ACT.Silu).then_inc(silu_done, 1)
            step(0, True)
            with act.Fori(1, n) as i:
                step(i, False)

        @block.vector
        def _(dve):
            ch = Chain(dve, chained)

            def step(i):
                for s in range(4):
                    dve.wait_ge(tap_done, 4 * i + s + 1)
                    ch.link(nc.vector.scalar_tensor_tensor(cg[:, s, 1:T], k.ps[s][:, 0:T - 1], coef(4 * i + s, 1), cg[:, s, 1:T], ALU.mult, ALU.add))
                    nc.vector.scalar_tensor_tensor(cg[:, s, 2:T], k.ps[s][:, 0:T - 2], coef(4 * i + s, 0), cg[:, s, 2:T], ALU.mult, ALU.add).then_inc(conv_done, 1)

            with dve.Fori(0, n) as i:
                ch.loop(4, i)
                step(i)
            ch.end(n)

        @block.gpsimd
        def _(pool):
            with pool.Fori(0, n) as i:
                for s in (1, 3):
                    pool.wait_ge(conv_done, 4 * i + s + 1)
                    pool.wait_ge(silu_done, 2 * i + (s + 1) // 2)
                    nc.gpsimd.tensor_tensor(h[:, bass.ds(2 * i + s // 2, 1), :], cg[:, s - 1:s, :], cg[:, s:s + 1, :], ALU.mult).then_inc(mul_done, 1)


def ffn(k, tag, layer, gain_next):
    with k.nc.sbuf_tensor(f"hidden{tag}", [P, KF, T], F32) as hidden:
        ffn_up(k, f"up{tag}", layer, k.a["ffn_up"][layer], hidden)
        out_proj(k, f"down{tag}", hidden, KF, k.a["ffn_down"][layer],
                 lambda m: k.p("gains", (4 * layer + 3) * KD + m), gain_next)


@phase
def store_out(k, src):
    nc = k.nc
    stored = k.sem("out_stored")
    with nc.Block() as block:
        @block.sync
        def _(sp):
            sp.dma_start(k.a["out"].rearrange("(k p) t -> p k t", p=P), src[:, :, :]).then_inc(stored, 16)
            sp.wait_ge(stored, 16)


LNEXP = "natural_log_exp_and_others"
HC = 8


@phase
def lower_bounds(k):
    nc = k.nc
    t = k.sb("lb_tmp", [P, 5, HC], F32)
    maxed, powered, bounded = (k.sem(s) for s in ("lb_maxed", "lb_powered", "lb_bounded"))
    l0, l1 = k.p("lb", 0, HC), k.p("lb", HC, HC)
    with nc.Block() as block:
        @block.vector
        def _(dve):
            ch = Chain(dve, maxed)
            ch.link(nc.vector.tensor_tensor(t[:, 0, :], l0, l1, ALU.max))
            nc.vector.tensor_tensor(t[:, 1, :], l0, t[:, 0, :], ALU.subtract)
            ch.link(nc.vector.tensor_tensor(t[:, 2, :], l1, t[:, 0, :], ALU.subtract))
            dve.wait_ge(powered, 1)
            ch2 = Chain(dve, bounded)
            ch2.link(nc.vector.tensor_tensor(t[:, 0, :], t[:, 1, :], t[:, 2, :], ALU.add))
            ch2.link(nc.vector.reciprocal(t[:, 3, :], t[:, 0, :]))
            ch2.link(nc.vector.tensor_tensor(t[:, 1:3, :], t[:, 1:3, :], t[:, 3:4, :].to_broadcast([P, 2, HC]), ALU.mult))
            ch2.link(nc.vector.tensor_tensor(t[:, 4, :], t[:, 1, :], t[:, 2, :], ALU.add))
            ch2.link(nc.vector.tensor_tensor(k.lb[:, 0, :], t[:, 4, :], t[:, 1, :], ALU.subtract))
            ch2.link(nc.vector.tensor_scalar(k.lb[:, 1, :], k.lb[:, 0, :], -1.0, 1.0, ALU.mult, ALU.add))

        @block.scalar
        def _(act):
            act.wait_ge(maxed, 2)
            nc.scalar.activation(t[:, 1:3, :], t[:, 1:3, :], ACT.Exp).then_inc(powered, 1)


@phase
def hgrn2(k, weights):
    nc = k.nc
    sem = k.sem
    sb = k.sb
    H = HC
    scale = P ** -0.5
    q, kk, v, gate = (sb(f"c_{s}", [P, T], F32) for s in ("q", "k", "v", "gate"))
    fbuf, ef, sig, logf, G, E, kdf, qd, kd, kdt, at, osb = (
        sb(f"c_{s}", [P, T], F32) for s in ("f", "ef", "sig", "logf", "G", "E", "kdf", "qd", "kd", "kdt", "attn", "o"))
    dif = sb("c_dif", [P, 2, T], F32)
    tick = sb("c_tick", [P, 2], F32)
    X = sb("c_X", [P, 2, T], F32)
    S = sb("c_S", [P, NT - 1, P], F32)
    b_q, b_f, b_g, b_v, b_x0, b_x1, b_kv, b_o = k.ps
    b_x = [b_x0, b_x1]
    w_loaded = [sem(f"c_w_loaded{s}") for s in range(4)]
    (proj_done, f_clamped, act_prep, sig_ready, ft_ready, logf_ready, g_ready, e_ready, kd_ready, tr_done, kdt_ready, kv_done,
     s_ready, diff_ready, lexp_ready, x_ready, lv_done, at_done, o_done, osb_ready, osq_ready, nrm_done, rs_ready, y_ready,
     ch_act, ch_dve) = (sem("c_" + s) for s in (
         "proj_done f_clamped act_prep sig_ready ft_ready logf_ready g_ready e_ready kd_ready tr_done kdt_ready kv_done "
         "s_ready diff_ready lexp_ready x_ready lv_done at_done o_done osb_ready osq_ready nrm_done rs_ready y_ready "
         "ch_act ch_dve").split())
    NL = len(LEVELS)

    def chunks(x):
        return x[:, :].rearrange("p (c l) -> p c l", l=P)

    def mask(name, lo):
        return k.c(name, lo, lo + P).rearrange("p (a l) -> p a l", a=1).to_broadcast([P, NT, P])

    def blocks(x, b):
        return x.rearrange("p (n e b) -> p n e b", e=2, b=b)

    with nc.Block() as block:
        @block.sync
        def _(sp):
            for s in range(4):
                sp.dma_start(k.w[:, s, :], weights[s, :, :]).then_inc(w_loaded[s], 16)
            with sp.Fori(1, H) as h:
                for s in range(4):
                    sp.wait_ge(proj_done, 4 * h - 3 + s)
                    sp.dma_start(k.w[:, s:s + 1, :], weights[bass.ds(4 * h + s, 1), :, :].rearrange("a p d -> p a d")).then_inc(w_loaded[s], 16)

        @block.tensor
        def _(pe):
            def project(h, s, first=False):
                pe.wait_ge(w_loaded[s], 16 * h + 16)
                if not first:
                    if s == 1:
                        pe.wait_ge(sig_ready, h)
                    else:
                        pe.wait_ge(act_prep, 3 * h - (2 if s == 0 else 1 if s == 2 else 0))
                if s < 3:
                    for m in range(KD):
                        ins = nc.tensor.matmul(k.ps[s][:, :], k.w[:, s, m * P:(m + 1) * P], k.u[:, m, :], start=m == 0, stop=m == KD - 1)
                else:
                    for j in range(NT):
                        for m in range(KD):
                            ins = nc.tensor.matmul(b_v[:, j * P:(j + 1) * P], k.u[:, m, j * P:(j + 1) * P], k.w[:, s, m * P:(m + 1) * P],
                                                   start=m == 0, stop=m == KD - 1)
                ins.then_inc(proj_done, 1)

            def level(h, l):
                pe.wait_ge(x_ready, NL * h + l + 1)
                if l >= 1:
                    pe.wait_ge(at_done, 8 * h + l)
                for c in range(NT):
                    xc = X[:, l % 2, c * P:(c + 1) * P]
                    ins = nc.tensor.matmul(b_x[(l + 1) % 2][:, c * P:(c + 1) * P], xc, xc, start=True, stop=True)
                ins.then_inc(lv_done, 1)

            def core(h, nxt, first):
                if nxt:
                    project(h + 1, 0)
                pe.wait_ge(sig_ready, h + 1)
                pe.wait_ge(g_ready, h + 1)
                if not first:
                    pe.wait_ge(rs_ready, h)
                for c in range(NT):
                    ins = nc.tensor.matmul(b_x0[:, c * P:(c + 1) * P], kk[:, c * P:(c + 1) * P], q[:, c * P:(c + 1) * P], start=True, stop=True)
                ins.then_inc(lv_done, 1)
                level(h, 0)
                level(h, 1)
                if nxt:
                    project(h + 1, 1)
                level(h, 2)
                level(h, 3)
                if nxt:
                    project(h + 1, 2)
                level(h, 4)
                level(h, 5)
                pe.wait_ge(kd_ready, h + 1)
                for c in range(NT - 1):
                    ins = nc.tensor.transpose(b_kv[:, c * P:(c + 1) * P], kd[:, c * P:(c + 1) * P], k.c("ident"))
                ins.then_inc(tr_done, 1)
                level(h, 6)
                pe.wait_ge(kdt_ready, h + 1)
                pe.wait_ge(act_prep, 3 * h + 3)
                for c in range(NT - 1):
                    ins = nc.tensor.matmul(b_kv[:, c * P:(c + 1) * P], kdt[:, c * P:(c + 1) * P], v[:, c * P:(c + 1) * P], start=True, stop=True)
                ins.then_inc(kv_done, 1)
                pe.wait_ge(at_done, 8 * h + 8)
                for c in range(NT):
                    s = slice(c * P, (c + 1) * P)
                    ins = nc.tensor.matmul(b_o[:, s], v[:, s], at[:, s], start=True, stop=c == 0)
                    if c:
                        if c == 1:
                            pe.wait_ge(s_ready, h + 1)
                        ins = nc.tensor.matmul(b_o[:, s], S[:, c - 1, :], qd[:, s], start=False, stop=True)
                ins.then_inc(o_done, 1)
                if nxt:
                    project(h + 1, 3)
                pe.wait_ge(osq_ready, h + 1)
                nc.tensor.matmul(b_x0[:, :], k.c("ones"), k.sq[:, 0, :], start=True, stop=True).then_inc(nrm_done, 1)

            for s in range(4):
                project(0, s, first=True)
            core(0, True, True)
            with pe.Fori(1, H - 1) as h:
                core(h, True, False)
            core(H - 1, False, False)

        @block.scalar
        def _(act):
            ch = Chain(act, ch_act)

            def step(h):
                act.wait_ge(proj_done, 4 * h + 1)
                nc.scalar.activation(q[:, :], b_q[:, :], ACT.Silu).then_inc(act_prep, 1)
                act.wait_ge(proj_done, 4 * h + 3)
                nc.scalar.activation(gate[:, :], b_g[:, :], ACT.Silu).then_inc(act_prep, 1)
                act.wait_ge(proj_done, 4 * h + 4)
                nc.scalar.activation(v[:, :], b_v[:, :], ACT.Copy).then_inc(act_prep, 1)
                nc.scalar.preload_act_table_set(LNEXP)
                act.wait_ge(f_clamped, h + 1)
                ch.link(nc.scalar.activation(ef[:, :], fbuf[:, :], ACT.Exp, scale=-1.0))
                ch.link(nc.scalar.activation(sig[:, :], ef[:, :], ACT.Ln, bias=1.0))
                nc.scalar.activation(sig[:, :], sig[:, :], ACT.Exp, scale=-1.0).then_inc(sig_ready, 1)
                act.wait_ge(ft_ready, h + 1)
                nc.scalar.activation(logf[:, :], fbuf[:, :], ACT.Ln).then_inc(logf_ready, 1)
                act.wait_ge(g_ready, h + 1)
                nc.scalar.activation(E[:, :], G[:, :], ACT.Exp)
                nc.scalar.activation(kdf[:, :], kdf[:, :], ACT.Exp, scale=-1.0).then_inc(e_ready, 1)
                for l, b in enumerate(LEVELS):
                    act.wait_ge(diff_ready, NL * h + l + 1)
                    d = blocks(dif[:, l % 2, :], b)
                    nc.scalar.activation(d[:, :, 0, :], d[:, :, 0, :], ACT.Exp, scale=-1.0)
                    nc.scalar.activation(d[:, :, 1, :], d[:, :, 1, :], ACT.Exp).then_inc(lexp_ready, 1)
                act.wait_ge(tr_done, h + 1)
                nc.scalar.activation(kdt[:, 0:T - P], b_kv[:, 0:T - P], ACT.Copy).then_inc(kdt_ready, 1)
                act.wait_ge(o_done, h + 1)
                nc.scalar.activation(osb[:, :], b_o[:, :], ACT.Copy, scale=scale).then_inc(osb_ready, 1)
                act.wait_ge(osb_ready, h + 1)
                nc.scalar.activation(k.sq[:, 0, :], osb[:, :], ACT.Square).then_inc(osq_ready, 1)
                act.wait_ge(nrm_done, h + 1)
                ch.link(nc.scalar.activation(k.rstd[:, :], b_x0[:, :], ACT.Ln, bias=k.epsc[:, 0:1], scale=1.0 / P))
                nc.scalar.activation(k.rstd[:, :], k.rstd[:, :], ACT.Exp, scale=-0.5).then_inc(rs_ready, 1)
                act.wait_ge(y_ready, h + 1)

            with act.Fori(0, H) as h:
                ch.loop(3, h)
                step(h)
            ch.end(H)

        @block.gpsimd
        def _(pool):
            def step(h):
                pool.wait_ge(e_ready, h + 1)
                nc.gpsimd.tensor_tensor(kd[:, :], kk[:, :], kdf[:, :], ALU.mult)
                nc.gpsimd.tensor_tensor(qd[:, :], q[:, :], E[:, :], ALU.mult).then_inc(kd_ready, 1)
                for l, b in enumerate(LEVELS):
                    pool.wait_ge(lexp_ready, NL * h + l + 1)
                    if l >= 2:
                        pool.wait_ge(lv_done, 8 * h + l)
                    d, x = blocks(dif[:, l % 2, :], b), blocks(X[:, l % 2, :], b)
                    nc.gpsimd.tensor_tensor(x[:, :, 0, :], blocks(kk[:, :], b)[:, :, 0, :], d[:, :, 0, :], ALU.mult)
                    nc.gpsimd.tensor_tensor(x[:, :, 1, :], blocks(q[:, :], b)[:, :, 1, :], d[:, :, 1, :], ALU.mult).then_inc(x_ready, 1)

            with pool.Fori(0, H) as h:
                step(h)

        @block.vector
        def _(dve):
            ch = Chain(dve, ch_dve)

            def diff(h, l):
                b = LEVELS[l]
                g = G[:, :].rearrange("p (n b) -> p n b", b=2 * b)
                ref = g[:, :, b - 1:b].to_broadcast([P, T // (2 * b), 2 * b])
                if l >= 2:
                    dve.wait_ge(x_ready, NL * h + l - 1)
                nc.vector.tensor_tensor(dif[:, l % 2, :].rearrange("p (n b) -> p n b", b=2 * b), g, ref, ALU.subtract).then_inc(diff_ready, 1)

            def step(h):
                dve.wait_ge(proj_done, 4 * h + 2)
                nc.vector.tensor_scalar(fbuf[:, :], b_f[:, :], -44.0, None, ALU.max).then_inc(f_clamped, 1)
                dve.wait_ge(sig_ready, h + 1)
                lb, omlb = k.lb[:, 0, bass.ds(h, 1)], k.lb[:, 1, bass.ds(h, 1)]
                ch.link(nc.vector.tensor_scalar(sig[:, :], sig[:, :], omlb, None, ALU.mult))
                nc.vector.tensor_scalar(fbuf[:, :], sig[:, :], lb, None, ALU.add).then_inc(ft_ready, 1)
                nc.vector.tensor_tensor(kk[:, :], ef[:, :], sig[:, :], ALU.mult)
                dve.wait_ge(logf_ready, h + 1)
                ch.link(nc.vector.tensor_tensor_scan(G[:, :], k.c("reset"), logf[:, :], 0.0, ALU.mult, ALU.add))
                nc.vector.tensor_tensor(chunks(kdf), chunks(G), chunks(G)[:, :, P - 1:P].to_broadcast([P, NT, P]), ALU.subtract).then_inc(g_ready, 1)
                diff(h, 0)
                diff(h, 1)
                dve.wait_ge(lv_done, 8 * h + 1)
                nc.vector.tensor_tensor(chunks(at), chunks(b_x0), mask("ident", 0), ALU.mult).then_inc(at_done, 1)
                for l in range(NL):
                    dve.wait_ge(lv_done, 8 * h + l + 2)
                    dve.wait_ge(at_done, 8 * h + l + 1)
                    if l + 2 < NL:
                        diff(h, l + 2)
                    else:
                        nc.vector.memset(tick[:, l + 2 - NL:l + 3 - NL], 0.0)
                    nc.vector.copy_predicated(chunks(at), mask("levels", l * P).bitcast(U32), chunks(b_x[(l + 1) % 2])).then_inc(at_done, 1)
                dve.wait_ge(kv_done, h + 1)
                ch.link(nc.vector.tensor_copy(S[:, 0, :], b_kv[:, 0:P]))
                ch.link(nc.vector.scalar_tensor_tensor(S[:, 1, :], S[:, 0, :], E[:, 2 * P - 1:2 * P], b_kv[:, P:2 * P], ALU.mult, ALU.add))
                nc.vector.scalar_tensor_tensor(S[:, 2, :], S[:, 1, :], E[:, 3 * P - 1:3 * P], b_kv[:, 2 * P:3 * P], ALU.mult, ALU.add).then_inc(s_ready, 1)
                dve.wait_ge(osb_ready, h + 1)
                ch.link(nc.vector.tensor_tensor(gate[:, :], gate[:, :], osb[:, :], ALU.mult))
                dve.wait_ge(rs_ready, h + 1)
                nc.vector.scalar_tensor_tensor(k.y[:, bass.ds(h, 1), :].rearrange("p a t -> p (a t)"), gate[:, :], k.p("cnorm", h),
                                               k.rstd[:, :], ALU.mult, ALU.mult).then_inc(y_ready, 1)

            with dve.Fori(0, H) as h:
                ch.loop(5, h)
                step(h)
            ch.end(H)


HA = 4
CAP = 15.0


@phase
def ab_gates(k, weights):
    nc = k.nc
    sem, sb = k.sem, k.sb
    R = sb("gate_rows", [HA, 12, T], F32)
    A = sb("decay_rate", [HA, 1], F32)
    r_i, r_f, r_a, r_b, r_sp, r_F, r_Aa, r_M, r_e, r_abs, r_G, r_t = (R[:, i, :] for i in range(12))
    w_loaded, proj_done, rows_taken, tanh_done, e1, l1, e2, rows_ready, spread, spread_used, turned, cols_ready, cexp, ch_d, ch_a = (
        sem("ab_" + s) for s in ("gw_loaded proj_done rows_taken tanh_done exp1 ln1 beta_ready rows_ready spread spread_used "
                                 "turned cols_ready cols_exp ch_dve ch_act").split())
    gb = lambda i: k.p("gbias", i)[0:HA]
    with nc.Block() as block:
        @block.sync
        def _(sp):
            sp.dma_start(k.w[:, 0, :], weights[0, :, :]).then_inc(w_loaded, 16)

        @block.tensor
        def _(pe):
            pe.wait_ge(w_loaded, 16)
            for m in range(KD):
                ins = nc.tensor.matmul(k.ps[0][:, :], k.w[:, 0, m * P:(m + 1) * P], k.u[:, m, :], start=m == 0, stop=m == KD - 1)
            ins.then_inc(proj_done, 1)
            pe.wait_ge(rows_ready, 1)
            pe.wait_ge(e2, 1)
            n = 0
            for kind, row in enumerate((r_M, r_e, r_G, r_b)):
                for h in range(HA):
                    if n >= 4:
                        pe.wait_ge(spread_used, n - 3)
                    nc.tensor.matmul(k.ps[1 + n % 4][:, :], k.c("sel", h * P, h * P + P)[0:HA, :], row, start=True, stop=True).then_inc(spread, 1)
                    n += 1
            for kind, row in enumerate((r_Aa, r_G, r_b)):
                for c in range(NT):
                    at = (kind * NT + c) * HA
                    ins = nc.tensor.transpose(k.ps[5][:, at:at + HA], row[:, c * P:(c + 1) * P], k.c("ident", 0, HA)[0:HA, :])
            ins.then_inc(turned, 1)

        @block.vector
        def _(dve):
            ch = Chain(dve, ch_d)
            dve.wait_ge(proj_done, 1)
            nc.vector.tensor_scalar(r_i, k.ps[0][0:HA, :], gb(0), 1.0 / CAP, ALU.add, ALU.mult)
            ch.link(nc.vector.tensor_copy(r_f, k.ps[0][32:32 + HA, :]))
            nc.vector.tensor_scalar(r_f, r_f, gb(1), 1.0 / CAP, ALU.add, ALU.mult)
            ch.link(nc.vector.tensor_copy(r_a, k.ps[0][64:64 + HA, :]))
            ch.link(nc.vector.tensor_scalar(r_a, r_a, k.p("adt", 1)[0:HA], None, ALU.add))
            nc.vector.scalar_tensor_tensor(r_abs, r_a, -1.0, r_a, ALU.mult, ALU.max)
            ch.link(nc.vector.tensor_scalar(r_b, k.ps[0][96:96 + HA, :], -44.0, None, ALU.max))
            nc.vector.tensor_scalar(r_a, r_a, 0.0, None, ALU.max).then_inc(rows_taken, 1)
            dve.wait_ge(tanh_done, 1)
            nc.vector.tensor_scalar(r_i, r_i, CAP, None, ALU.mult)
            dve.wait_ge(l1, 1)
            dve.wait_ge(rows_taken, 1)
            ch.link(nc.vector.tensor_tensor_scan(r_F, r_sp, r_sp, 0.0, ALU.add, ALU.max))
            ch.link(nc.vector.tensor_tensor(r_Aa, r_i, r_F, ALU.add))
            ch.link(nc.vector.tensor_tensor_scan(r_M, r_Aa, r_Aa, 0.0, ALU.max, ALU.max))
            nc.vector.tensor_tensor(r_e, r_F, r_M, ALU.subtract)
            ch.link(nc.vector.tensor_tensor(r_t, r_a, r_abs, ALU.add))
            ch.link(nc.vector.tensor_scalar(r_t, r_t, A[:, 0:1], None, ALU.mult))
            nc.vector.tensor_tensor_scan(r_G, k.c("reset")[0:HA, :], r_t, 0.0, ALU.mult, ALU.add).then_inc(rows_ready, 1)
            for n in (0, 1, 2, 3, 8, 9, 10, 11, 12, 13, 14, 15):
                kind, h = divmod(n, HA)
                dve.wait_ge(spread, n + 1)
                if n == 8:
                    dve.wait_ge(spread_used, 8)
                nc.vector.tensor_copy(k.bc[:, kind, h, :], k.ps[1 + n % 4][:, :]).then_inc(spread_used, 1)
            dve.wait_ge(turned, 1)
            dve.wait_ge(spread_used, 16)
            t = k.ps[5][:, 0:3 * NT * HA].rearrange("p (k c h) -> p k h c", k=3, c=NT)
            ch.link(nc.vector.tensor_copy(k.cols[:, 0:3, :, :], t))
            last = k.bc[:, 2, :, :].rearrange("p h (c l) -> p h c l", l=P)[:, :, :, P - 1]
            nc.vector.tensor_copy(k.cols[:, 5, :, :], last)
            ch.link(nc.vector.tensor_tensor(k.cols[:, 3, :, :], k.cols[:, 1, :, :], last, ALU.subtract))
            nc.vector.tensor_copy(k.cols[:, 4, :, :], k.cols[:, 1, :, :]).then_inc(cols_ready, 1)
            dve.wait_ge(cexp, 1)
            ch.link(nc.vector.tensor_tensor(k.cols[:, 4, :, :], k.cols[:, 4, :, :], k.cols[:, 2, :, :], ALU.mult))

        @block.scalar
        def _(act):
            ch = Chain(act, ch_a)
            act.wait_ge(rows_taken, 1)
            ch.link(nc.scalar.activation(R[:, 0:2, :], R[:, 0:2, :], ACT.Tanh))
            nc.scalar.activation(r_t, r_f, ACT.Copy, scale=CAP).then_inc(tanh_done, 1)
            nc.scalar.preload_act_table_set(LNEXP)
            act.wait_ge(tanh_done, 1)
            nc.scalar.activation(r_sp, r_t, ACT.Exp, scale=-1.0)
            nc.scalar.activation(r_abs, r_abs, ACT.Exp, scale=-1.0)
            nc.scalar.activation(A[:, 0:1], k.p("adt", 0)[0:HA], ACT.Exp)
            ch.link(nc.scalar.activation(r_b, r_b, ACT.Exp, scale=-1.0))
            nc.scalar.activation(r_sp, r_sp, ACT.Ln, bias=1.0)
            nc.scalar.activation(r_abs, r_abs, ACT.Ln, bias=1.0).then_inc(l1, 1)
            ch.link(nc.scalar.activation(r_b, r_b, ACT.Ln, bias=1.0))
            nc.scalar.activation(r_b, r_b, ACT.Exp, scale=-1.0).then_inc(e2, 1)
            for n in range(4, 8):
                act.wait_ge(spread, n + 1)
                act.wait_ge(spread_used, n)
                nc.scalar.activation(k.bc[:, 1, n - 4, :], k.ps[1 + n % 4][:, :], ACT.Exp).then_inc(spread_used, 1)
            act.wait_ge(cols_ready, 1)
            nc.scalar.activation(k.cols[:, 3, :, :], k.cols[:, 3, :, :], ACT.Exp)
            nc.scalar.activation(k.cols[:, 4:6, :, :], k.cols[:, 4:6, :, :], ACT.Exp, scale=-1.0).then_inc(cexp, 1)


@phase
def mlstm(k, weights):
    nc = k.nc
    sem, sb = k.sem, k.sb
    H = HA
    DK = 64
    acc, q, kk, v, og, osb, den = (sb(f"m_{s}", [n, T], F32) for s, n in
                                   (("acc", P), ("q", DK), ("k", DK), ("v", P), ("og", P), ("o", P), ("den", P)))
    hc = sb("m_hc", [P, NT], F32)
    off = [0, 512, 896, 1152, 1280]
    W = sb("m_W", [P, off[4]], F32)
    b_qk, b_o, b_v, _, b_s0, b_s1, b_num, b_den = k.ps
    b_s = [b_s0, b_s1]
    w_loaded = [sem(f"m_w_loaded{s}") for s in range(3)]
    (proj_done, tap_done, conv_done, act_prep, o_clamped, qk_ready, og_ready, arg_ready, d_ready, st_done, wt_ready, pv_done,
     osb_ready, osq_ready, nrm_done, rs_ready, y_ready, ch_act, ch_dve) = (sem("m_" + s) for s in (
         "proj_done tap_done conv_done act_prep o_clamped qk_ready og_ready arg_ready d_ready st_done wt_ready pv_done "
         "osb_ready osq_ready nrm_done rs_ready y_ready ch_act ch_dve").split())

    with nc.Block() as block:
        @block.sync
        def _(sp):
            for s in range(3):
                sp.dma_start(k.w[:, s, :], weights[s, :, :]).then_inc(w_loaded[s], 16)
            with sp.Fori(1, H) as h:
                for s in range(3):
                    sp.wait_ge(proj_done, 3 * h - 2 + s)
                    sp.dma_start(k.w[:, s:s + 1, :], weights[bass.ds(3 * h + s, 1), :, :].rearrange("a p d -> p a d")).then_inc(w_loaded[s], 16)

        @block.tensor
        def _(pe):
            def project(h, s, first=False):
                pe.wait_ge(w_loaded[s], 16 * h + 16)
                if not first:
                    if s == 0:
                        pe.wait_ge(conv_done, h)
                    elif s == 1:
                        pe.wait_ge(o_clamped, h)
                    else:
                        pe.wait_ge(act_prep, h)
                if s < 2:
                    for m in range(KD):
                        ins = nc.tensor.matmul(k.ps[s][:, :], k.w[:, s, m * P:(m + 1) * P], k.u[:, m, :], start=m == 0, stop=m == KD - 1)
                else:
                    for j in range(NT):
                        for m in range(KD):
                            ins = nc.tensor.matmul(b_v[:, j * P:(j + 1) * P], k.u[:, m, j * P:(j + 1) * P], k.w[:, s, m * P:(m + 1) * P],
                                                   start=m == 0, stop=m == KD - 1)
                ins.then_inc(proj_done, 1)

            def score(h, j):
                if j >= 2:
                    pe.wait_ge(wt_ready, 4 * h + j - 1)
                nc.tensor.matmul(b_s[j % 2][:, 0:T - j * P], kk[:, j * P:(j + 1) * P], q[:, j * P:T], start=True, stop=True).then_inc(st_done, 1)

            def core(h, nxt, first):
                if nxt:
                    project(h + 1, 0)
                pe.wait_ge(qk_ready, h + 1)
                if not first:
                    pe.wait_ge(rs_ready, h)
                score(h, 0)
                score(h, 1)
                if nxt:
                    project(h + 1, 1)
                score(h, 2)
                score(h, 3)
                pe.wait_ge(act_prep, h + 1)
                for j in range(NT):
                    pe.wait_ge(wt_ready, 4 * h + j + 1)
                    w = W[:, off[j]:off[j + 1]]
                    nc.tensor.matmul(b_num[:, j * P:T], v[:, j * P:(j + 1) * P], w, start=j == 0, stop=j == NT - 1)
                    ins = nc.tensor.matmul(b_den[:, j * P:T], k.c("ones"), w, start=j == 0, stop=j == NT - 1)
                ins.then_inc(pv_done, 1)
                if nxt:
                    project(h + 1, 2)
                pe.wait_ge(osq_ready, h + 1)
                nc.tensor.matmul(b_s0[:, :], k.c("ones"), k.sq[:, 0, :], start=True, stop=True).then_inc(nrm_done, 1)

            for s in range(3):
                project(0, s, first=True)
            core(0, True, True)
            with pe.Fori(1, H - 1) as h:
                core(h, True, False)
            core(H - 1, False, False)

        @block.scalar
        def _(act):
            ch = Chain(act, ch_act)

            def step(h):
                act.wait_ge(proj_done, 3 * h + 1)
                nc.scalar.activation(acc[:, :], b_qk[:, :], ACT.Copy, scale=k.p("mconv", 4 * h + 3)).then_inc(tap_done, 1)
                act.wait_ge(proj_done, 3 * h + 3)
                nc.scalar.activation(v[:, :], b_v[:, :], ACT.Copy).then_inc(act_prep, 1)
                act.wait_ge(conv_done, h + 1)
                nc.scalar.activation(q[:, :], acc[0:DK, :], ACT.Silu)
                nc.scalar.activation(kk[:, :], acc[DK:P, :], ACT.Silu).then_inc(qk_ready, 1)
                nc.scalar.preload_act_table_set(LNEXP)
                act.wait_ge(arg_ready, h + 1)
                nc.scalar.activation(W[:, :], W[:, :], ACT.Exp, scale=-1.0).then_inc(d_ready, 1)
                act.wait_ge(o_clamped, h + 1)
                ch.link(nc.scalar.activation(og[:, :], og[:, :], ACT.Exp, scale=-1.0))
                ch.link(nc.scalar.activation(og[:, :], og[:, :], ACT.Ln, bias=1.0))
                nc.scalar.activation(og[:, :], og[:, :], ACT.Exp, scale=-1.0).then_inc(og_ready, 1)
                act.wait_ge(osb_ready, h + 1)
                nc.scalar.activation(k.sq[:, 0, :], osb[:, :], ACT.Square).then_inc(osq_ready, 1)
                act.wait_ge(nrm_done, h + 1)
                ch.link(nc.scalar.activation(k.rstd[:, :], b_s0[:, :], ACT.Ln, bias=k.epsc[:, 0:1], scale=1.0 / P))
                nc.scalar.activation(k.rstd[:, :], k.rstd[:, :], ACT.Exp, scale=-0.5).then_inc(rs_ready, 1)

            with act.Fori(0, H) as h:
                ch.loop(3, h)
                step(h)
            ch.end(H)

        @block.vector
        def _(dve):
            ch = Chain(dve, ch_dve)

            def step(h):
                ch.link(nc.vector.tensor_copy(hc[:, :].rearrange("p (a c) -> p a c", a=1), k.cols[:, 0, bass.ds(h, 1), :]))
                for j in range(NT):
                    ins = nc.vector.tensor_scalar(W[:, off[j]:off[j + 1]].rearrange("p (a t) -> p a t", a=1),
                                                  k.bc[:, 0, bass.ds(h, 1), j * P:T], hc[:, j:j + 1], 0.0, ALU.subtract, ALU.max)
                ins.then_inc(arg_ready, 1)
                dve.wait_ge(tap_done, h + 1)
                for tap in (2, 1, 0):
                    ins = nc.vector.scalar_tensor_tensor(acc[:, 3 - tap:T], b_qk[:, 0:T - 3 + tap], k.p("mconv", 4 * h + tap), acc[:, 3 - tap:T], ALU.mult, ALU.add)
                    if tap:
                        ch.link(ins)
                ins.then_inc(conv_done, 1)
                dve.wait_ge(proj_done, 3 * h + 2)
                nc.vector.tensor_scalar(og[:, :], b_o[:, :], -44.0, None, ALU.max).then_inc(o_clamped, 1)
                dve.wait_ge(d_ready, h + 1)
                for j in range(NT):
                    dve.wait_ge(st_done, 4 * h + j + 1)
                    w = W[:, off[j]:off[j + 1]]
                    ch.link(nc.vector.scalar_tensor_tensor(w, b_s[j % 2][:, 0:T - j * P], DK ** -0.5, w, ALU.mult, ALU.mult))
                    nc.vector.tensor_tensor(w[:, 0:P], w[:, 0:P], k.c("upper"), ALU.mult).then_inc(wt_ready, 1)
                dve.wait_ge(pv_done, h + 1)
                ch.link(nc.vector.scalar_tensor_tensor(den[:, :].rearrange("p (a t) -> p a t", a=1), b_den[:, :].rearrange("p (a t) -> p a t", a=1), -1.0,
                                                       k.bc[:, 1, bass.ds(h, 1), :], ALU.mult, ALU.max))
                ch.link(nc.vector.tensor_tensor(den[:, :], den[:, :], b_den[:, :], ALU.max))
                ch.link(nc.vector.reciprocal(den[:, :], den[:, :]))
                nc.vector.tensor_tensor(osb[:, :], b_num[:, :], den[:, :], ALU.mult).then_inc(osb_ready, 1)
                dve.wait_ge(og_ready, h + 1)
                dve.wait_ge(osb_ready, h + 1)
                ch.link(nc.vector.tensor_tensor(og[:, :], og[:, :], osb[:, :], ALU.mult))
                dve.wait_ge(rs_ready, h + 1)
                nc.vector.scalar_tensor_tensor(k.y[:, bass.ds(h, 1), :].rearrange("p a t -> p (a t)"), og[:, :], k.p("mnorm", h),
                                               k.rstd[:, :], ALU.mult, ALU.mult).then_inc(y_ready, 1)
                dve.wait_ge(y_ready, h + 1)

            with dve.Fori(0, H) as h:
                ch.loop(1 + 2 + NT + 4, h)
                step(h)
            ch.end(H)


@phase
def delta(k, weights):
    nc = k.nc
    sem, sb = k.sem, k.sb
    H, NL = HA, len(LEVELS)
    scale = P ** -0.5
    q, kk, v, gate, rk, dec, db, at, At, EG, qd, kd, kb, vb, BT, Tm, TT, Y, nwT, vn, osb = (sb("g_" + s, [P, T], F32) for s in (
        "q k v gate rk dec db attn At EG qd kd kb vb BT T TT Y nwT vn o").split())
    S = sb("g_S", [P, NT - 1, P], F32)
    hc = sb("g_hc", [P, 6, NT], F32)
    b0, b1, b2, b3, b4, b5, b6, b7 = k.ps
    conv = ((b0, q), (b1, kk), (b2, v))
    w_loaded = [sem(f"g_w_loaded{s}") for s in range(4)]
    (proj_done, tap_done, conv_done, silu_done, gate_done, hc_ready, sq_ready, nrm_qk, rqk_ready, qk_ready, qk_turned, v_turned, kdb_ready,
     vb_ready, kk_done, arg_ready, dec_ready, eg_ready, masked, db_ready, t_ready, bt_ready, y_done, y_copied, z_done, w_done, nw_ready, vn_done, vn_ready,
     kv_done, s_ready, o_done, osb_ready, osq_ready, nrm_done, rs_ready, y_ready, qd_ready, ch_act, ch_dve, ch_pool) = (sem("g_" + s) for s in (
         "proj_done tap_done conv_done silu_done gate_done hc_ready sq_ready nrm_qk rqk_ready qk_ready qk_turned v_turned kdb_ready "
         "vb_ready kk_done arg_ready dec_ready eg_ready masked db_ready t_ready bt_ready y_done y_copied z_done w_done nw_ready vn_done vn_ready "
         "kv_done s_ready o_done osb_ready osq_ready nrm_done rs_ready y_ready qd_ready ch_act ch_dve ch_pool").split())

    def cs(c):
        return slice(c * P, (c + 1) * P)

    def chunks(x):
        return x[:, :].rearrange("p (c l) -> p c l", l=P)

    def mask(name, lo=0):
        return k.c(name, lo, lo + P).rearrange("p (a l) -> p a l", a=1).to_broadcast([P, NT, P])

    def row(kind, h):
        return k.bc[:, kind, bass.ds(h, 1), :]

    def one(x):
        return x.rearrange("p (a t) -> p a t", a=1)

    with nc.Block() as block:
        @block.sync
        def _(sp):
            for s in range(4):
                sp.dma_start(k.w[:, s, :], weights[s, :, :]).then_inc(w_loaded[s], 16)
            with sp.Fori(1, H) as h:
                for s in range(4):
                    sp.wait_ge(proj_done, 4 * h - 3 + s)
                    sp.dma_start(k.w[:, s:s + 1, :], weights[bass.ds(4 * h + s, 1), :, :].rearrange("a p d -> p a d")).then_inc(w_loaded[s], 16)

        @block.tensor
        def _(pe):
            def project(h, lo, hi, first=False):
                for n in range(lo, hi):
                    s, m = divmod(n, KD)
                    if m == 0:
                        pe.wait_ge(w_loaded[s], 16 * h + 16)
                        if not first:
                            if s < 3:
                                pe.wait_ge(conv_done, 3 * h - 2 + s)
                            else:
                                pe.wait_ge(gate_done, h)
                    ins = nc.tensor.matmul(k.ps[s][:, :], k.w[:, s, m * P:(m + 1) * P], k.u[:, m, :], start=m == 0, stop=m == KD - 1)
                    if m == KD - 1:
                        ins.then_inc(proj_done, 1)

            def four(bank, lhsT, rhs, cols=None):
                for c in range(NT):
                    ins = nc.tensor.matmul(bank[:, cs(c)], lhsT[:, cs(c)], rhs[:, cs(c)], start=True, stop=True)
                return ins

            def core(h, nxt, first):
                fill = (lambda lo, hi: project(h + 1, lo, hi)) if nxt else (lambda lo, hi: None)
                fill(0, 4)
                if not first:
                    pe.wait_ge(rs_ready, h)
                pe.wait_ge(sq_ready, h + 1)
                nc.tensor.matmul(b4[:, :], k.c("ones"), k.sq[:, 0, :], start=True, stop=True)
                nc.tensor.matmul(b5[:, :], k.c("ones"), k.sq[:, 1, :], start=True, stop=True).then_inc(nrm_qk, 1)
                if not first:
                    pe.wait_ge(osb_ready, h)
                for c in range(NT):
                    ins = nc.tensor.transpose(b7[:, cs(c)], v[:, cs(c)], k.c("ident"))
                ins.then_inc(v_turned, 1)
                fill(4, 8)
                pe.wait_ge(qk_ready, h + 1)
                for c in range(NT):
                    ins = nc.tensor.transpose(b6[:, cs(c)], kk[:, cs(c)], k.c("ident"))
                ins.then_inc(qk_turned, 1)
                four(b4, kk, kk)
                four(b5, kk, q).then_inc(kk_done, 1)
                fill(8, 11)
                for l in range(NL):
                    pe.wait_ge(bt_ready, NL * h + l + 1)
                    pe.wait_ge(t_ready, 8 * h + l + 1)
                    four(b4, BT, Tm).then_inc(y_done, 1)
                    fill(11 + 3 * l, 12 + 3 * l)
                    pe.wait_ge(y_copied, NL * h + l + 1)
                    if l == 0:
                        pe.wait_ge(kdb_ready, h + 1)
                    four(b5, TT, Y)
                    four(b6, Y, TT).then_inc(z_done, 1)
                    fill(12 + 3 * l, 14 + 3 * l)
                pe.wait_ge(t_ready, 8 * h + 8)
                for c in range(1, NT):
                    ins = nc.tensor.matmul(b4[:, cs(c)], kb[:, cs(c)], TT[:, cs(c)], start=True, stop=True)
                ins.then_inc(w_done, 1)
                pe.wait_ge(vb_ready, h + 1)
                pe.wait_ge(qd_ready, h + 1)
                for c in range(NT):
                    if c == 1:
                        pe.wait_ge(nw_ready, h + 1)
                    ins = nc.tensor.matmul(b5[:, cs(c)], TT[:, cs(c)], vb[:, cs(c)], start=True, stop=c == 0)
                    if c:
                        pe.wait_ge(s_ready, 3 * h + c)
                        ins = nc.tensor.matmul(b5[:, cs(c)], nwT[:, cs(c)], S[:, c - 1, :], start=False, stop=True)
                    ins.then_inc(vn_done, 1)
                    if c:
                        nc.tensor.matmul(b7[:, cs(c)], S[:, c - 1, :], qd[:, cs(c)], start=True, stop=False)
                    pe.wait_ge(vn_ready, 4 * h + c + 1)
                    ins = nc.tensor.matmul(b7[:, cs(c)], vn[:, cs(c)], at[:, cs(c)], start=c == 0, stop=True)
                    if c == NT - 1:
                        ins.then_inc(o_done, 1)
                    else:
                        nc.tensor.matmul(b6[:, cs(c)], kd[:, cs(c)], vn[:, cs(c)], start=True, stop=True).then_inc(kv_done, 1)
                pe.wait_ge(osq_ready, h + 1)
                nc.tensor.matmul(b4[:, :], k.c("ones"), k.sq[:, 0, :], start=True, stop=True).then_inc(nrm_done, 1)

            project(0, 0, 32, first=True)
            core(0, True, True)
            with pe.Fori(1, H - 1) as h:
                core(h, True, False)
            core(H - 1, False, False)

        @block.scalar
        def _(act):
            ch = Chain(act, ch_act)

            def step(h):
                for i, (bank, x) in enumerate(conv):
                    act.wait_ge(proj_done, 4 * h + i + 1)
                    nc.scalar.activation(x[:, :], bank[:, :], ACT.Copy, scale=k.p("gconv", 12 * h + 4 * i + 3)).then_inc(tap_done, 1)
                act.wait_ge(proj_done, 4 * h + 4)
                nc.scalar.activation(gate[:, :], b3[:, :], ACT.Silu).then_inc(gate_done, 1)
                for i, (bank, x) in enumerate(conv):
                    act.wait_ge(conv_done, 3 * h + i + 1)
                    nc.scalar.activation(x[:, :], x[:, :], ACT.Silu).then_inc(silu_done, 1)
                act.wait_ge(silu_done, 3 * h + 3)
                nc.scalar.activation(k.sq[:, 0, :], q[:, :], ACT.Square)
                nc.scalar.activation(k.sq[:, 1, :], kk[:, :], ACT.Square).then_inc(sq_ready, 1)
                nc.scalar.preload_act_table_set(LNEXP)
                act.wait_ge(nrm_qk, h + 1)
                nc.scalar.activation(k.rstd[:, :], b4[:, :], ACT.Ln, bias=k.epsc[:, 0:1])
                ch.link(nc.scalar.activation(rk[:, :], b5[:, :], ACT.Ln, bias=k.epsc[:, 0:1]))
                nc.scalar.activation(k.rstd[:, :], k.rstd[:, :], ACT.Exp, scale=-0.5)
                nc.scalar.activation(rk[:, :], rk[:, :], ACT.Exp, scale=-0.5).then_inc(rqk_ready, 1)
                act.wait_ge(v_turned, h + 1)
                act.wait_ge(hc_ready, h + 1)
                for c in range(NT):
                    ins = nc.scalar.activation(vb[:, cs(c)], b7[:, cs(c)], ACT.Copy, scale=hc[:, 2, c:c + 1])
                ins.then_inc(vb_ready, 1)
                act.wait_ge(arg_ready, h + 1)
                nc.scalar.activation(dec[:, :], dec[:, :], ACT.Exp, scale=-1.0).then_inc(dec_ready, 1)
                nc.scalar.activation(one(EG[:, :]), row(2, h), ACT.Exp, scale=-1.0).then_inc(eg_ready, 1)
                for l in range(NL):
                    act.wait_ge(y_done, NL * h + l + 1)
                    nc.scalar.activation(Y[:, :], b4[:, :], ACT.Copy).then_inc(y_copied, 1)
                act.wait_ge(w_done, h + 1)
                nc.scalar.activation(nwT[:, P:T], b4[:, P:T], ACT.Copy, scale=-1.0).then_inc(nw_ready, 1)
                for c in range(NT):
                    act.wait_ge(vn_done, NT * h + c + 1)
                    nc.scalar.activation(vn[:, cs(c)], b5[:, cs(c)], ACT.Copy).then_inc(vn_ready, 1)
                act.wait_ge(o_done, h + 1)
                nc.scalar.activation(osb[:, :], b7[:, :], ACT.Copy, scale=scale).then_inc(osb_ready, 1)
                act.wait_ge(osb_ready, h + 1)
                nc.scalar.activation(k.sq[:, 0, :], osb[:, :], ACT.Square).then_inc(osq_ready, 1)
                act.wait_ge(nrm_done, h + 1)
                ch.link(nc.scalar.activation(k.rstd[:, :], b4[:, :], ACT.Ln, bias=k.epsc[:, 0:1], scale=1.0 / P))
                nc.scalar.activation(k.rstd[:, :], k.rstd[:, :], ACT.Exp, scale=-0.5).then_inc(rs_ready, 1)
                act.wait_ge(y_ready, h + 1)

            with act.Fori(0, H) as h:
                ch.loop(2, h)
                step(h)
            ch.end(H)

        @block.gpsimd
        def _(pool):
            ch = Chain(pool, ch_pool)

            def step(h):
                pool.wait_ge(dec_ready, h + 1)
                ch.link(nc.gpsimd.tensor_tensor(chunks(dec), chunks(dec), mask("upper"), ALU.mult))
                nc.gpsimd.tensor_tensor(one(db[:, :]), one(dec[:, :]), row(3, h), ALU.mult).then_inc(db_ready, 1)
                pool.wait_ge(eg_ready, h + 1)
                pool.wait_ge(qk_ready, h + 1)
                nc.gpsimd.tensor_tensor(qd[:, :], q[:, :], EG[:, :], ALU.mult).then_inc(qd_ready, 1)
                pool.wait_ge(masked, h + 1)
                for l in range(NL):
                    if l:
                        pool.wait_ge(y_done, NL * h + l)
                    nc.gpsimd.tensor_tensor(chunks(BT), chunks(At), mask("levels", l * P), ALU.mult).then_inc(bt_ready, 1)

            with pool.Fori(0, H) as h:
                ch.loop(1, h)
                step(h)
            ch.end(H)

        @block.vector
        def _(dve):
            ch = Chain(dve, ch_dve)

            def step(h):
                nc.vector.tensor_copy(hc[:, :, :].rearrange("p k (a c) -> p k a c", a=1), k.cols[:, :, bass.ds(h, 1), :]).then_inc(hc_ready, 1)
                for i, (bank, x) in enumerate(conv):
                    dve.wait_ge(tap_done, 3 * h + i + 1)
                    for tap in (2, 1, 0):
                        ins = nc.vector.scalar_tensor_tensor(x[:, 3 - tap:T], bank[:, 0:T - 3 + tap], k.p("gconv", 12 * h + 4 * i + tap), x[:, 3 - tap:T], ALU.mult, ALU.add)
                        if tap:
                            ch.link(ins)
                    ins.then_inc(conv_done, 1)
                dve.wait_ge(hc_ready, h + 1)
                for c in range(NT):
                    g = k.bc[:, 2, bass.ds(h, 1), cs(c)]
                    ins = nc.vector.tensor_scalar(one(dec[:, cs(c)]), g, hc[:, 1, c:c + 1], 0.0, ALU.subtract, ALU.max)
                ins.then_inc(arg_ready, 1)
                nc.vector.tensor_copy(chunks(Tm), mask("ident"))
                nc.vector.tensor_copy(chunks(TT), mask("ident")).then_inc(t_ready, 1)
                dve.wait_ge(rqk_ready, h + 1)
                nc.vector.tensor_tensor(kk[:, :], kk[:, :], rk[:, :], ALU.mult)
                nc.vector.tensor_tensor(q[:, :], q[:, :], k.rstd[:, :], ALU.mult).then_inc(qk_ready, 1)
                dve.wait_ge(kk_done, h + 1)
                dve.wait_ge(db_ready, h + 1)
                nc.vector.tensor_tensor(At[:, :], b4[:, :], db[:, :], ALU.mult).then_inc(masked, 1)
                nc.vector.tensor_tensor(at[:, :], b5[:, :], dec[:, :], ALU.mult)
                for c in range(NT):
                    nc.vector.tensor_scalar(kd[:, cs(c)], b6[:, cs(c)], hc[:, 3, c:c + 1], None, ALU.mult)
                    ins = nc.vector.tensor_scalar(kb[:, cs(c)], b6[:, cs(c)], hc[:, 4, c:c + 1], None, ALU.mult)
                ins.then_inc(kdb_ready, 1)
                for l in range(NL):
                    dve.wait_ge(z_done, NL * h + l + 1)
                    dve.wait_ge(t_ready, 8 * h + l + 1)
                    nc.vector.tensor_tensor(Tm[:, :], Tm[:, :], b5[:, :], ALU.subtract)
                    nc.vector.tensor_tensor(TT[:, :], TT[:, :], b6[:, :], ALU.subtract).then_inc(t_ready, 1)
                for c in range(NT - 1):
                    dve.wait_ge(kv_done, 3 * h + c + 1)
                    if c == 0:
                        nc.vector.tensor_copy(S[:, 0, :], b6[:, cs(0)]).then_inc(s_ready, 1)
                    else:
                        dve.wait_ge(s_ready, 3 * h + c)
                        nc.vector.scalar_tensor_tensor(S[:, c, :], S[:, c - 1, :], hc[:, 5, c:c + 1], b6[:, cs(c)], ALU.mult, ALU.add).then_inc(s_ready, 1)
                dve.wait_ge(osb_ready, h + 1)
                ch.link(nc.vector.tensor_tensor(gate[:, :], gate[:, :], osb[:, :], ALU.mult))
                dve.wait_ge(rs_ready, h + 1)
                nc.vector.scalar_tensor_tensor(k.y[:, bass.ds(HA + h, 1), :].rearrange("p a t -> p (a t)"), gate[:, :], k.p("gnorm", h),
                                               k.rstd[:, :], ALU.mult, ALU.mult).then_inc(y_ready, 1)
                dve.wait_ge(y_ready, h + 1)

            with dve.Fori(0, H) as h:
                ch.loop(7, h)
                step(h)
            ch.end(H)


HI, DI = 8, 32
HF = 6
DH = 64
TOPK = 128
NEG = -3e38
OFF = [0, P, 3 * P, 6 * P, 10 * P]


@phase
def shared_inputs(k, weights, pool_w):
    nc = k.nc
    sem, sb = k.sem, k.sb
    rows = sb("s_rows", [HI, 4, T], F32)
    iq = sb("s_iq", [P, 2, T], F32)
    ik = sb("s_ik", [P, T], F32)
    pv, pg, pp, pw = (sb("s_" + s, [P, 2, n], F32) for s, n in (("pv", T), ("pg", T), ("pp", T), ("pw", P)))
    s2 = sb("s_sum", [P, 2, T], F32)
    relu = sb("s_relu", [P, 2, T], F32)
    iw = sb("s_iw", [P, NT, HI], F32)
    sc = sb("s_score", [P, OFF[4]], F32)
    m8 = sb("s_max8", [P, NT, 8], F32)
    NW = 8
    w_loaded = [sem(f"s_w_loaded{s}") for s in range(4)]
    (pw_loaded, proj_done, bank_free, rows_taken, ln_done, f_ready, spread, spread_used, turned, iw_ready, dots_done, relu_ready,
     relu_used, pool_ready, pool_done, ch_dve, ch_act, ch_tk) = (sem("s_" + s) for s in (
         "pw_loaded proj_done bank_free rows_taken ln_done f_ready spread spread_used turned iw_ready dots_done relu_ready "
         "relu_used pool_ready pool_done ch_dve ch_act ch_topk").split())
    items = [(t, h) for t in range(1, NT) for h in range(HI)]
    r_f, r_n, r_F, r_w = (rows[:, i, :] for i in range(4))

    with nc.Block() as block:
        @block.sync
        def _(sp):
            for n in range(NW):
                if n >= 4:
                    sp.wait_ge(proj_done, n - 3)
                sp.dma_start(k.w[:, n % 4, :], weights[n, :, :]).then_inc(w_loaded[n % 4], 16)
            sp.dma_start(pw[:, :, :], pool_w).then_inc(pw_loaded, 16)

        @block.tensor
        def _(pe):
            def project(n):
                pe.wait_ge(w_loaded[n % 4], 16 * (n // 4) + 16)
                if n == 4:
                    pe.wait_ge(iw_ready, 1)
                if n > 4:
                    pe.wait_ge(bank_free, n - 4)
                for m in range(KD):
                    ins = nc.tensor.matmul(k.ps[n % 4][:, :], k.w[:, n % 4, m * P:(m + 1) * P], k.u[:, m, :], start=m == 0, stop=m == KD - 1)
                ins.then_inc(proj_done, 1)
            for n in range(5):
                project(n)
            pe.wait_ge(iw_ready, 1)
            for t in range(NT):
                ins = nc.tensor.transpose(k.ps[4][:, t * HI:(t + 1) * HI], r_w[:, t * P:(t + 1) * P], k.c("ident", 0, HI)[0:HI, :])
            ins.then_inc(turned, 1)
            pe.wait_ge(bank_free, 3)
            pe.wait_ge(iw_ready, 2)
            for n, (t, h) in enumerate(items):
                if n >= 4:
                    pe.wait_ge(relu_ready, n - 3)
                r = slice(DI * (h % 4), DI * (h % 4) + DI)
                nc.tensor.matmul(k.ps[4 + n % 4][:, 0:(t + 1) * P], iq[r, h // 4, t * P:(t + 1) * P], ik[r, 0:(t + 1) * P],
                                 start=True, stop=True, tile_position=(DI * (h % 4), 0)).then_inc(dots_done, 1)
            for n in range(5, NW):
                project(n)
            pe.wait_ge(f_ready, 1)
            for h in range(HF):
                if h < 4:
                    pe.wait_ge(relu_ready, len(items))
                else:
                    pe.wait_ge(spread_used, h - 3)
                nc.tensor.matmul(k.ps[4 + h % 4][:, :], k.c("sel", h * P, h * P + P)[0:HF, :], r_F[0:HF, :], start=True, stop=True).then_inc(spread, 1)
            pe.wait_ge(pw_loaded, 16)
            pe.wait_ge(pool_ready, 2)
            pe.wait_ge(bank_free, 7)
            for i in range(2):
                nc.tensor.matmul(k.ps[i][:, :], pw[:, i, :], pp[:, i, :], start=True, stop=True).then_inc(pool_done, 1)

        @block.scalar
        def _(act):
            ch = Chain(act, ch_act)
            act.wait_ge(proj_done, 2)
            nc.scalar.activation(ik[:, :], k.ps[1][:, :], ACT.Copy).then_inc(bank_free, 1)
            for i in range(2):
                act.wait_ge(proj_done, 3 + i)
                nc.scalar.activation(iq[:, i, :], k.ps[2 + i][:, :], ACT.Copy).then_inc(bank_free, 1)
            nc.scalar.preload_act_table_set(LNEXP)
            act.wait_ge(rows_taken, 1)
            ch.link(nc.scalar.activation(r_n[0:HF], r_n[0:HF], ACT.Exp, scale=-1.0))
            nc.scalar.activation(r_n[0:HF], r_n[0:HF], ACT.Ln, bias=1.0).then_inc(ln_done, 1)
            for n, (t, h) in enumerate(items):
                act.wait_ge(dots_done, n + 1)
                if n >= 2:
                    act.wait_ge(relu_used, n - 1)
                nc.scalar.activation(relu[:, n % 2, 0:(t + 1) * P], k.ps[4 + n % 4][:, 0:(t + 1) * P], ACT.Relu).then_inc(relu_ready, 1)
                if n == 3:
                    act.wait_ge(proj_done, 5)
                    nc.scalar.activation(pv[:, 0, :], k.ps[0][:, :], ACT.Copy).then_inc(bank_free, 1)
            act.wait_ge(proj_done, 6)
            nc.scalar.activation(pv[:, 1, :], k.ps[1][:, :], ACT.Copy).then_inc(bank_free, 1)
            for i in range(2):
                act.wait_ge(proj_done, 7 + i)
                nc.scalar.activation(pg[:, i, :], k.ps[2 + i][:, :], ACT.Silu).then_inc(bank_free, 1)

        @block.vector
        def _(dve):
            ch = Chain(dve, ch_dve)
            dve.wait_ge(proj_done, 1)
            nc.vector.tensor_scalar(r_f[0:HF], k.ps[0][0:HF, :], k.p("foxb", 0)[0:HF], None, ALU.add)
            nc.vector.tensor_scalar(r_w, k.ps[0][32:32 + HI, :], HI ** -0.5, None, ALU.mult).then_inc(iw_ready, 1)
            dve.wait_ge(iw_ready, 1)
            ch.link(nc.vector.scalar_tensor_tensor(r_n[0:HF], r_f[0:HF], -1.0, r_f[0:HF], ALU.mult, ALU.max))
            nc.vector.tensor_scalar(r_f[0:HF], r_f[0:HF], -1.0, 0.0, ALU.mult, ALU.max).then_inc(rows_taken, 1)
            dve.wait_ge(rows_taken, 1)
            dve.wait_ge(ln_done, 1)
            ch.link(nc.vector.tensor_tensor(r_f[0:HF], r_f[0:HF], r_n[0:HF], ALU.add))
            nc.vector.tensor_tensor_scan(r_F[0:HF], r_f[0:HF], r_f[0:HF], 0.0, ALU.add, ALU.max).then_inc(f_ready, 1)
            dve.wait_ge(turned, 1)
            nc.vector.tensor_copy(iw[:, :, :], k.ps[4][:, 0:NT * HI].rearrange("p (t h) -> p t h", h=HI)).then_inc(iw_ready, 1)
            dve.wait_ge(iw_ready, 2)
            for n, (t, h) in enumerate(items):
                dve.wait_ge(relu_ready, n + 1)
                s, r, w = sc[:, OFF[t]:OFF[t + 1]], relu[:, n % 2, 0:(t + 1) * P], iw[:, t, h:h + 1]
                if h == 0:
                    nc.vector.tensor_scalar(s, r, w, None, ALU.mult).then_inc(relu_used, 1)
                else:
                    dve.wait_ge(relu_used, n)
                    nc.vector.scalar_tensor_tensor(s, r, w, s, ALU.mult, ALU.add).then_inc(relu_used, 1)
                if h == HI - 1:
                    dve.wait_ge(relu_used, n + 1)
                    ch.link(nc.vector.tensor_tensor(s[:, t * P:], s[:, t * P:], k.c("chunkdiag"), ALU.add))
            for i in range(2):
                dve.wait_ge(bank_free, 4 + i)
                src, wins = pv[:, i, :], 2 + 2 * i
                have, keep = src, {}
                for n in range(wins):
                    d, dst = 1 << n, s2[:, n % 2, :]
                    nc.vector.tensor_copy(dst[:, 0:d], have[:, 0:d])
                    ch.link(nc.vector.tensor_tensor(dst[:, d:], have[:, d:], have[:, 0:T - d], ALU.add))
                    have = dst
                rc = k.c("rcount", i * T, (i + 1) * T)
                for half in range(2):
                    r = slice(64 * half, 64 * half + 64)
                    ins = nc.vector.tensor_tensor(pp[r, i, :], s2[r, half, :], rc[r], ALU.mult)
                ch.link(ins)
                nc.vector.tensor_tensor(pp[:, i, :], pp[:, i, :], src, ALU.subtract).then_inc(pool_ready, 1)
            for h in range(HF):
                dve.wait_ge(spread, h + 1)
                nc.vector.tensor_copy(k.fb[:, h, :], k.ps[4 + h % 4][:, :]).then_inc(spread_used, 1)
            for i in range(2):
                dve.wait_ge(pool_done, i + 1)
                ch.link(nc.vector.scalar_tensor_tensor(k.y[:, i, :], k.ps[i][:, :], k.p("pscale", i), pg[:, i, :], ALU.mult, ALU.mult))
            tk = Chain(dve, ch_tk)
            dve.wait_ge(pool_ready, 2)
            for r in range(TOPK // 8):
                for t in range(1, NT):
                    ins = nc.vector.max(m8[:, t, :], sc[:, OFF[t]:OFF[t + 1]])
                tk.link(ins)
                for t in range(1, NT):
                    s = sc[:, OFF[t]:OFF[t + 1]]
                    ins = nc.vector.match_replace(s, m8[:, t, :], s, NEG)
                tk.link(ins)
            nc.vector.tensor_copy(k.bias[:, 0:P], k.c("chunkdiag"))
            nc.vector.tensor_scalar(k.bias[:, P:OFF[4]], sc[:, P:OFF[4]], NEG / 2, -BIG, ALU.is_gt, ALU.mult)


@phase
def attention(k, tag, weights, y0, fox):
    nc = k.nc
    sem, sb = k.sem, k.sb
    NP, NI = HF // 2, 2 * NT
    items = [(a, t) for a in range(2) for t in range(NT)]
    q, kk, v, gate = (sb(f"{tag}_{s}", [P, T], F32) for s in ("q", "k", "v", "gate"))
    L = sb(f"{tag}_logits", [P, 2, T], F32)
    PT = sb(f"{tag}_probsT", [P, 2, T], F32)
    st = sb(f"{tag}_stats", [P, NI, 4], F32)
    w_loaded = [sem(f"{tag}_w_loaded{s}") for s in range(4)]
    (proj_done, act_prep, st_done, logits_ready, max_ready, exp_done, inv_ready, p_ready, turned, pt_ready, pv_done, y_ready, ch_dve) = (
        sem(f"{tag}_{s}") for s in ("proj_done act_prep st_done logits_ready max_ready exp_done inv_ready p_ready turned pt_ready pv_done y_ready ch_dve").split())
    b_s, b_t, b_o = k.ps[4:6], k.ps[6], k.ps[7]

    with nc.Block() as block:
        @block.sync
        def _(sp):
            for s in range(4):
                sp.dma_start(k.w[:, s, :], weights[s, :, :]).then_inc(w_loaded[s], 16)
            with sp.Fori(1, NP) as i:
                for s in range(4):
                    sp.wait_ge(proj_done, 4 * i - 3 + s)
                    sp.dma_start(k.w[:, s:s + 1, :], weights[bass.ds(4 * i + s, 1), :, :].rearrange("a p d -> p a d")).then_inc(w_loaded[s], 16)

        @block.tensor
        def _(pe):
            def project(i, s, first=False):
                pe.wait_ge(w_loaded[s], 16 * i + 16)
                if not first:
                    pe.wait_ge(act_prep, 4 * i - 3 + s)
                if s < 3:
                    for m in range(KD):
                        ins = nc.tensor.matmul(k.ps[s][:, :], k.w[:, s, m * P:(m + 1) * P], k.u[:, m, :], start=m == 0, stop=m == KD - 1)
                else:
                    for j in range(NT):
                        for m in range(KD):
                            ins = nc.tensor.matmul(k.ps[3][:, j * P:(j + 1) * P], k.u[:, m, j * P:(j + 1) * P], k.w[:, s, m * P:(m + 1) * P],
                                                   start=m == 0, stop=m == KD - 1)
                ins.then_inc(proj_done, 1)

            def score(i, n):
                a, t = items[n]
                if n >= 2:
                    pe.wait_ge(logits_ready, NI * i + n - 1)
                r = slice(DH * a, DH * a + DH)
                nc.tensor.matmul(b_s[n % 2][:, 0:(t + 1) * P], q[r, t * P:(t + 1) * P], kk[r, 0:(t + 1) * P], start=True, stop=True).then_inc(st_done, 1)

            def core(i, nxt):
                if nxt:
                    project(i + 1, 0)
                pe.wait_ge(act_prep, 4 * i + 4)
                score(i, 0)
                score(i, 1)
                for n, (a, t) in enumerate(items):
                    pe.wait_ge(p_ready, NI * i + n + 1)
                    for j in range(t + 1):
                        ins = nc.tensor.transpose(b_t[:, j * P:(j + 1) * P], L[:, n % 2, j * P:(j + 1) * P], k.c("ident"))
                    ins.then_inc(turned, 1)
                    if n + 2 < NI:
                        score(i, n + 2)
                    if nxt and n in (1, 3, 5):
                        project(i + 1, 1 + n // 2)
                    pe.wait_ge(pt_ready, NI * i + n + 1)
                    for j in range(t + 1):
                        ins = nc.tensor.matmul(b_o[DH * a:DH * a + DH, t * P:(t + 1) * P], v[:, j * P + DH * a:j * P + DH * a + DH],
                                               PT[:, n % 2, j * P:(j + 1) * P], start=j == 0, stop=j == t)
                    ins.then_inc(pv_done, 1)

            for s in range(4):
                project(0, s, first=True)
            core(0, True)
            with pe.Fori(1, NP - 1) as i:
                core(i, True)
            core(NP - 1, False)

        @block.scalar
        def _(act):
            def step(i):
                for s, x in enumerate((q, kk, gate, v)):
                    act.wait_ge(proj_done, 4 * i + s + 1)
                    nc.scalar.activation(x[:, :], k.ps[s][:, :], ACT.Silu if s == 2 else ACT.Copy).then_inc(act_prep, 1)

                def turn(n):
                    t = items[n][1]
                    act.wait_ge(turned, NI * i + n + 1)
                    if n >= 2:
                        act.wait_ge(pv_done, NI * i + n - 1)
                    nc.scalar.activation(PT[:, n % 2, 0:(t + 1) * P], b_t[:, 0:(t + 1) * P], ACT.Copy).then_inc(pt_ready, 1)
                for n, (a, t) in enumerate(items):
                    act.wait_ge(max_ready, NI * i + n + 1)
                    l = L[:, n % 2, 0:(t + 1) * P]
                    nc.scalar.activation(l, l, ACT.Exp, bias=st[:, n, 0:1], accum_out=st[:, n, 1:2]).then_inc(exp_done, 1)
                    if n:
                        turn(n - 1)
                turn(NI - 1)
                act.wait_ge(y_ready, i + 1)

            with act.Fori(0, NP) as i:
                step(i)

        @block.gpsimd
        def _(pool):
            with pool.Fori(0, NP) as i:
                for n, (a, t) in enumerate(items):
                    pool.wait_ge(inv_ready, NI * i + n + 1)
                    l = L[:, n % 2, 0:(t + 1) * P]
                    nc.gpsimd.tensor_tensor(l, l, st[:, n, 2:3].to_broadcast([P, (t + 1) * P]), ALU.mult).then_inc(p_ready, 1)

        @block.vector
        def _(dve):
            ch = Chain(dve, ch_dve)

            def step(i):
                def inverse(n):
                    dve.wait_ge(exp_done, NI * i + n + 1)
                    nc.vector.reciprocal(st[:, n, 2:3], st[:, n, 1:2]).then_inc(inv_ready, 1)
                for n, (a, t) in enumerate(items):
                    w = (t + 1) * P
                    dve.wait_ge(st_done, NI * i + n + 1)
                    if n >= 2:
                        dve.wait_ge(turned, NI * i + n - 1)
                    l = L[:, n % 2, 0:w]
                    if fox:
                        b = k.fb[:, bass.ds(2 * i + a, 1), 0:w]
                        one = lambda x: x.rearrange("p (a t) -> p a t", a=1)
                        nc.vector.scalar_tensor_tensor(one(l), one(b_s[n % 2][:, 0:w]), DH ** -0.5, b, ALU.mult, ALU.add).then_inc(logits_ready, 1)
                        dve.wait_ge(logits_ready, NI * i + n + 1)
                        ch.link(nc.vector.tensor_tensor(l[:, w - P:w], l[:, w - P:w], k.c("causal"), ALU.add))
                    else:
                        nc.vector.scalar_tensor_tensor(l, b_s[n % 2][:, 0:w], DH ** -0.5, k.bias[:, OFF[t]:OFF[t + 1]], ALU.mult, ALU.add).then_inc(logits_ready, 1)
                        dve.wait_ge(logits_ready, NI * i + n + 1)
                    nc.vector.tensor_reduce(st[:, n, 0:1], l, AX, ALU.max, negate=True).then_inc(max_ready, 1)
                    if n:
                        inverse(n - 1)
                inverse(NI - 1)
                dve.wait_ge(pv_done, NI * i + NI)
                nc.vector.tensor_tensor(k.y[:, bass.ds(i + y0, 1), :], gate[:, :].rearrange("p (a t) -> p a t", a=1),
                                        b_o[:, :].rearrange("p (a t) -> p a t", a=1), ALU.mult).then_inc(y_ready, 1)
                dve.wait_ge(y_ready, i + 1)

            with dve.Fori(0, NP) as i:
                ch.loop(NI if fox else 0, i)
                step(i)
            ch.end(NP)


def program(nc, a):
    k = Core(nc, a)
    gains = lambda layer, i: lambda m: k.p("gains", (4 * layer + i) * KD + m)
    load_inputs(k)
    lower_bounds(k)
    norm_in(k, "in0", gains(0, 0))
    with ExitStack() as s:
        k.bc = s.enter_context(nc.sbuf_tensor("gate_bc", [P, 4, HA, T], F32))
        k.cols = s.enter_context(nc.sbuf_tensor("gate_cols", [P, 6, HA, NT], F32))
        ab_gates(k, a["ab_gate"])
        mlstm(k, a["m_in"])
        delta(k, a["g_in"])
    out_proj(k, "ab", k.y, KD, a["ab_out"], gains(0, 1), gains(0, 2))
    ffn(k, "0", 0, gains(1, 0))
    k.clear_semaphores()
    hgrn2(k, a["c_in"])
    out_proj(k, "c", k.y, KD, a["c_out"], gains(1, 1), gains(1, 2))
    ffn(k, "1", 1, lambda m: k.p("norm2", m))
    with ExitStack() as s:
        k.fb = s.enter_context(nc.sbuf_tensor("forget_bc", [P, HF, T], F32))
        k.bias = s.enter_context(nc.sbuf_tensor("choice_bias", [P, OFF[4]], F32))
        shared_inputs(k, a["shared_in"], a["pool_w"])
        attention(k, "fox", a["fox_in"], 5, True)
        attention(k, "dsa", a["dsa_in"], 2, False)
    out_proj(k, "two", k.y, KD, a["out2"], None, lambda m: k.p("final2", m))
    store_out(k, k.u)


def constants():
    i = np.arange(P)
    s, l = i[:, None], i[None, :]
    parts = {
        "ident": s == l,
        "ones": np.ones((P, P)),
        "upper": s <= l,
        "causal": np.where(l <= s, 0.0, -BIG),
        "chunkdiag": np.where(l < (s // 64 + 1) * 64, 0.0, -BIG),
        "levels": np.concatenate([(s // (2 * b) == l // (2 * b)) & (s // b % 2 == 0) & (l // b % 2 == 1) for b in LEVELS], 1),
        "sel": np.repeat(s == np.arange(6)[None, :], P, 1),
        "reset": np.broadcast_to((np.arange(T) % P != 0).astype(np.float32), (P, T)),
        "rcount": np.concatenate([1.0 / np.minimum(np.arange(T)[None, :] + 1, np.where(i < 64, a, b)[:, None]) for a, b in ((2, 4), (8, 16))], 1),
    }
    return np.concatenate([np.asarray(parts[n], np.float32) for n, _ in _CST], 1)


def columns(d):
    def fold(v):
        v = v.reshape(-1, P)
        return v.T

    def head_rows(v):
        out = np.zeros((P, v.shape[1]), np.float32)
        out[:v.shape[0]] = v
        return out
    f = np.concatenate([d["ffn_conv_w"], d["ffn_conv_b"][:, None, :]], 1)
    f = f.reshape(2, 4, 2, KF, P).transpose(4, 0, 3, 2, 1)
    m = d["ab_conv_m"][0].reshape(4, 2, 4, 64).transpose(1, 3, 2, 0).reshape(P, 16)
    g = d["ab_conv_g"][0].reshape(4, 3, 4, P).transpose(3, 2, 1, 0)
    parts = {
        "gains": fold(d["norm_gains"]), "norm2": fold(d["norm_g_2"]), "final2": fold(d["final_g_2"]),
        "ffn": f.reshape(P, -1), "mconv": m, "gconv": g.reshape(P, -1),
        "mnorm": fold(d["ab_m_norm"]), "gnorm": fold(d["ab_g_norm"]), "cnorm": fold(d["c_norm"]),
        "lb": fold(d["c_lb_logits"]), "pscale": fold(d["pool_scale_2"]),
        "gbias": head_rows(d["ab_m_gate_bias"][0].T),
        "adt": head_rows(np.stack([d["ab_g_a_log"][0], d["ab_g_dt_bias"][0]], 1)),
        "foxb": head_rows(d["fox_bf_2"][0][:, None]),
    }
    return np.concatenate([parts[n] for n, _ in _COLS], 1)


def tiles(w):
    return w.reshape(KD, P, -1, P).transpose(2, 1, 0, 3).reshape(-1, P, D)


def layout_ffn(d):
    up = np.stack([tiles(w.reshape(D, 2, KF, P).transpose(0, 2, 1, 3).reshape(D, 2 * FF)) for w in d["ffn_w_up"]])
    return {"x": d["x"][0].T, "cst": constants(), "col": columns(d), "ffn_up": up, "ffn_down": d["ffn_w_down"]}


def layout_c(d):
    w = d["c_w_in"][0].reshape(D, 4, HC, P)[:, [0, 1, 3, 2]].transpose(0, 2, 1, 3).reshape(D, 4 * HC * P)
    return {"c_in": tiles(w), "c_out": d["c_w_out"][0]}


def layout_ab(d):
    w = d["ab_w_in"][0]
    cut = lambda lo, n: w[:, lo:lo + n]
    gate = np.zeros((D, P), np.float32)
    for i, lo in enumerate((1536, 1540, 3592, 3596)):
        gate[:, 32 * i:32 * i + 4] = cut(lo, 4)
    m = []
    for h in range(4):
        m += [cut(64 * h, 64), cut(256 + 64 * h, 64), cut(1024 + P * h, P), cut(512 + P * h, P)]
    g = []
    for h in range(4):
        g += [cut(1544 + 512 * i + P * h, P) for i in (0, 1, 2, 3)]
    return {"ab_gate": tiles(gate), "m_in": tiles(np.concatenate(m, 1)), "g_in": tiles(np.concatenate(g, 1)), "ab_out": d["ab_w_out"][0]}


def layout_2(d):
    w = d["w_in_2"][0]
    names = ("pv", 256), ("pg", 256), ("dq", 384), ("dk", 384), ("dv", 384), ("dg", 384), ("iq", 256), ("ik", 32), ("iw", 8), ("fq", 384), ("fk", 384), ("fv", 384), ("fg", 384), ("ff", 6)
    part, at = {}, 0
    for n, m in names:
        part[n] = w[:, at:at + m]
        at += m
    gate = np.zeros((D, P), np.float32)
    gate[:, 0:6], gate[:, 32:40] = part["ff"], part["iw"]
    shared = tiles(np.concatenate([gate] + [part["ik"]] * 4 + [part["iq"], part["pv"], part["pg"]], 1))
    pairs = lambda names: tiles(np.concatenate([part[n][:, P * i:P * i + P] for i in range(3) for n in names], 1))
    pw = np.zeros((P, 2, P), np.float32)
    for g in range(4):
        o = 64 * (g % 2)
        pw[o:o + 64, g // 2, o:o + 64] = d["pool_w_2"][0, g]
    return {"shared_in": shared, "pool_w": pw, "dsa_in": pairs(("dq", "dk", "dg", "dv")), "fox_in": pairs(("fq", "fk", "fg", "fv")), "out2": d["w_out_2"][0]}


def layout(d):
    return {**layout_ffn(d), **layout_ab(d), **layout_c(d), **layout_2(d)}


def kernel(**inputs):
    import concourse.bacc as _bacc
    from concourse.bass_utils import run_bass_kernel_spmd as _run

    d = {n: np.asarray(v) for n, v in inputs.items()}
    arrays = {n: np.ascontiguousarray(v) for n, v in layout(d).items()}
    nc = _bacc.Bacc("TRN2", target_bir_lowering=False, num_devices=1)
    aps = {n: nc.dram_tensor(n, v.shape, mybir.dt.from_np(v.dtype), kind="ExternalInput").ap() for n, v in arrays.items()}
    aps["out"] = nc.dram_tensor("out", (D, T), F32, kind="ExternalOutput").ap()
    program(nc, aps)
    r = _run(nc, [arrays], core_ids=[0])
    return r.results[0]["out"].T[None]
```

```python
from contextlib import ExitStack

import numpy as np
import concourse.bass as bass
from concourse import mybir
from concourse.alu_op_type import AluOpType as ALU

F32 = mybir.dt.float32
F32R = mybir.dt.float32r
U32 = mybir.dt.uint32
ACT = mybir.ActivationFunctionType
AX = mybir.AxisListType.X

P = 128
T = 512
NT = T // P
D = 1024
KD = D // P
FF = 2816
KF = FF // P
EPS = 1e-6
BIG = 1e30

LEVELS = [1 << n for n in range(7)]
_CST = [("ident", P), ("ones", P), ("upper", P), ("causal", P), ("chunkdiag", P), ("levels", P * len(LEVELS)),
        ("reset", T), ("rcount", 2 * T), ("sel", 6 * P)]
CST = {}
_at = 0
for _n, _w in _CST:
    CST[_n] = (_at, _w)
    _at += _w
NCST = _at

_COLS = [("gains", 8 * KD), ("norm2", KD), ("final2", KD), ("ffn", 2 * 2 * KF * 4), ("mconv", 4 * 4), ("gconv", 4 * 3 * 4),
         ("mnorm", 4), ("gnorm", 4), ("cnorm", 8), ("lb", 2 * 8), ("pscale", 2), ("gbias", 2), ("adt", 2), ("foxb", 1)]
COL = {}
_at = 0
for _n, _w in _COLS:
    COL[_n] = (_at, _w)
    _at += _w
NCOL = _at


class Chain:

    def __init__(self, eng, sem):
        self.eng, self.sem, self.base, self.n = eng, sem, 0, 0

    def link(self, ins):
        self.n += 1
        ins.then_inc(self.sem, 1)
        self.eng.wait_ge(self.sem, self.base + self.n)

    def loop(self, per_step, i):
        self.base, self.enter, self.n = self.base + self.n + i * per_step, (self.base + self.n, per_step), 0

    def end(self, steps):
        before, per_step = self.enter
        assert self.n == per_step, (self.n, per_step)
        self.base, self.n = before + per_step * steps, 0


def phase(f):
    def run(k, *args):
        with ExitStack() as k.stack:
            f(k, *args)
    return run


class Core:

    def __init__(self, nc, a):
        self.nc, self.a, self.sems = nc, a, []
        sb = nc.alloc_sbuf_tensor
        self.x = sb("x_res", [P, KD, T], F32)
        self.uh = sb("u_high", [P, KD, T], F32R)
        self.ul = sb("u_low", [P, KD, T], F32R)
        self.ws = [(sb(f"w{s}_high", [P, D], F32R), sb(f"w{s}_low", [P, D], F32R)) for s in range(2)]
        self.y = sb("y_mix", [P, KD, T], F32)
        self.w = sb("w_ring", [P, 4, D], F32)
        self.sq = sb("sq", [P, 2, T], F32)
        self.rstd = sb("rstd", [P, T], F32)
        self.cst = sb("cst_sb", [P, NCST], F32)
        self.col = sb("col_sb", [P, NCOL], F32)
        self.epsc = sb("eps_col", [P, 1], F32)
        self.lb = sb("lb_cols", [P, 2, KD], F32)
        self.w_loaded = [nc.alloc_semaphore(f"w_loaded{s}") for s in range(4)]
        self.loads = [0] * 4
        self.ahead = 0
        self.ps = [nc.alloc_psum_tensor(f"bank{i}", [P, T], F32) for i in range(8)]

    def sb(self, name, shape, dtype=F32):
        return self.stack.enter_context(self.nc.sbuf_tensor(name, shape, dtype))

    def sem(self, name):
        self.sems.append(self.nc.alloc_semaphore(name))
        return self.sems[-1]

    def load(self, sp, s, tile):
        sp.dma_start(self.w[:, s, :], tile).then_inc(self.w_loaded[s], 16)

    def load_ahead(self, sp, tiles):
        for s, tile in enumerate(tiles):
            self.load(sp, s, tile)
        self.ahead = len(tiles)

    def first_loads(self, sp, tiles):
        for s in range(self.ahead, len(tiles)):
            self.load(sp, s, tiles[s])
        self.ahead = 0

    def loaded(self, s, i):
        return 16 * (self.loads[s] + i) + 16

    def split_high(self, act, s, i, j, w_high):
        act.wait_ge(self.w_loaded[s], self.loaded(s, i))
        self.nc.scalar.activation(self.ws[j][0][:, :], self.w[:, s, :], ACT.Copy).then_inc(w_high, 1)

    def split_low(self, eng, s, n, j, w_high, w_split):
        high, low = self.ws[j]
        eng.wait_ge(w_high, n + 1)
        eng.tensor_tensor(low[:, :], self.w[:, s, :], high[:, :].bitcast(F32), ALU.subtract).then_inc(w_split, 1)

    def product(self, out, a, b, start=True, stop=True):
        nc = self.nc
        nc.tensor.matmul(out, a[0], b[0], start=start, stop=False)
        nc.tensor.matmul(out, a[0], b[1], start=False, stop=False)
        return nc.tensor.matmul(out, a[1], b[0], start=False, stop=stop)

    def by_feature(self, out, j):
        for m in range(KD):
            s = slice(m * P, (m + 1) * P)
            ins = self.product(out, [x[:, s] for x in self.ws[j]], [x[:, m, :] for x in (self.uh, self.ul)], m == 0, m == KD - 1)
        return ins

    def by_token(self, out, j, first=0, last=NT):
        for c in range(first, last):
            for m in range(KD):
                ins = self.product(out[:, c * P:(c + 1) * P], [x[:, m, c * P:(c + 1) * P] for x in (self.uh, self.ul)],
                                   [x[:, m * P:(m + 1) * P] for x in self.ws[j]], m == 0, m == KD - 1)
        return ins

    def clear_semaphores(self):
        self.nc.clear_and_free_semaphores(self.sems)
        self.nc.all_engine_barrier()
        self.sems = []

    def c(self, name, lo=0, hi=None):
        at, w = CST[name]
        return self.cst[:, at + lo:at + (w if hi is None else hi)]

    def p(self, name, i, n=1):
        at, _ = COL[name]
        return self.col[:, bass.ds(at + i, n)]


@phase
def load_inputs(k, ahead):
    nc, a = k.nc, k.a
    loaded, eps_set = k.sem("inputs_loaded"), k.sem("eps_set")
    with nc.Block() as block:
        @block.sync
        def _(sp):
            sp.dma_start(k.x[:, :, :], a["x"].rearrange("(k p) t -> p k t", p=P)).then_inc(loaded, 16)
            sp.dma_start(k.cst[:, :], a["cst"]).then_inc(loaded, 16)
            sp.dma_start(k.col[:, :], a["col"]).then_inc(loaded, 16)
            sp.dma_start(k.w[:, 3, :], ahead).then_inc(k.w_loaded[3], 16)
            sp.wait_ge(loaded, 48)

        @block.vector
        def _(dve):
            nc.vector.memset(k.epsc[:, :], EPS).then_inc(eps_set, 1)
            dve.wait_ge(eps_set, 1)


def u_parts(k, gain, rooted, normed, high, ch, tmp):
    nc = k.nc

    def vector(dve):
        dve.wait_ge(rooted, 1)
        ch.link(nc.vector.reciprocal(k.rstd[:, :], k.rstd[:, :]))

        def low(m):
            dve.wait_ge(high, m + 1)
            return nc.vector.tensor_tensor(k.ul[:, m, :], tmp[:, m, :], k.uh[:, m, :].bitcast(F32), ALU.subtract)
        for m in range(KD):
            nc.vector.scalar_tensor_tensor(tmp[:, m, :], k.x[:, m, :], gain(m), k.rstd[:, :], ALU.mult, ALU.mult).then_inc(normed, 1)
            if m >= 2 and m % 2 == 0:
                low(m - 2)
        low(KD - 2)

    def scalar(act):
        for m in range(KD):
            act.wait_ge(normed, m + 1)
            nc.scalar.activation(k.uh[:, m, :], tmp[:, m, :], ACT.Copy).then_inc(high, 1)

    def gpsimd(pool):
        for m in range(1, KD, 2):
            pool.wait_ge(high, m + 1)
            nc.gpsimd.tensor_tensor(k.ul[:, m, :], tmp[:, m, :], k.uh[:, m, :].bitcast(F32), ALU.subtract)
    return vector, scalar, gpsimd


@phase
def norm_in(k, tag, gain):
    nc = k.nc
    squared, summed, rooted, chained, normed, high = (k.sem(f"{s}_{tag}") for s in
                                                      ("squared", "summed", "rooted", "chained", "normed", "high"))
    tmp = k.sb(f"normed_{tag}", [P, KD, T])
    ch = Chain(None, chained)
    on_vector, on_scalar, on_gpsimd = u_parts(k, gain, rooted, normed, high, ch, tmp)
    with nc.Block() as block:
        @block.scalar
        def _(act):
            for m in range(KD):
                if m >= 2:
                    act.wait_ge(summed, m - 1)
                nc.scalar.activation(k.sq[:, m % 2, :], k.x[:, m, :], ACT.Square).then_inc(squared, 1)
            act.wait_ge(summed, KD)
            nc.scalar.activation(k.rstd[:, :], k.ps[0][:, :], ACT.Sqrt, bias=k.epsc[:, 0:1], scale=1.0 / D).then_inc(rooted, 1)
            on_scalar(act)

        @block.tensor
        def _(pe):
            for m in range(KD):
                pe.wait_ge(squared, m + 1)
                nc.tensor.matmul(k.ps[0][:, :], k.c("ones"), k.sq[:, m % 2, :], start=m == 0, stop=m == KD - 1).then_inc(summed, 1)

        @block.vector
        def _(dve):
            ch.eng = dve
            on_vector(dve)

        @block.gpsimd
        def _(pool):
            on_gpsimd(pool)


@phase
def out_proj(k, tag, src, tiles, weights, gain_post, gain_next, ahead):
    nc = k.nc
    final = not ahead
    names = ("w_high", "w_split", "src_high", "src_split", "tile_done", "mixed", "moved", "squared", "summed", "rooted", "added", "squared2",
             "summed2", "rooted2", "chained", "normed", "high", "stored")
    w_high, w_split, src_high, src_split, tile_done, mixed, moved, squared, summed, rooted, added, squared2, summed2, rooted2, chained, normed, high, stored = (
        k.sem(f"{s}_{tag}") for s in names)
    pairs = tiles // 2
    mx = k.sb(f"mixed_sb_{tag}", [P, KD, T])
    sp2 = [(k.sb(f"src{s}_high_{tag}", [P, T], F32R), k.sb(f"src{s}_low_{tag}", [P, T], F32R)) for s in range(2)]
    ch = Chain(None, chained)
    on_vector, on_scalar, on_gpsimd = u_parts(k, gain_next, rooted2, normed, high, ch, mx)

    def tile(n):
        return src[:, bass.ds(n, 1), :].rearrange("p a t -> p (a t)")

    with nc.Block() as block:
        @block.sync
        def _(sp):
            k.first_loads(sp, [weights[s * P:(s + 1) * P, :] for s in range(2)])
            with sp.Fori(1, pairs) as i:
                for s in range(2):
                    sp.wait_ge(w_split, 2 * i - 1 + s)
                    k.load(sp, s, weights[bass.ds((2 * i + s) * P, P), :])
            if ahead:
                sp.wait_ge(w_split, tiles)
                k.load_ahead(sp, ahead)
            else:
                for m in range(KD):
                    sp.wait_ge(normed, m + 1)
                    sp.dma_start(k.a["out"][m * P:(m + 1) * P, :], mx[:, m, :]).then_inc(stored, 16)
                sp.wait_ge(stored, 16 * KD)

        @block.tensor
        def _(pe):
            def step(i, s, start, stop):
                pe.wait_ge(w_split, 2 * i + s + 1)
                pe.wait_ge(src_split, 2 * i + s + 1)
                for m in range(KD):
                    ins = k.product(k.ps[m][:, :], [x[:, m * P:(m + 1) * P] for x in k.ws[s]], [x[:, :] for x in sp2[s]], start, stop)
                    if stop:
                        ins.then_inc(mixed, 1)
                if not stop:
                    ins.then_inc(tile_done, 1)
            step(0, 0, True, False)
            step(0, 1, False, False)
            with pe.Fori(1, pairs - 1) as i:
                step(i, 0, False, False)
                step(i, 1, False, False)
            step(pairs - 1, 0, False, False)
            step(pairs - 1, 1, False, True)
            if gain_post:
                pe.wait_ge(moved, 1)
                for m in range(KD):
                    pe.wait_ge(squared, m + 1)
                    nc.tensor.matmul(k.ps[0][:, :], k.c("ones"), k.sq[:, m % 2, :], start=m == 0, stop=m == KD - 1).then_inc(summed, 1)
            for m in range(KD):
                if m == 0:
                    pe.wait_ge(moved if gain_post else added, 2)
                pe.wait_ge(squared2, m + 1)
                nc.tensor.matmul(k.ps[1][:, :], k.c("ones"), k.sq[:, m % 2, :], start=m == 0, stop=m == KD - 1).then_inc(summed2, 1)

        @block.scalar
        def _(act):
            def step(i, s, first):
                if not first:
                    act.wait_ge(tile_done, 2 * i + s - 1)
                act.wait_ge(k.w_loaded[s], k.loaded(s, i))
                nc.scalar.activation(k.ws[s][0][:, :], k.w[:, s, :], ACT.Copy).then_inc(w_high, 1)
                nc.scalar.activation(sp2[s][0][:, :], tile(2 * i + s), ACT.Copy).then_inc(src_high, 1)
            step(0, 0, True)
            step(0, 1, True)
            with act.Fori(1, pairs) as i:
                step(i, 0, False)
                step(i, 1, False)
            if gain_post:
                for m in range(KD):
                    act.wait_ge(moved, m + 1)
                    if m >= 2:
                        act.wait_ge(summed, m - 1)
                    nc.scalar.activation(k.sq[:, m % 2, :], mx[:, m, :], ACT.Square).then_inc(squared, 1)
                act.wait_ge(summed, KD)
                nc.scalar.activation(k.rstd[:, :], k.ps[0][:, :], ACT.Sqrt, bias=k.epsc[:, 0:1], scale=1.0 / D).then_inc(rooted, 1)
            for m in range(KD):
                act.wait_ge(added, m + 1)
                if m >= 2:
                    act.wait_ge(summed2, m - 1)
                nc.scalar.activation(k.sq[:, m % 2, :], k.x[:, m, :], ACT.Square).then_inc(squared2, 1)
            act.wait_ge(summed2, KD)
            nc.scalar.activation(k.rstd[:, :], k.ps[1][:, :], ACT.Sqrt, bias=k.epsc[:, 0:1], scale=1.0 / D).then_inc(rooted2, 1)
            if not final:
                on_scalar(act)

        @block.vector
        def _(dve):
            ch.eng = dve

            def step(n, s):
                dve.wait_ge(w_high, n + 1)
                nc.vector.tensor_tensor(k.ws[s][1][:, :], k.w[:, s, :], k.ws[s][0][:, :].bitcast(F32), ALU.subtract).then_inc(w_split, 1)
                dve.wait_ge(src_high, n + 1)
                high_, low = sp2[s]
                one = lambda x: x.rearrange("p (a t) -> p a t", a=1)
                nc.vector.tensor_tensor(one(low[:, :]), src[:, bass.ds(n, 1), :], one(high_[:, :]).bitcast(F32), ALU.subtract).then_inc(src_split, 1)
            with dve.Fori(0, pairs) as i:
                step(2 * i, 0)
                step(2 * i + 1, 1)
            if gain_post:
                for m in range(KD):
                    dve.wait_ge(mixed, m + 1)
                    nc.vector.tensor_copy(mx[:, m, :], k.ps[m][:, :]).then_inc(moved, 1)
                dve.wait_ge(moved, KD)
                dve.wait_ge(rooted, 1)
                ch.link(nc.vector.reciprocal(k.rstd[:, :], k.rstd[:, :]))
                for m in range(KD):
                    ins = nc.vector.scalar_tensor_tensor(mx[:, m, :], mx[:, m, :], gain_post(m), k.rstd[:, :], ALU.mult, ALU.mult)
                ch.link(ins)
                for m in range(KD):
                    nc.vector.tensor_tensor(k.x[:, m, :], k.x[:, m, :], mx[:, m, :], ALU.add).then_inc(added, 1)
            else:
                for m in range(KD):
                    dve.wait_ge(mixed, m + 1)
                    nc.vector.tensor_tensor(k.x[:, m, :], k.x[:, m, :], k.ps[m][:, :], ALU.add).then_inc(added, 1)
                dve.wait_ge(added, KD)
            if final:
                dve.wait_ge(rooted2, 1)
                ch.link(nc.vector.reciprocal(k.rstd[:, :], k.rstd[:, :]))
                for m in range(KD):
                    nc.vector.scalar_tensor_tensor(mx[:, m, :], k.x[:, m, :], gain_next(m), k.rstd[:, :], ALU.mult, ALU.mult).then_inc(normed, 1)
            else:
                on_vector(dve)

        if not final:
            @block.gpsimd
            def _(pool):
                on_gpsimd(pool)
    for s in range(2):
        k.loads[s] += pairs


@phase
def ffn_up(k, tag, layer, weights, h, ahead):
    nc, sem = k.nc, k.sem
    w_high, w_split, up_done, tap_done, conv_done, silu_done, mul_done, chained = (sem(f"{s}_{tag}") for s in (
        "w_high", "w_split", "up_done", "tap_done", "conv_done", "silu_done", "mul_done", "chained"))
    cg = k.sb(f"conv_{tag}", [P, 4, T])
    n = KF // 2

    def coef(tile, j):
        return k.p("ffn", (layer * 2 * KF + tile) * 4 + j)

    with nc.Block() as block:
        @block.sync
        def _(sp):
            k.first_loads(sp, [weights[s, :, :] for s in range(4)])
            with sp.Fori(1, n) as i:
                for s in range(4):
                    sp.wait_ge(w_split, 4 * i - 3 + s)
                    k.load(sp, s, weights[bass.ds(4 * i + s, 1), :, :].rearrange("a p d -> p (a d)"))
            sp.wait_ge(w_split, 4 * n)
            k.load_ahead(sp, ahead)

        @block.tensor
        def _(pe):
            def step(i, first):
                for s in range(4):
                    pe.wait_ge(w_split, 4 * i + s + 1)
                    if not first:
                        pe.wait_ge(conv_done, 4 * i - 3 + s)
                    k.by_feature(k.ps[s][:, :], s % 2).then_inc(up_done, 1)
            step(0, True)
            with pe.Fori(1, n) as i:
                step(i, False)

        @block.scalar
        def _(act):
            def high(i, s, first=False):
                act.wait_ge(k.w_loaded[s], k.loaded(s, i))
                if not first:
                    act.wait_ge(up_done, 4 * i + s - 1)
                nc.scalar.activation(k.ws[s % 2][0][:, :], k.w[:, s, :], ACT.Copy).then_inc(w_high, 1)

            def step(i, first, last):
                for s in range(4):
                    if s < 3:
                        high(i, s + 1, first=first and s == 0)
                    elif not last:
                        high(i + 1, 0)
                    act.wait_ge(up_done, 4 * i + s + 1)
                    if not first:
                        act.wait_ge(mul_done, 2 * i - 1 + s // 2)
                    nc.scalar.activation(cg[:, s, :], k.ps[s][:, :], ACT.Identity, bias=coef(4 * i + s, 3), scale=coef(4 * i + s, 2)).then_inc(tap_done, 1)
                    if s % 2:
                        act.wait_ge(conv_done, 4 * i + s)
                        nc.scalar.activation(cg[:, s - 1, :], cg[:, s - 1, :], ACT.Silu).then_inc(silu_done, 1)
            high(0, 0, first=True)
            step(0, True, False)
            with act.Fori(1, n - 1) as i:
                step(i, False, False)
            step(n - 1, False, True)

        @block.vector
        def _(dve):
            ch = Chain(dve, chained)

            def low(n, s):
                dve.wait_ge(w_high, n + 1)
                nc.vector.tensor_tensor(k.ws[s % 2][1][:, :], k.w[:, s, :], k.ws[s % 2][0][:, :].bitcast(F32), ALU.subtract).then_inc(w_split, 1)

            def step(i, last):
                for s in range(4):
                    if not (last and s == 3):
                        low(4 * i + s + 1, (s + 1) % 4)
                    dve.wait_ge(tap_done, 4 * i + s + 1)
                    ch.link(nc.vector.scalar_tensor_tensor(cg[:, s, 1:T], k.ps[s][:, 0:T - 1], coef(4 * i + s, 1), cg[:, s, 1:T], ALU.mult, ALU.add))
                    nc.vector.scalar_tensor_tensor(cg[:, s, 2:T], k.ps[s][:, 0:T - 2], coef(4 * i + s, 0), cg[:, s, 2:T], ALU.mult, ALU.add).then_inc(conv_done, 1)

            low(0, 0)
            with dve.Fori(0, n - 1) as i:
                ch.loop(4, i)
                step(i, False)
            ch.end(n - 1)
            step(n - 1, True)

        @block.gpsimd
        def _(pool):
            with pool.Fori(0, n) as i:
                for s in (1, 3):
                    pool.wait_ge(conv_done, 4 * i + s + 1)
                    pool.wait_ge(silu_done, 2 * i + (s + 1) // 2)
                    nc.gpsimd.tensor_tensor(h[:, bass.ds(2 * i + s // 2, 1), :], cg[:, s - 1:s, :], cg[:, s:s + 1, :], ALU.mult).then_inc(mul_done, 1)
    for s in range(4):
        k.loads[s] += n


def ffn(k, tag, layer, gain_next, ahead):
    down = k.a["ffn_down"][layer]
    with k.nc.sbuf_tensor(f"hidden{tag}", [P, KF, T], F32) as hidden:
        ffn_up(k, f"up{tag}", layer, k.a["ffn_up"][layer], hidden, [down[s * P:(s + 1) * P, :] for s in range(2)])
        out_proj(k, f"down{tag}", hidden, KF, down, lambda m: k.p("gains", (4 * layer + 3) * KD + m), gain_next, ahead)


LNEXP = "natural_log_exp_and_others"
HC = 8


@phase
def lower_bounds(k):
    nc = k.nc
    t = k.sb("lb_tmp", [P, 5, HC], F32)
    maxed, powered, bounded = (k.sem(s) for s in ("lb_maxed", "lb_powered", "lb_bounded"))
    l0, l1 = k.p("lb", 0, HC), k.p("lb", HC, HC)
    with nc.Block() as block:
        @block.vector
        def _(dve):
            ch = Chain(dve, maxed)
            ch.link(nc.vector.tensor_tensor(t[:, 0, :], l0, l1, ALU.max))
            nc.vector.tensor_tensor(t[:, 1, :], l0, t[:, 0, :], ALU.subtract)
            ch.link(nc.vector.tensor_tensor(t[:, 2, :], l1, t[:, 0, :], ALU.subtract))
            dve.wait_ge(powered, 1)
            ch2 = Chain(dve, bounded)
            ch2.link(nc.vector.tensor_tensor(t[:, 0, :], t[:, 1, :], t[:, 2, :], ALU.add))
            ch2.link(nc.vector.reciprocal(t[:, 3, :], t[:, 0, :]))
            ch2.link(nc.vector.tensor_tensor(t[:, 1:3, :], t[:, 1:3, :], t[:, 3:4, :].to_broadcast([P, 2, HC]), ALU.mult))
            ch2.link(nc.vector.tensor_tensor(t[:, 4, :], t[:, 1, :], t[:, 2, :], ALU.add))
            ch2.link(nc.vector.tensor_tensor(k.lb[:, 0, :], t[:, 4, :], t[:, 1, :], ALU.subtract))
            ch2.link(nc.vector.tensor_scalar(k.lb[:, 1, :], k.lb[:, 0, :], -1.0, 1.0, ALU.mult, ALU.add))

        @block.scalar
        def _(act):
            act.wait_ge(maxed, 2)
            nc.scalar.activation(t[:, 1:3, :], t[:, 1:3, :], ACT.Exp).then_inc(powered, 1)


@phase
def hgrn2(k, weights, ahead):
    nc = k.nc
    sem = k.sem
    sb = k.sb
    H = HC
    scale = P ** -0.5
    q, kk, v, gate = (sb(f"c_{s}", [P, T], F32) for s in ("q", "k", "v", "gate"))
    fbuf, ef, sig, logf, G, E, kdf, qd, kd, kdt, at, osb = (
        sb(f"c_{s}", [P, T], F32) for s in ("f", "ef", "sig", "logf", "G", "E", "kdf", "qd", "kd", "kdt", "attn", "o"))
    dif = sb("c_dif", [P, 4, T], F32)
    tick = sb("c_tick", [P, 4], F32)
    X = sb("c_X", [P, 4, T], F32)
    S = sb("c_S", [P, NT - 1, P], F32)
    b_q, b_f, b_g, b_v, b_x0, b_x1, b_kv, b_o = k.ps
    b_x = [b_x0, b_x1]
    w_high, w_split = sem("c_w_high"), sem("c_w_split")
    k.ws += [(sb(f"c_w{s}_high", [P, D], F32R), sb(f"c_w{s}_low", [P, D], F32R)) for s in (2, 3)]
    R = 4
    (proj_done, f_clamped, act_prep, sig_ready, ft_ready, logf_ready, g_ready, e_ready, kd_ready, tr_done, kdt_ready, kv_done,
     s_ready, diff_ready, lexp_ready, x_ready, lv_done, at_done, o_done, osb_ready, osq_ready, nrm_done, rs_ready, y_ready,
     ch_act, ch_dve) = (sem("c_" + s) for s in (
         "proj_done f_clamped act_prep sig_ready ft_ready logf_ready g_ready e_ready kd_ready tr_done kdt_ready kv_done "
         "s_ready diff_ready lexp_ready x_ready lv_done at_done o_done osb_ready osq_ready nrm_done rs_ready y_ready "
         "ch_act ch_dve").split())
    NL = len(LEVELS)

    def chunks(x):
        return x[:, :].rearrange("p (c l) -> p c l", l=P)

    def mask(name, lo):
        return k.c(name, lo, lo + P).rearrange("p (a l) -> p a l", a=1).to_broadcast([P, NT, P])

    def blocks(x, b):
        return x.rearrange("p (n e b) -> p n e b", e=2, b=b)

    with nc.Block() as block:
        @block.sync
        def _(sp):
            k.first_loads(sp, [weights[s, :, :] for s in range(4)])
            with sp.Fori(1, H) as h:
                for s in range(4):
                    sp.wait_ge(w_split, 4 * h - 3 + s)
                    k.load(sp, s, weights[bass.ds(4 * h + s, 1), :, :].rearrange("a p d -> p (a d)"))
            sp.wait_ge(w_split, 4 * H)
            k.load_ahead(sp, ahead)

        @block.tensor
        def _(pe):
            def project(h, s, first=False, between=None):
                pe.wait_ge(w_split, 4 * h + s + 1)
                if not first:
                    if s == 1:
                        pe.wait_ge(sig_ready, h)
                    else:
                        pe.wait_ge(act_prep, 3 * h - (2 if s == 0 else 1 if s == 2 else 0))
                if s < 3:
                    k.by_feature(k.ps[s][:, :], s).then_inc(proj_done, 1)
                else:
                    k.by_token(b_v, s, 0, NT // 2)
                    if between:
                        between()
                    k.by_token(b_v, s, NT // 2, NT).then_inc(proj_done, 1)

            def level(h, l):
                pe.wait_ge(x_ready, NL * h + l + 1)
                if l >= 1:
                    pe.wait_ge(at_done, 8 * h + l)
                for c in range(NT):
                    xc = X[:, l % R, c * P:(c + 1) * P]
                    ins = nc.tensor.matmul(b_x[(l + 1) % 2][:, c * P:(c + 1) * P], xc, xc, start=True, stop=True)
                ins.then_inc(lv_done, 1)

            def core(h, nxt, first):
                if nxt:
                    project(h + 1, 0)
                    project(h + 1, 1)
                pe.wait_ge(sig_ready, h + 1)
                pe.wait_ge(g_ready, h + 1)
                if not first:
                    pe.wait_ge(rs_ready, h)
                for c in range(NT):
                    ins = nc.tensor.matmul(b_x0[:, c * P:(c + 1) * P], kk[:, c * P:(c + 1) * P], q[:, c * P:(c + 1) * P], start=True, stop=True)
                ins.then_inc(lv_done, 1)
                for l in range(4):
                    level(h, l)
                if nxt:
                    project(h + 1, 2)
                for l in range(4, NL):
                    level(h, l)
                pe.wait_ge(kd_ready, h + 1)
                for c in range(NT - 1):
                    ins = nc.tensor.transpose(b_kv[:, c * P:(c + 1) * P], kd[:, c * P:(c + 1) * P], k.c("ident"))
                ins.then_inc(tr_done, 1)
                pe.wait_ge(kdt_ready, h + 1)
                pe.wait_ge(act_prep, 3 * h + 3)
                for c in range(NT - 1):
                    ins = nc.tensor.matmul(b_kv[:, c * P:(c + 1) * P], kdt[:, c * P:(c + 1) * P], v[:, c * P:(c + 1) * P], start=True, stop=True)
                ins.then_inc(kv_done, 1)
                pe.wait_ge(at_done, 8 * h + 8)
                for c in range(NT):
                    s = slice(c * P, (c + 1) * P)
                    ins = nc.tensor.matmul(b_o[:, s], v[:, s], at[:, s], start=True, stop=c == 0)
                    if c:
                        if c == 1:
                            pe.wait_ge(s_ready, h + 1)
                        ins = nc.tensor.matmul(b_o[:, s], S[:, c - 1, :], qd[:, s], start=False, stop=True)
                ins.then_inc(o_done, 1)

                def norm():
                    pe.wait_ge(osq_ready, h + 1)
                    nc.tensor.matmul(b_x0[:, :], k.c("ones"), k.sq[:, 0, :], start=True, stop=True).then_inc(nrm_done, 1)
                if nxt:
                    project(h + 1, 3, between=norm)
                else:
                    norm()

            for s in range(4):
                project(0, s, first=True)
            core(0, True, True)
            with pe.Fori(1, H - 1) as h:
                core(h, True, False)
            core(H - 1, False, False)

        @block.scalar
        def _(act):
            ch = Chain(act, ch_act)

            def high(h, s):
                act.wait_ge(proj_done, 4 * h + s - 3)
                k.split_high(act, s, h, s, w_high)

            def step(h, nxt, nxt2):
                act.wait_ge(proj_done, 4 * h + 1)
                nc.scalar.activation(q[:, :], b_q[:, :], ACT.Silu).then_inc(act_prep, 1)
                act.wait_ge(proj_done, 4 * h + 3)
                nc.scalar.activation(gate[:, :], b_g[:, :], ACT.Silu).then_inc(act_prep, 1)
                act.wait_ge(proj_done, 4 * h + 4)
                nc.scalar.activation(v[:, :], b_v[:, :], ACT.Copy).then_inc(act_prep, 1)
                nc.scalar.preload_act_table_set(LNEXP)
                act.wait_ge(f_clamped, h + 1)
                ch.link(nc.scalar.activation(ef[:, :], fbuf[:, :], ACT.Exp, scale=-1.0))
                ch.link(nc.scalar.activation(sig[:, :], ef[:, :], ACT.Ln, bias=1.0))
                nc.scalar.activation(sig[:, :], sig[:, :], ACT.Exp, scale=-1.0).then_inc(sig_ready, 1)
                if nxt:
                    high(h + 1, 1)
                act.wait_ge(ft_ready, h + 1)
                nc.scalar.activation(logf[:, :], fbuf[:, :], ACT.Ln).then_inc(logf_ready, 1)
                act.wait_ge(g_ready, h + 1)
                nc.scalar.activation(E[:, :], G[:, :], ACT.Exp)
                nc.scalar.activation(kdf[:, :], kdf[:, :], ACT.Exp, scale=-1.0).then_inc(e_ready, 1)
                for l, b in enumerate(LEVELS):
                    act.wait_ge(diff_ready, NL * h + l + 1)
                    d = blocks(dif[:, l % R, :], b)
                    nc.scalar.activation(d[:, :, 0, :], d[:, :, 0, :], ACT.Exp, scale=-1.0)
                    nc.scalar.activation(d[:, :, 1, :], d[:, :, 1, :], ACT.Exp).then_inc(lexp_ready, 1)
                    if nxt and l in (0, 4):
                        high(h + 1, 2 + l // 4)
                act.wait_ge(tr_done, h + 1)
                nc.scalar.activation(kdt[:, 0:T - P], b_kv[:, 0:T - P], ACT.Copy).then_inc(kdt_ready, 1)
                act.wait_ge(o_done, h + 1)
                nc.scalar.activation(osb[:, :], b_o[:, :], ACT.Copy, scale=scale).then_inc(osb_ready, 1)
                act.wait_ge(osb_ready, h + 1)
                nc.scalar.activation(k.sq[:, 0, :], osb[:, :], ACT.Square).then_inc(osq_ready, 1)
                if nxt2:
                    high(h + 2, 0)
                act.wait_ge(nrm_done, h + 1)
                ch.link(nc.scalar.activation(k.rstd[:, :], b_x0[:, :], ACT.Ln, bias=k.epsc[:, 0:1], scale=1.0 / P))
                nc.scalar.activation(k.rstd[:, :], k.rstd[:, :], ACT.Exp, scale=-0.5).then_inc(rs_ready, 1)
                act.wait_ge(y_ready, h + 1)

            for s in range(4):
                k.split_high(act, s, 0, s, w_high)
            high(1, 0)
            with act.Fori(0, H - 2) as h:
                ch.loop(3, h)
                step(h, True, True)
            ch.end(H - 2)
            step(H - 2, True, False)
            step(H - 1, False, False)

        @block.gpsimd
        def _(pool):
            def step(h):
                pool.wait_ge(e_ready, h + 1)
                nc.gpsimd.tensor_tensor(kd[:, :], kk[:, :], kdf[:, :], ALU.mult)
                nc.gpsimd.tensor_tensor(qd[:, :], q[:, :], E[:, :], ALU.mult).then_inc(kd_ready, 1)
                for l, b in enumerate(LEVELS):
                    pool.wait_ge(lexp_ready, NL * h + l + 1)
                    if l >= R:
                        pool.wait_ge(lv_done, 8 * h + l + 2 - R)
                    d, x = blocks(dif[:, l % R, :], b), blocks(X[:, l % R, :], b)
                    nc.gpsimd.tensor_tensor(x[:, :, 0, :], blocks(kk[:, :], b)[:, :, 0, :], d[:, :, 0, :], ALU.mult)
                    nc.gpsimd.tensor_tensor(x[:, :, 1, :], blocks(q[:, :], b)[:, :, 1, :], d[:, :, 1, :], ALU.mult).then_inc(x_ready, 1)

            with pool.Fori(0, H) as h:
                step(h)

        @block.vector
        def _(dve):
            ch = Chain(dve, ch_dve)

            def diff(h, l):
                b = LEVELS[l]
                g = G[:, :].rearrange("p (n b) -> p n b", b=2 * b)
                ref = g[:, :, b - 1:b].to_broadcast([P, T // (2 * b), 2 * b])
                if l >= R:
                    dve.wait_ge(x_ready, NL * h + l + 1 - R)
                nc.vector.tensor_tensor(dif[:, l % R, :].rearrange("p (n b) -> p n b", b=2 * b), g, ref, ALU.subtract).then_inc(diff_ready, 1)

            def low(h, s):
                k.split_low(dve, s, 4 * h + s, s, w_high, w_split)

            def step(h, nxt, nxt2):
                dve.wait_ge(proj_done, 4 * h + 2)
                nc.vector.tensor_scalar(fbuf[:, :], b_f[:, :], -44.0, None, ALU.max).then_inc(f_clamped, 1)
                dve.wait_ge(sig_ready, h + 1)
                lb, omlb = k.lb[:, 0, bass.ds(h, 1)], k.lb[:, 1, bass.ds(h, 1)]
                ch.link(nc.vector.tensor_scalar(sig[:, :], sig[:, :], omlb, None, ALU.mult))
                nc.vector.tensor_scalar(fbuf[:, :], sig[:, :], lb, None, ALU.add).then_inc(ft_ready, 1)
                nc.vector.tensor_tensor(kk[:, :], ef[:, :], sig[:, :], ALU.mult)
                if nxt:
                    low(h + 1, 1)
                dve.wait_ge(logf_ready, h + 1)
                ch.link(nc.vector.tensor_tensor_scan(G[:, :], k.c("reset"), logf[:, :], 0.0, ALU.mult, ALU.add))
                nc.vector.tensor_tensor(chunks(kdf), chunks(G), chunks(G)[:, :, P - 1:P].to_broadcast([P, NT, P]), ALU.subtract).then_inc(g_ready, 1)
                for l in range(R):
                    diff(h, l)
                if nxt:
                    low(h + 1, 2)
                dve.wait_ge(lv_done, 8 * h + 1)
                nc.vector.tensor_tensor(chunks(at), chunks(b_x0), mask("ident", 0), ALU.mult).then_inc(at_done, 1)
                for l in range(NL):
                    dve.wait_ge(lv_done, 8 * h + l + 2)
                    dve.wait_ge(at_done, 8 * h + l + 1)
                    if l + R < NL:
                        diff(h, l + R)
                    elif nxt and l == 4:
                        low(h + 1, 3)
                    else:
                        nc.vector.memset(tick[:, l + R - NL:l + R + 1 - NL], 0.0)
                    nc.vector.copy_predicated(chunks(at), mask("levels", l * P).bitcast(U32), chunks(b_x[(l + 1) % 2])).then_inc(at_done, 1)
                dve.wait_ge(kv_done, h + 1)
                ch.link(nc.vector.tensor_copy(S[:, 0, :], b_kv[:, 0:P]))
                ch.link(nc.vector.scalar_tensor_tensor(S[:, 1, :], S[:, 0, :], E[:, 2 * P - 1:2 * P], b_kv[:, P:2 * P], ALU.mult, ALU.add))
                nc.vector.scalar_tensor_tensor(S[:, 2, :], S[:, 1, :], E[:, 3 * P - 1:3 * P], b_kv[:, 2 * P:3 * P], ALU.mult, ALU.add).then_inc(s_ready, 1)
                dve.wait_ge(osb_ready, h + 1)
                ch.link(nc.vector.tensor_tensor(gate[:, :], gate[:, :], osb[:, :], ALU.mult))
                if nxt2:
                    low(h + 2, 0)
                dve.wait_ge(rs_ready, h + 1)
                nc.vector.scalar_tensor_tensor(k.y[:, bass.ds(h, 1), :].rearrange("p a t -> p (a t)"), gate[:, :], k.p("cnorm", h),
                                               k.rstd[:, :], ALU.mult, ALU.mult).then_inc(y_ready, 1)

            for s in range(4):
                low(0, s)
            low(1, 0)
            with dve.Fori(0, H - 2) as h:
                ch.loop(5, h)
                step(h, True, True)
            ch.end(H - 2)
            step(H - 2, True, False)
            step(H - 1, False, False)
    for s in range(4):
        k.loads[s] += H
    del k.ws[2:]


HA = 4
CAP = 15.0


@phase
def ab_gates(k, ahead):
    nc = k.nc
    sem, sb = k.sem, k.sb
    R = sb("gate_rows", [HA, 12, T], F32)
    A = sb("decay_rate", [HA, 1], F32)
    r_i, r_f, r_a, r_b, r_sp, r_F, r_Aa, r_M, r_e, r_abs, r_G, r_t = (R[:, i, :] for i in range(12))
    w_high, w_split, proj_done, rows_taken, tanh_done, e1, l1, e2, rows_ready, spread, spread_used, turned, cols_ready, cexp, ch_d, ch_a = (
        sem("ab_" + s) for s in ("w_high w_split proj_done rows_taken tanh_done exp1 ln1 beta_ready rows_ready spread spread_used "
                                 "turned cols_ready cols_exp ch_dve ch_act").split())
    gb = lambda i: k.p("gbias", i)[0:HA]
    with nc.Block() as block:
        @block.sync
        def _(sp):
            k.load_ahead(sp, ahead)

        @block.tensor
        def _(pe):
            pe.wait_ge(w_split, 1)
            k.by_feature(k.ps[0][:, :], 0).then_inc(proj_done, 1)
            pe.wait_ge(rows_ready, 1)
            pe.wait_ge(e2, 1)
            n = 0
            for kind, row in enumerate((r_M, r_e, r_G, r_b)):
                for h in range(HA):
                    if n >= 4:
                        pe.wait_ge(spread_used, n - 3)
                    nc.tensor.matmul(k.ps[1 + n % 4][:, :], k.c("sel", h * P, h * P + P)[0:HA, :], row, start=True, stop=True).then_inc(spread, 1)
                    n += 1
            for kind, row in enumerate((r_Aa, r_G, r_b)):
                for c in range(NT):
                    at = (kind * NT + c) * HA
                    ins = nc.tensor.transpose(k.ps[5][:, at:at + HA], row[:, c * P:(c + 1) * P], k.c("ident", 0, HA)[0:HA, :])
            ins.then_inc(turned, 1)

        @block.gpsimd
        def _(pool):
            k.split_low(pool, 3, 0, 0, w_high, w_split)

        @block.vector
        def _(dve):
            ch = Chain(dve, ch_d)
            dve.wait_ge(proj_done, 1)
            nc.vector.tensor_scalar(r_i, k.ps[0][0:HA, :], gb(0), 1.0 / CAP, ALU.add, ALU.mult)
            ch.link(nc.vector.tensor_copy(r_f, k.ps[0][32:32 + HA, :]))
            nc.vector.tensor_scalar(r_f, r_f, gb(1), 1.0 / CAP, ALU.add, ALU.mult)
            ch.link(nc.vector.tensor_copy(r_a, k.ps[0][64:64 + HA, :]))
            ch.link(nc.vector.tensor_scalar(r_a, r_a, k.p("adt", 1)[0:HA], None, ALU.add))
            nc.vector.scalar_tensor_tensor(r_abs, r_a, -1.0, r_a, ALU.mult, ALU.max)
            ch.link(nc.vector.tensor_scalar(r_b, k.ps[0][96:96 + HA, :], -44.0, None, ALU.max))
            nc.vector.tensor_scalar(r_a, r_a, 0.0, None, ALU.max).then_inc(rows_taken, 1)
            dve.wait_ge(tanh_done, 1)
            nc.vector.tensor_scalar(r_i, r_i, CAP, None, ALU.mult)
            dve.wait_ge(l1, 1)
            dve.wait_ge(rows_taken, 1)
            ch.link(nc.vector.tensor_tensor_scan(r_F, r_sp, r_sp, 0.0, ALU.add, ALU.max))
            ch.link(nc.vector.tensor_tensor(r_Aa, r_i, r_F, ALU.add))
            ch.link(nc.vector.tensor_tensor_scan(r_M, r_Aa, r_Aa, 0.0, ALU.max, ALU.max))
            nc.vector.tensor_tensor(r_e, r_F, r_M, ALU.subtract)
            ch.link(nc.vector.tensor_tensor(r_t, r_a, r_abs, ALU.add))
            ch.link(nc.vector.tensor_scalar(r_t, r_t, A[:, 0:1], None, ALU.mult))
            nc.vector.tensor_tensor_scan(r_G, k.c("reset")[0:HA, :], r_t, 0.0, ALU.mult, ALU.add).then_inc(rows_ready, 1)
            for n in (0, 1, 2, 3, 8, 9, 10, 11, 12, 13, 14, 15):
                kind, h = divmod(n, HA)
                dve.wait_ge(spread, n + 1)
                if n == 8:
                    dve.wait_ge(spread_used, 8)
                nc.vector.tensor_copy((k.bcm, k.bcg)[kind // 2][:, kind % 2, h, :], k.ps[1 + n % 4][:, :]).then_inc(spread_used, 1)
            dve.wait_ge(turned, 1)
            dve.wait_ge(spread_used, 16)
            t = k.ps[5][:, 0:3 * NT * HA].rearrange("p (k c h) -> p k h c", k=3, c=NT)
            ch.link(nc.vector.tensor_copy(k.cols[:, 0:3, :, :], t))
            last = k.bcg[:, 0, :, :].rearrange("p h (c l) -> p h c l", l=P)[:, :, :, P - 1]
            nc.vector.tensor_copy(k.cols[:, 5, :, :], last)
            ch.link(nc.vector.tensor_tensor(k.cols[:, 3, :, :], k.cols[:, 1, :, :], last, ALU.subtract))
            nc.vector.tensor_copy(k.cols[:, 4, :, :], k.cols[:, 1, :, :]).then_inc(cols_ready, 1)
            dve.wait_ge(cexp, 1)
            ch.link(nc.vector.tensor_tensor(k.cols[:, 4, :, :], k.cols[:, 4, :, :], k.cols[:, 2, :, :], ALU.mult))

        @block.scalar
        def _(act):
            ch = Chain(act, ch_a)
            k.split_high(act, 3, 0, 0, w_high)
            act.wait_ge(rows_taken, 1)
            ch.link(nc.scalar.activation(R[:, 0:2, :], R[:, 0:2, :], ACT.Tanh))
            nc.scalar.activation(r_t, r_f, ACT.Copy, scale=CAP).then_inc(tanh_done, 1)
            nc.scalar.preload_act_table_set(LNEXP)
            act.wait_ge(tanh_done, 1)
            nc.scalar.activation(r_sp, r_t, ACT.Exp, scale=-1.0)
            nc.scalar.activation(r_abs, r_abs, ACT.Exp, scale=-1.0)
            nc.scalar.activation(A[:, 0:1], k.p("adt", 0)[0:HA], ACT.Exp)
            ch.link(nc.scalar.activation(r_b, r_b, ACT.Exp, scale=-1.0))
            nc.scalar.activation(r_sp, r_sp, ACT.Ln, bias=1.0)
            nc.scalar.activation(r_abs, r_abs, ACT.Ln, bias=1.0).then_inc(l1, 1)
            ch.link(nc.scalar.activation(r_b, r_b, ACT.Ln, bias=1.0))
            nc.scalar.activation(r_b, r_b, ACT.Exp, scale=-1.0).then_inc(e2, 1)
            for n in range(4, 8):
                act.wait_ge(spread, n + 1)
                act.wait_ge(spread_used, n)
                nc.scalar.activation(k.bcm[:, 1, n - 4, :], k.ps[1 + n % 4][:, :], ACT.Exp).then_inc(spread_used, 1)
            act.wait_ge(cols_ready, 1)
            nc.scalar.activation(k.cols[:, 3, :, :], k.cols[:, 3, :, :], ACT.Exp)
            nc.scalar.activation(k.cols[:, 4:6, :, :], k.cols[:, 4:6, :, :], ACT.Exp, scale=-1.0).then_inc(cexp, 1)
    k.loads[3] += 1


@phase
def mlstm(k, weights, ahead):
    nc = k.nc
    sem, sb = k.sem, k.sb
    H = HA
    DK = 64
    acc, q, kk, v, og, osb, den = (sb(f"m_{s}", [n, T], F32) for s, n in
                                   (("acc", P), ("q", DK), ("k", DK), ("v", P), ("og", P), ("o", P), ("den", P)))
    hc = sb("m_hc", [P, NT], F32)
    off = [0, 512, 896, 1152, 1280]
    W = sb("m_W", [P, off[4]], F32)
    b_qk, b_o, b_v, _, b_s0, b_s1, b_num, b_den = k.ps
    b_s = [b_s0, b_s1]
    w_high, w_split = sem("m_w_high"), sem("m_w_split")
    k.ws.append((sb("m_w2_high", [P, D], F32R), sb("m_w2_low", [P, D], F32R)))
    (proj_done, tap_done, conv_done, act_prep, o_clamped, qk_ready, og_ready, arg_ready, d_ready, st_done, wt_ready, pv_done,
     osb_ready, osq_ready, nrm_done, rs_ready, y_ready, ch_act, ch_dve) = (sem("m_" + s) for s in (
         "proj_done tap_done conv_done act_prep o_clamped qk_ready og_ready arg_ready d_ready st_done wt_ready pv_done "
         "osb_ready osq_ready nrm_done rs_ready y_ready ch_act ch_dve").split())

    with nc.Block() as block:
        @block.sync
        def _(sp):
            k.first_loads(sp, [weights[s, :, :] for s in range(3)])
            with sp.Fori(1, H) as h:
                for s in range(3):
                    sp.wait_ge(w_split, 3 * h - 2 + s)
                    k.load(sp, s, weights[bass.ds(3 * h + s, 1), :, :].rearrange("a p d -> p (a d)"))
            sp.wait_ge(w_split, 3 * H)
            k.load_ahead(sp, ahead)

        @block.tensor
        def _(pe):
            def project(h, s, first=False):
                pe.wait_ge(w_split, 3 * h + s + 1)
                if not first:
                    if s == 0:
                        pe.wait_ge(conv_done, h)
                    elif s == 1:
                        pe.wait_ge(o_clamped, h)
                    else:
                        pe.wait_ge(act_prep, h)
                ins = k.by_feature(k.ps[s][:, :], s) if s < 2 else k.by_token(b_v, s)
                ins.then_inc(proj_done, 1)

            def score(h, j):
                if j >= 2:
                    pe.wait_ge(wt_ready, 4 * h + j - 1)
                nc.tensor.matmul(b_s[j % 2][:, 0:T - j * P], kk[:, j * P:(j + 1) * P], q[:, j * P:T], start=True, stop=True).then_inc(st_done, 1)

            def core(h, nxt, first):
                if nxt:
                    project(h + 1, 0)
                pe.wait_ge(qk_ready, h + 1)
                if not first:
                    pe.wait_ge(rs_ready, h)
                score(h, 0)
                score(h, 1)
                if nxt:
                    project(h + 1, 1)
                score(h, 2)
                score(h, 3)
                pe.wait_ge(act_prep, h + 1)
                for j in range(NT):
                    pe.wait_ge(wt_ready, 4 * h + j + 1)
                    w = W[:, off[j]:off[j + 1]]
                    nc.tensor.matmul(b_num[:, j * P:T], v[:, j * P:(j + 1) * P], w, start=j == 0, stop=j == NT - 1)
                    ins = nc.tensor.matmul(b_den[:, j * P:T], k.c("ones"), w, start=j == 0, stop=j == NT - 1)
                ins.then_inc(pv_done, 1)
                if nxt:
                    project(h + 1, 2)
                pe.wait_ge(osq_ready, h + 1)
                nc.tensor.matmul(b_s0[:, :], k.c("ones"), k.sq[:, 0, :], start=True, stop=True).then_inc(nrm_done, 1)

            for s in range(3):
                project(0, s, first=True)
            core(0, True, True)
            with pe.Fori(1, H - 1) as h:
                core(h, True, False)
            core(H - 1, False, False)

        @block.scalar
        def _(act):
            ch = Chain(act, ch_act)

            def high(h, s):
                act.wait_ge(proj_done, 3 * h + s - 2)
                k.split_high(act, s, h, s, w_high)

            def step(h, nxt):
                act.wait_ge(proj_done, 3 * h + 1)
                nc.scalar.activation(acc[:, :], b_qk[:, :], ACT.Copy, scale=k.p("mconv", 4 * h + 3)).then_inc(tap_done, 1)
                act.wait_ge(proj_done, 3 * h + 3)
                nc.scalar.activation(v[:, :], b_v[:, :], ACT.Copy).then_inc(act_prep, 1)
                if nxt:
                    for s in range(3):
                        high(h + 1, s)
                act.wait_ge(conv_done, h + 1)
                nc.scalar.activation(q[:, :], acc[0:DK, :], ACT.Silu)
                nc.scalar.activation(kk[:, :], acc[DK:P, :], ACT.Silu).then_inc(qk_ready, 1)
                nc.scalar.preload_act_table_set(LNEXP)
                act.wait_ge(arg_ready, h + 1)
                nc.scalar.activation(W[:, :], W[:, :], ACT.Exp, scale=-1.0).then_inc(d_ready, 1)
                act.wait_ge(o_clamped, h + 1)
                ch.link(nc.scalar.activation(og[:, :], og[:, :], ACT.Exp, scale=-1.0))
                ch.link(nc.scalar.activation(og[:, :], og[:, :], ACT.Ln, bias=1.0))
                nc.scalar.activation(og[:, :], og[:, :], ACT.Exp, scale=-1.0).then_inc(og_ready, 1)
                act.wait_ge(osb_ready, h + 1)
                nc.scalar.activation(k.sq[:, 0, :], osb[:, :], ACT.Square).then_inc(osq_ready, 1)
                act.wait_ge(nrm_done, h + 1)
                ch.link(nc.scalar.activation(k.rstd[:, :], b_s0[:, :], ACT.Ln, bias=k.epsc[:, 0:1], scale=1.0 / P))
                nc.scalar.activation(k.rstd[:, :], k.rstd[:, :], ACT.Exp, scale=-0.5).then_inc(rs_ready, 1)

            for s in range(3):
                k.split_high(act, s, 0, s, w_high)
            with act.Fori(0, H - 1) as h:
                ch.loop(3, h)
                step(h, True)
            ch.end(H - 1)
            step(H - 1, False)

        @block.gpsimd
        def _(pool):
            for s in range(3):
                k.split_low(pool, s, s, s, w_high, w_split)
            with pool.Fori(1, H) as h:
                for s in range(3):
                    k.split_low(pool, s, 3 * h + s, s, w_high, w_split)

        @block.vector
        def _(dve):
            ch = Chain(dve, ch_dve)

            def step(h):
                ch.link(nc.vector.tensor_copy(hc[:, :].rearrange("p (a c) -> p a c", a=1), k.cols[:, 0, bass.ds(h, 1), :]))
                for j in range(NT):
                    ins = nc.vector.tensor_scalar(W[:, off[j]:off[j + 1]].rearrange("p (a t) -> p a t", a=1),
                                                  k.bcm[:, 0, bass.ds(h, 1), j * P:T], hc[:, j:j + 1], 0.0, ALU.subtract, ALU.max)
                ins.then_inc(arg_ready, 1)
                dve.wait_ge(tap_done, h + 1)
                for tap in (2, 1, 0):
                    ins = nc.vector.scalar_tensor_tensor(acc[:, 3 - tap:T], b_qk[:, 0:T - 3 + tap], k.p("mconv", 4 * h + tap), acc[:, 3 - tap:T], ALU.mult, ALU.add)
                    if tap:
                        ch.link(ins)
                ins.then_inc(conv_done, 1)
                dve.wait_ge(proj_done, 3 * h + 2)
                nc.vector.tensor_scalar(og[:, :], b_o[:, :], -44.0, None, ALU.max).then_inc(o_clamped, 1)
                dve.wait_ge(d_ready, h + 1)
                for j in range(NT):
                    dve.wait_ge(st_done, 4 * h + j + 1)
                    w = W[:, off[j]:off[j + 1]]
                    ch.link(nc.vector.scalar_tensor_tensor(w, b_s[j % 2][:, 0:T - j * P], DK ** -0.5, w, ALU.mult, ALU.mult))
                    nc.vector.tensor_tensor(w[:, 0:P], w[:, 0:P], k.c("upper"), ALU.mult).then_inc(wt_ready, 1)
                dve.wait_ge(pv_done, h + 1)
                ch.link(nc.vector.scalar_tensor_tensor(den[:, :].rearrange("p (a t) -> p a t", a=1), b_den[:, :].rearrange("p (a t) -> p a t", a=1), -1.0,
                                                       k.bcm[:, 1, bass.ds(h, 1), :], ALU.mult, ALU.max))
                ch.link(nc.vector.tensor_tensor(den[:, :], den[:, :], b_den[:, :], ALU.max))
                ch.link(nc.vector.reciprocal(den[:, :], den[:, :]))
                nc.vector.tensor_tensor(osb[:, :], b_num[:, :], den[:, :], ALU.mult).then_inc(osb_ready, 1)
                dve.wait_ge(og_ready, h + 1)
                dve.wait_ge(osb_ready, h + 1)
                ch.link(nc.vector.tensor_tensor(og[:, :], og[:, :], osb[:, :], ALU.mult))
                dve.wait_ge(rs_ready, h + 1)
                nc.vector.scalar_tensor_tensor(k.y[:, bass.ds(h, 1), :].rearrange("p a t -> p (a t)"), og[:, :], k.p("mnorm", h),
                                               k.rstd[:, :], ALU.mult, ALU.mult).then_inc(y_ready, 1)
                dve.wait_ge(y_ready, h + 1)

            with dve.Fori(0, H) as h:
                ch.loop(1 + 2 + NT + 4, h)
                step(h)
            ch.end(H)
    k.ws.pop()
    for s in range(3):
        k.loads[s] += H


@phase
def delta(k, weights, ahead):
    nc = k.nc
    sem, sb = k.sem, k.sb
    H, NL = HA, len(LEVELS)
    scale = P ** -0.5
    q, kk, v, gate, rk, dec, db, at, At, EG, qd, kd, kb, vb, BT, Tm, TT, Y, nwT, vn, osb = (sb("g_" + s, [P, T], F32) for s in (
        "q k v gate rk dec db attn At EG qd kd kb vb BT T TT Y nwT vn o").split())
    S = sb("g_S", [P, NT - 1, P], F32)
    hc = sb("g_hc", [P, 6, NT], F32)
    b0, b1, b2, b3, b4, b5, b6, b7 = k.ps
    conv = ((b0, q), (b1, kk), (b2, v))
    w_high, w_split = sem("g_w_high"), sem("g_w_split")
    k.ws += [(sb(f"g_w{s}_high", [P, D], F32R), sb(f"g_w{s}_low", [P, D], F32R)) for s in (2, 3)]
    (proj_done, tap_done, conv_done, silu_done, gate_done, hc_ready, sq_ready, nrm_qk, rqk_ready, qk_ready, qk_turned, v_turned, kdb_ready,
     vb_ready, kk_done, arg_ready, dec_ready, eg_ready, masked, db_ready, t_ready, bt_ready, y_done, y_copied, z_done, w_done, nw_ready, vn_done, vn_ready,
     kv_done, s_ready, o_done, osb_ready, osq_ready, nrm_done, rs_ready, y_ready, qd_ready, ch_act, ch_dve, ch_pool) = (sem("g_" + s) for s in (
         "proj_done tap_done conv_done silu_done gate_done hc_ready sq_ready nrm_qk rqk_ready qk_ready qk_turned v_turned kdb_ready "
         "vb_ready kk_done arg_ready dec_ready eg_ready masked db_ready t_ready bt_ready y_done y_copied z_done w_done nw_ready vn_done vn_ready "
         "kv_done s_ready o_done osb_ready osq_ready nrm_done rs_ready y_ready qd_ready ch_act ch_dve ch_pool").split())

    def cs(c):
        return slice(c * P, (c + 1) * P)

    def chunks(x):
        return x[:, :].rearrange("p (c l) -> p c l", l=P)

    def mask(name, lo=0):
        return k.c(name, lo, lo + P).rearrange("p (a l) -> p a l", a=1).to_broadcast([P, NT, P])

    def row(kind, h):
        return k.bcg[:, kind, bass.ds(h, 1), :]

    def one(x):
        return x.rearrange("p (a t) -> p a t", a=1)

    with nc.Block() as block:
        @block.sync
        def _(sp):
            k.first_loads(sp, [weights[s, :, :] for s in range(4)])
            with sp.Fori(1, H) as h:
                for s in range(4):
                    sp.wait_ge(w_split, 4 * h - 3 + s)
                    k.load(sp, s, weights[bass.ds(4 * h + s, 1), :, :].rearrange("a p d -> p (a d)"))
            sp.wait_ge(w_split, 4 * H)
            k.load_ahead(sp, ahead)

        @block.tensor
        def _(pe):
            def project(h, lo, hi, first=False):
                for n in range(lo, hi):
                    s, m = divmod(n, KD)
                    if m == 0:
                        pe.wait_ge(w_split, 4 * h + s + 1)
                        if not first:
                            if s < 3:
                                pe.wait_ge(conv_done, 3 * h - 2 + s)
                            else:
                                pe.wait_ge(gate_done, h)
                    ins = k.product(k.ps[s][:, :], [x[:, m * P:(m + 1) * P] for x in k.ws[s]], [x[:, m, :] for x in (k.uh, k.ul)],
                                    m == 0, m == KD - 1)
                    if m == KD - 1:
                        ins.then_inc(proj_done, 1)

            def four(bank, lhsT, rhs, cols=None):
                for c in range(NT):
                    ins = nc.tensor.matmul(bank[:, cs(c)], lhsT[:, cs(c)], rhs[:, cs(c)], start=True, stop=True)
                return ins

            def core(h, nxt, first):
                fill = (lambda lo, hi: project(h + 1, lo, hi)) if nxt else (lambda lo, hi: None)
                fill(0, 4)
                if not first:
                    pe.wait_ge(rs_ready, h)
                pe.wait_ge(sq_ready, h + 1)
                nc.tensor.matmul(b4[:, :], k.c("ones"), k.sq[:, 0, :], start=True, stop=True)
                nc.tensor.matmul(b5[:, :], k.c("ones"), k.sq[:, 1, :], start=True, stop=True).then_inc(nrm_qk, 1)
                if not first:
                    pe.wait_ge(osb_ready, h)
                for c in range(NT):
                    ins = nc.tensor.transpose(b7[:, cs(c)], v[:, cs(c)], k.c("ident"))
                ins.then_inc(v_turned, 1)
                fill(4, 8)
                pe.wait_ge(qk_ready, h + 1)
                for c in range(NT):
                    ins = nc.tensor.transpose(b6[:, cs(c)], kk[:, cs(c)], k.c("ident"))
                ins.then_inc(qk_turned, 1)
                four(b4, kk, kk)
                four(b5, kk, q).then_inc(kk_done, 1)
                fill(8, 11)
                for l in range(NL):
                    pe.wait_ge(bt_ready, NL * h + l + 1)
                    pe.wait_ge(t_ready, 8 * h + l + 1)
                    four(b4, BT, Tm).then_inc(y_done, 1)
                    fill(11 + 3 * l, 12 + 3 * l)
                    pe.wait_ge(y_copied, NL * h + l + 1)
                    if l == 0:
                        pe.wait_ge(kdb_ready, h + 1)
                    four(b5, TT, Y)
                    four(b6, Y, TT).then_inc(z_done, 1)
                    fill(12 + 3 * l, 14 + 3 * l)
                pe.wait_ge(t_ready, 8 * h + 8)
                for c in range(1, NT):
                    ins = nc.tensor.matmul(b4[:, cs(c)], kb[:, cs(c)], TT[:, cs(c)], start=True, stop=True)
                ins.then_inc(w_done, 1)
                pe.wait_ge(vb_ready, h + 1)
                pe.wait_ge(qd_ready, h + 1)
                for c in range(NT):
                    if c == 1:
                        pe.wait_ge(nw_ready, h + 1)
                    ins = nc.tensor.matmul(b5[:, cs(c)], TT[:, cs(c)], vb[:, cs(c)], start=True, stop=c == 0)
                    if c:
                        pe.wait_ge(s_ready, 3 * h + c)
                        ins = nc.tensor.matmul(b5[:, cs(c)], nwT[:, cs(c)], S[:, c - 1, :], start=False, stop=True)
                    ins.then_inc(vn_done, 1)
                    if c:
                        nc.tensor.matmul(b7[:, cs(c)], S[:, c - 1, :], qd[:, cs(c)], start=True, stop=False)
                    pe.wait_ge(vn_ready, 4 * h + c + 1)
                    ins = nc.tensor.matmul(b7[:, cs(c)], vn[:, cs(c)], at[:, cs(c)], start=c == 0, stop=True)
                    if c == NT - 1:
                        ins.then_inc(o_done, 1)
                    else:
                        nc.tensor.matmul(b6[:, cs(c)], kd[:, cs(c)], vn[:, cs(c)], start=True, stop=True).then_inc(kv_done, 1)
                pe.wait_ge(osq_ready, h + 1)
                nc.tensor.matmul(b4[:, :], k.c("ones"), k.sq[:, 0, :], start=True, stop=True).then_inc(nrm_done, 1)

            project(0, 0, 32, first=True)
            core(0, True, True)
            with pe.Fori(1, H - 1) as h:
                core(h, True, False)
            core(H - 1, False, False)

        @block.scalar
        def _(act):
            ch = Chain(act, ch_act)

            def high(h, s):
                act.wait_ge(proj_done, 4 * h + s - 3)
                k.split_high(act, s, h, s, w_high)

            def step(h, nxt, nxt2):
                for i, (bank, x) in enumerate(conv):
                    act.wait_ge(proj_done, 4 * h + i + 1)
                    nc.scalar.activation(x[:, :], bank[:, :], ACT.Copy, scale=k.p("gconv", 12 * h + 4 * i + 3)).then_inc(tap_done, 1)
                act.wait_ge(proj_done, 4 * h + 4)
                nc.scalar.activation(gate[:, :], b3[:, :], ACT.Silu).then_inc(gate_done, 1)
                for i, (bank, x) in enumerate(conv):
                    act.wait_ge(conv_done, 3 * h + i + 1)
                    nc.scalar.activation(x[:, :], x[:, :], ACT.Silu).then_inc(silu_done, 1)
                act.wait_ge(silu_done, 3 * h + 3)
                nc.scalar.activation(k.sq[:, 0, :], q[:, :], ACT.Square)
                nc.scalar.activation(k.sq[:, 1, :], kk[:, :], ACT.Square).then_inc(sq_ready, 1)
                nc.scalar.preload_act_table_set(LNEXP)
                act.wait_ge(nrm_qk, h + 1)
                nc.scalar.activation(k.rstd[:, :], b4[:, :], ACT.Ln, bias=k.epsc[:, 0:1])
                ch.link(nc.scalar.activation(rk[:, :], b5[:, :], ACT.Ln, bias=k.epsc[:, 0:1]))
                nc.scalar.activation(k.rstd[:, :], k.rstd[:, :], ACT.Exp, scale=-0.5)
                nc.scalar.activation(rk[:, :], rk[:, :], ACT.Exp, scale=-0.5).then_inc(rqk_ready, 1)
                act.wait_ge(v_turned, h + 1)
                act.wait_ge(hc_ready, h + 1)
                for c in range(NT):
                    ins = nc.scalar.activation(vb[:, cs(c)], b7[:, cs(c)], ACT.Copy, scale=hc[:, 2, c:c + 1])
                ins.then_inc(vb_ready, 1)
                act.wait_ge(arg_ready, h + 1)
                nc.scalar.activation(dec[:, :], dec[:, :], ACT.Exp, scale=-1.0).then_inc(dec_ready, 1)
                nc.scalar.activation(one(EG[:, :]), row(0, h), ACT.Exp, scale=-1.0).then_inc(eg_ready, 1)
                if nxt:
                    high(h + 1, 1)
                for l in range(NL):
                    act.wait_ge(y_done, NL * h + l + 1)
                    nc.scalar.activation(Y[:, :], b4[:, :], ACT.Copy).then_inc(y_copied, 1)
                    if nxt and l in (0, 2):
                        high(h + 1, 2 + l // 2)
                if nxt2:
                    high(h + 2, 0)
                act.wait_ge(w_done, h + 1)
                nc.scalar.activation(nwT[:, P:T], b4[:, P:T], ACT.Copy, scale=-1.0).then_inc(nw_ready, 1)
                for c in range(NT):
                    act.wait_ge(vn_done, NT * h + c + 1)
                    nc.scalar.activation(vn[:, cs(c)], b5[:, cs(c)], ACT.Copy).then_inc(vn_ready, 1)
                act.wait_ge(o_done, h + 1)
                nc.scalar.activation(osb[:, :], b7[:, :], ACT.Copy, scale=scale).then_inc(osb_ready, 1)
                act.wait_ge(osb_ready, h + 1)
                nc.scalar.activation(k.sq[:, 0, :], osb[:, :], ACT.Square).then_inc(osq_ready, 1)
                act.wait_ge(nrm_done, h + 1)
                ch.link(nc.scalar.activation(k.rstd[:, :], b4[:, :], ACT.Ln, bias=k.epsc[:, 0:1], scale=1.0 / P))
                nc.scalar.activation(k.rstd[:, :], k.rstd[:, :], ACT.Exp, scale=-0.5).then_inc(rs_ready, 1)
                act.wait_ge(y_ready, h + 1)

            for s in range(4):
                k.split_high(act, s, 0, s, w_high)
            high(1, 0)
            with act.Fori(0, H - 2) as h:
                ch.loop(2, h)
                step(h, True, True)
            ch.end(H - 2)
            step(H - 2, True, False)
            step(H - 1, False, False)

        @block.gpsimd
        def _(pool):
            ch = Chain(pool, ch_pool)

            def low(h, s):
                k.split_low(pool, s, 4 * h + s, s, w_high, w_split)

            def step(h, nxt, nxt2):
                pool.wait_ge(dec_ready, h + 1)
                ch.link(nc.gpsimd.tensor_tensor(chunks(dec), chunks(dec), mask("upper"), ALU.mult))
                nc.gpsimd.tensor_tensor(one(db[:, :]), one(dec[:, :]), row(1, h), ALU.mult).then_inc(db_ready, 1)
                pool.wait_ge(eg_ready, h + 1)
                pool.wait_ge(qk_ready, h + 1)
                nc.gpsimd.tensor_tensor(qd[:, :], q[:, :], EG[:, :], ALU.mult).then_inc(qd_ready, 1)
                if nxt:
                    low(h + 1, 1)
                pool.wait_ge(masked, h + 1)
                for l in range(NL):
                    if l:
                        pool.wait_ge(y_done, NL * h + l)
                    nc.gpsimd.tensor_tensor(chunks(BT), chunks(At), mask("levels", l * P), ALU.mult).then_inc(bt_ready, 1)
                    if nxt and l in (0, 2):
                        low(h + 1, 2 + l // 2)
                if nxt2:
                    low(h + 2, 0)

            for s in range(4):
                low(0, s)
            low(1, 0)
            with pool.Fori(0, H - 2) as h:
                ch.loop(1, h)
                step(h, True, True)
            ch.end(H - 2)
            step(H - 2, True, False)
            step(H - 1, False, False)

        @block.vector
        def _(dve):
            ch = Chain(dve, ch_dve)

            def step(h):
                nc.vector.tensor_copy(hc[:, :, :].rearrange("p k (a c) -> p k a c", a=1), k.cols[:, :, bass.ds(h, 1), :]).then_inc(hc_ready, 1)
                for i, (bank, x) in enumerate(conv):
                    dve.wait_ge(tap_done, 3 * h + i + 1)
                    for tap in (2, 1, 0):
                        ins = nc.vector.scalar_tensor_tensor(x[:, 3 - tap:T], bank[:, 0:T - 3 + tap], k.p("gconv", 12 * h + 4 * i + tap), x[:, 3 - tap:T], ALU.mult, ALU.add)
                        if tap:
                            ch.link(ins)
                    ins.then_inc(conv_done, 1)
                dve.wait_ge(hc_ready, h + 1)
                for c in range(NT):
                    g = k.bcg[:, 0, bass.ds(h, 1), cs(c)]
                    ins = nc.vector.tensor_scalar(one(dec[:, cs(c)]), g, hc[:, 1, c:c + 1], 0.0, ALU.subtract, ALU.max)
                ins.then_inc(arg_ready, 1)
                nc.vector.tensor_copy(chunks(Tm), mask("ident"))
                nc.vector.tensor_copy(chunks(TT), mask("ident")).then_inc(t_ready, 1)
                dve.wait_ge(rqk_ready, h + 1)
                nc.vector.tensor_tensor(kk[:, :], kk[:, :], rk[:, :], ALU.mult)
                nc.vector.tensor_tensor(q[:, :], q[:, :], k.rstd[:, :], ALU.mult).then_inc(qk_ready, 1)
                dve.wait_ge(kk_done, h + 1)
                dve.wait_ge(db_ready, h + 1)
                nc.vector.tensor_tensor(At[:, :], b4[:, :], db[:, :], ALU.mult).then_inc(masked, 1)
                nc.vector.tensor_tensor(at[:, :], b5[:, :], dec[:, :], ALU.mult)
                for c in range(NT):
                    nc.vector.tensor_scalar(kd[:, cs(c)], b6[:, cs(c)], hc[:, 3, c:c + 1], None, ALU.mult)
                    ins = nc.vector.tensor_scalar(kb[:, cs(c)], b6[:, cs(c)], hc[:, 4, c:c + 1], None, ALU.mult)
                ins.then_inc(kdb_ready, 1)
                for l in range(NL):
                    dve.wait_ge(z_done, NL * h + l + 1)
                    dve.wait_ge(t_ready, 8 * h + l + 1)
                    nc.vector.tensor_tensor(Tm[:, :], Tm[:, :], b5[:, :], ALU.subtract)
                    nc.vector.tensor_tensor(TT[:, :], TT[:, :], b6[:, :], ALU.subtract).then_inc(t_ready, 1)
                for c in range(NT - 1):
                    dve.wait_ge(kv_done, 3 * h + c + 1)
                    if c == 0:
                        nc.vector.tensor_copy(S[:, 0, :], b6[:, cs(0)]).then_inc(s_ready, 1)
                    else:
                        dve.wait_ge(s_ready, 3 * h + c)
                        nc.vector.scalar_tensor_tensor(S[:, c, :], S[:, c - 1, :], hc[:, 5, c:c + 1], b6[:, cs(c)], ALU.mult, ALU.add).then_inc(s_ready, 1)
                dve.wait_ge(osb_ready, h + 1)
                ch.link(nc.vector.tensor_tensor(gate[:, :], gate[:, :], osb[:, :], ALU.mult))
                dve.wait_ge(rs_ready, h + 1)
                nc.vector.scalar_tensor_tensor(k.y[:, bass.ds(HA + h, 1), :].rearrange("p a t -> p (a t)"), gate[:, :], k.p("gnorm", h),
                                               k.rstd[:, :], ALU.mult, ALU.mult).then_inc(y_ready, 1)
                dve.wait_ge(y_ready, h + 1)

            with dve.Fori(0, H) as h:
                ch.loop(7, h)
                step(h)
            ch.end(H)
    for s in range(4):
        k.loads[s] += H
    del k.ws[2:]


HI, DI = 8, 32
HF = 6
DH = 64
TOPK = 128
NEG = -3e38
OFF = [0, P, 3 * P, 6 * P, 10 * P]


@phase
def shared_inputs(k, weights, pool_w, ahead):
    nc = k.nc
    sem, sb = k.sem, k.sb
    rows = sb("s_rows", [HI, 4, T], F32)
    iq = sb("s_iq", [P, 2, T], F32)
    ik = sb("s_ik", [P, T], F32)
    pv, pg, pp, pw = (sb("s_" + s, [P, 2, n], F32) for s, n in (("pv", T), ("pg", T), ("pp", T), ("pw", P)))
    s2 = sb("s_sum", [P, 2, T], F32)
    relu = sb("s_relu", [P, 2, T], F32)
    iw = sb("s_iw", [P, NT, HI], F32)
    sc = sb("s_score", [P, OFF[4]], F32)
    m8 = sb("s_max8", [P, NT, 8], F32)
    NW = 8
    w_high, w_split = sem("s_w_high"), sem("s_w_split")
    k.ws += [(sb(f"s_w{s}_high", [P, D], F32R), sb(f"s_w{s}_low", [P, D], F32R)) for s in (2, 3)]
    (pw_loaded, proj_done, bank_free, rows_taken, ln_done, f_ready, spread, spread_used, turned, iw_ready, dots_done, relu_ready,
     relu_used, pool_ready, pool_done, ch_dve, ch_act, ch_tk) = (sem("s_" + s) for s in (
         "pw_loaded proj_done bank_free rows_taken ln_done f_ready spread spread_used turned iw_ready dots_done relu_ready "
         "relu_used pool_ready pool_done ch_dve ch_act ch_topk").split())
    items = [(t, h) for t in range(1, NT) for h in range(HI)]
    r_f, r_n, r_F, r_w = (rows[:, i, :] for i in range(4))

    with nc.Block() as block:
        @block.sync
        def _(sp):
            k.first_loads(sp, [weights[s, :, :] for s in range(4)])
            for n in range(4, NW):
                sp.wait_ge(w_split, n - 3)
                k.load(sp, n % 4, weights[n, :, :])
            sp.dma_start(pw[:, :, :], pool_w).then_inc(pw_loaded, 16)
            sp.wait_ge(w_split, NW)
            k.load_ahead(sp, ahead)

        @block.tensor
        def _(pe):
            def project(n):
                pe.wait_ge(w_split, n + 1)
                if n == 4:
                    pe.wait_ge(iw_ready, 1)
                if n > 4:
                    pe.wait_ge(bank_free, n - 4)
                k.by_feature(k.ps[n % 4][:, :], n % 4).then_inc(proj_done, 1)
            for n in range(5):
                project(n)
            pe.wait_ge(iw_ready, 1)
            for t in range(NT):
                ins = nc.tensor.transpose(k.ps[4][:, t * HI:(t + 1) * HI], r_w[:, t * P:(t + 1) * P], k.c("ident", 0, HI)[0:HI, :])
            ins.then_inc(turned, 1)
            pe.wait_ge(bank_free, 3)
            pe.wait_ge(iw_ready, 2)
            for n, (t, h) in enumerate(items):
                if n >= 4:
                    pe.wait_ge(relu_ready, n - 3)
                r = slice(DI * (h % 4), DI * (h % 4) + DI)
                nc.tensor.matmul(k.ps[4 + n % 4][:, 0:(t + 1) * P], iq[r, h // 4, t * P:(t + 1) * P], ik[r, 0:(t + 1) * P],
                                 start=True, stop=True, tile_position=(DI * (h % 4), 0)).then_inc(dots_done, 1)
            for n in range(5, NW):
                project(n)
            pe.wait_ge(f_ready, 1)
            for h in range(HF):
                if h < 4:
                    pe.wait_ge(relu_ready, len(items))
                else:
                    pe.wait_ge(spread_used, h - 3)
                nc.tensor.matmul(k.ps[4 + h % 4][:, :], k.c("sel", h * P, h * P + P)[0:HF, :], r_F[0:HF, :], start=True, stop=True).then_inc(spread, 1)
            pe.wait_ge(pw_loaded, 16)
            pe.wait_ge(pool_ready, 2)
            pe.wait_ge(bank_free, 7)
            for i in range(2):
                nc.tensor.matmul(k.ps[i][:, :], pw[:, i, :], pp[:, i, :], start=True, stop=True).then_inc(pool_done, 1)

        @block.scalar
        def _(act):
            ch = Chain(act, ch_act)
            def high(n):
                if n >= 4:
                    act.wait_ge(proj_done, n - 3)
                k.split_high(act, n % 4, n // 4, n % 4, w_high)
            for n in range(4):
                high(n)
            act.wait_ge(proj_done, 2)
            nc.scalar.activation(ik[:, :], k.ps[1][:, :], ACT.Copy).then_inc(bank_free, 1)
            high(4)
            high(5)
            for i in range(2):
                act.wait_ge(proj_done, 3 + i)
                nc.scalar.activation(iq[:, i, :], k.ps[2 + i][:, :], ACT.Copy).then_inc(bank_free, 1)
            high(6)
            high(7)
            nc.scalar.preload_act_table_set(LNEXP)
            act.wait_ge(rows_taken, 1)
            ch.link(nc.scalar.activation(r_n[0:HF], r_n[0:HF], ACT.Exp, scale=-1.0))
            nc.scalar.activation(r_n[0:HF], r_n[0:HF], ACT.Ln, bias=1.0).then_inc(ln_done, 1)
            for n, (t, h) in enumerate(items):
                act.wait_ge(dots_done, n + 1)
                if n >= 2:
                    act.wait_ge(relu_used, n - 1)
                nc.scalar.activation(relu[:, n % 2, 0:(t + 1) * P], k.ps[4 + n % 4][:, 0:(t + 1) * P], ACT.Relu).then_inc(relu_ready, 1)
                if n == 3:
                    act.wait_ge(proj_done, 5)
                    nc.scalar.activation(pv[:, 0, :], k.ps[0][:, :], ACT.Copy).then_inc(bank_free, 1)
            act.wait_ge(proj_done, 6)
            nc.scalar.activation(pv[:, 1, :], k.ps[1][:, :], ACT.Copy).then_inc(bank_free, 1)
            for i in range(2):
                act.wait_ge(proj_done, 7 + i)
                nc.scalar.activation(pg[:, i, :], k.ps[2 + i][:, :], ACT.Silu).then_inc(bank_free, 1)

        @block.gpsimd
        def _(pool):
            for n in range(NW):
                k.split_low(pool, n % 4, n, n % 4, w_high, w_split)

        @block.vector
        def _(dve):
            ch = Chain(dve, ch_dve)
            dve.wait_ge(proj_done, 1)
            nc.vector.tensor_scalar(r_f[0:HF], k.ps[0][0:HF, :], k.p("foxb", 0)[0:HF], None, ALU.add)
            nc.vector.tensor_scalar(r_w, k.ps[0][32:32 + HI, :], HI ** -0.5, None, ALU.mult).then_inc(iw_ready, 1)
            dve.wait_ge(iw_ready, 1)
            ch.link(nc.vector.scalar_tensor_tensor(r_n[0:HF], r_f[0:HF], -1.0, r_f[0:HF], ALU.mult, ALU.max))
            nc.vector.tensor_scalar(r_f[0:HF], r_f[0:HF], -1.0, 0.0, ALU.mult, ALU.max).then_inc(rows_taken, 1)
            dve.wait_ge(rows_taken, 1)
            dve.wait_ge(ln_done, 1)
            ch.link(nc.vector.tensor_tensor(r_f[0:HF], r_f[0:HF], r_n[0:HF], ALU.add))
            nc.vector.tensor_tensor_scan(r_F[0:HF], r_f[0:HF], r_f[0:HF], 0.0, ALU.add, ALU.max).then_inc(f_ready, 1)
            dve.wait_ge(turned, 1)
            nc.vector.tensor_copy(iw[:, :, :], k.ps[4][:, 0:NT * HI].rearrange("p (t h) -> p t h", h=HI)).then_inc(iw_ready, 1)
            dve.wait_ge(iw_ready, 2)
            for n, (t, h) in enumerate(items):
                dve.wait_ge(relu_ready, n + 1)
                s, r, w = sc[:, OFF[t]:OFF[t + 1]], relu[:, n % 2, 0:(t + 1) * P], iw[:, t, h:h + 1]
                if h == 0:
                    nc.vector.tensor_scalar(s, r, w, None, ALU.mult).then_inc(relu_used, 1)
                else:
                    dve.wait_ge(relu_used, n)
                    nc.vector.scalar_tensor_tensor(s, r, w, s, ALU.mult, ALU.add).then_inc(relu_used, 1)
                if h == HI - 1:
                    dve.wait_ge(relu_used, n + 1)
                    ch.link(nc.vector.tensor_tensor(s[:, t * P:], s[:, t * P:], k.c("chunkdiag"), ALU.add))
            for i in range(2):
                dve.wait_ge(bank_free, 4 + i)
                src, wins = pv[:, i, :], 2 + 2 * i
                have, keep = src, {}
                for n in range(wins):
                    d, dst = 1 << n, s2[:, n % 2, :]
                    nc.vector.tensor_copy(dst[:, 0:d], have[:, 0:d])
                    ch.link(nc.vector.tensor_tensor(dst[:, d:], have[:, d:], have[:, 0:T - d], ALU.add))
                    have = dst
                rc = k.c("rcount", i * T, (i + 1) * T)
                for half in range(2):
                    r = slice(64 * half, 64 * half + 64)
                    ins = nc.vector.tensor_tensor(pp[r, i, :], s2[r, half, :], rc[r], ALU.mult)
                ch.link(ins)
                nc.vector.tensor_tensor(pp[:, i, :], pp[:, i, :], src, ALU.subtract).then_inc(pool_ready, 1)
            for h in range(HF):
                dve.wait_ge(spread, h + 1)
                nc.vector.tensor_copy(k.fb[:, h, :], k.ps[4 + h % 4][:, :]).then_inc(spread_used, 1)
            for i in range(2):
                dve.wait_ge(pool_done, i + 1)
                ch.link(nc.vector.scalar_tensor_tensor(k.y[:, i, :], k.ps[i][:, :], k.p("pscale", i), pg[:, i, :], ALU.mult, ALU.mult))
            tk = Chain(dve, ch_tk)
            dve.wait_ge(pool_ready, 2)
            for r in range(TOPK // 8):
                for t in range(1, NT):
                    ins = nc.vector.max(m8[:, t, :], sc[:, OFF[t]:OFF[t + 1]])
                tk.link(ins)
                for t in range(1, NT):
                    s = sc[:, OFF[t]:OFF[t + 1]]
                    ins = nc.vector.match_replace(s, m8[:, t, :], s, NEG)
                tk.link(ins)
            nc.vector.tensor_copy(k.bias[:, 0:P], k.c("chunkdiag"))
            nc.vector.tensor_scalar(k.bias[:, P:OFF[4]], sc[:, P:OFF[4]], NEG / 2, -BIG, ALU.is_gt, ALU.mult)
    for s in range(4):
        k.loads[s] += NW // 4
    del k.ws[2:]


@phase
def attention(k, tag, weights, y0, fox, ahead):
    nc = k.nc
    sem, sb = k.sem, k.sb
    NP, NI = HF // 2, 2 * NT
    R = 4
    items = [(a, t) for a in range(2) for t in range(NT)]
    q, kk, v, gate = (sb(f"{tag}_{s}", [P, T], F32) for s in ("q", "k", "v", "gate"))
    L = sb(f"{tag}_logits", [P, R, T], F32)
    PT = sb(f"{tag}_probsT", [P, 2, T], F32)
    st = sb(f"{tag}_stats", [P, NI, 4], F32)
    w_high, w_split = sem(f"{tag}_w_high"), sem(f"{tag}_w_split")
    k.ws += [(sb(f"{tag}_w{s}_high", [P, D], F32R), sb(f"{tag}_w{s}_low", [P, D], F32R)) for s in (2, 3)]
    (proj_done, act_prep, st_done, logits_ready, max_ready, exp_done, p_ready, turned, pt_ready, pv_done, y_ready, ch_dve) = (
        sem(f"{tag}_{s}") for s in ("proj_done act_prep st_done logits_ready max_ready exp_done p_ready turned pt_ready pv_done y_ready ch_dve").split())
    b_s, b_t, b_o = k.ps[4:6], k.ps[6], k.ps[7]

    with nc.Block() as block:
        @block.sync
        def _(sp):
            k.first_loads(sp, [weights[s, :, :] for s in range(4)])
            with sp.Fori(1, NP) as i:
                for s in range(4):
                    sp.wait_ge(w_split, 4 * i - 3 + s)
                    k.load(sp, s, weights[bass.ds(4 * i + s, 1), :, :].rearrange("a p d -> p (a d)"))
            sp.wait_ge(w_split, 4 * NP)
            k.load_ahead(sp, ahead)

        @block.tensor
        def _(pe):
            def project(i, s, first=False):
                pe.wait_ge(w_split, 4 * i + s + 1)
                if not first:
                    pe.wait_ge(act_prep, 4 * i - 3 + s)
                ins = k.by_feature(k.ps[s][:, :], s) if s < 3 else k.by_token(k.ps[3], s)
                ins.then_inc(proj_done, 1)

            def score(i, n):
                a, t = items[n]
                if n >= 2:
                    pe.wait_ge(logits_ready, NI * i + n - 1)
                r = slice(DH * a, DH * a + DH)
                nc.tensor.matmul(b_s[n % 2][:, 0:(t + 1) * P], q[r, t * P:(t + 1) * P], kk[r, 0:(t + 1) * P], start=True, stop=True).then_inc(st_done, 1)

            def turn(i, n):
                pe.wait_ge(p_ready, NI * i + n + 1)
                if n:
                    pe.wait_ge(pt_ready, NI * i + n)
                for j in range(items[n][1] + 1):
                    ins = nc.tensor.transpose(b_t[:, j * P:(j + 1) * P], L[:, n % R, j * P:(j + 1) * P], k.c("ident"))
                ins.then_inc(turned, 1)

            def values(i, n):
                a, t = items[n]
                pe.wait_ge(pt_ready, NI * i + n + 1)
                for j in range(t + 1):
                    ins = nc.tensor.matmul(b_o[DH * a:DH * a + DH, t * P:(t + 1) * P], v[:, j * P + DH * a:j * P + DH * a + DH],
                                           PT[:, n % 2, j * P:(j + 1) * P], start=j == 0, stop=j == t)
                ins.then_inc(pv_done, 1)

            def core(i, nxt):
                pe.wait_ge(act_prep, 4 * i + 2)
                score(i, 0)
                score(i, 1)
                if nxt:
                    project(i + 1, 0)
                pe.wait_ge(act_prep, 4 * i + 4)
                score(i, 2)
                for n in range(NI):
                    turn(i, n)
                    if n + 3 < NI:
                        score(i, n + 3)
                    if nxt and n in (1, 3, 5):
                        project(i + 1, 1 + n // 2)
                    if n:
                        values(i, n - 1)
                values(i, NI - 1)

            for s in range(4):
                project(0, s, first=True)
            core(0, True)
            with pe.Fori(1, NP - 1) as i:
                core(i, True)
            core(NP - 1, False)

        @block.scalar
        def _(act):
            def high(i, s):
                act.wait_ge(proj_done, 4 * i + s - 3)
                k.split_high(act, s, i, s, w_high)

            def step(i, nxt):
                for s, x in enumerate((q, kk, gate, v)):
                    act.wait_ge(proj_done, 4 * i + s + 1)
                    nc.scalar.activation(x[:, :], k.ps[s][:, :], ACT.Silu if s == 2 else ACT.Copy).then_inc(act_prep, 1)

                if nxt:
                    high(i + 1, 0)

                def turn(n):
                    t = items[n][1]
                    act.wait_ge(turned, NI * i + n + 1)
                    if n >= 2:
                        act.wait_ge(pv_done, NI * i + n - 1)
                    nc.scalar.activation(PT[:, n % 2, 0:(t + 1) * P], b_t[:, 0:(t + 1) * P], ACT.Copy).then_inc(pt_ready, 1)
                for n, (a, t) in enumerate(items):
                    act.wait_ge(max_ready, NI * i + n + 1)
                    l = L[:, n % R, 0:(t + 1) * P]
                    nc.scalar.activation(l, l, ACT.Exp, bias=st[:, n, 0:1], accum_out=st[:, n, 1:2]).then_inc(exp_done, 1)
                    if nxt and n in (0, 2, 4):
                        high(i + 1, 1 + n // 2)
                    if n >= 2:
                        turn(n - 2)
                turn(NI - 2)
                turn(NI - 1)
                act.wait_ge(y_ready, i + 1)

            for s in range(4):
                k.split_high(act, s, 0, s, w_high)
            with act.Fori(0, NP - 1) as i:
                step(i, True)
            step(NP - 1, False)

        @block.gpsimd
        def _(pool):
            for s in range(4):
                k.split_low(pool, s, s, s, w_high, w_split)
            with pool.Fori(1, NP) as i:
                for s in range(4):
                    k.split_low(pool, s, 4 * i + s, s, w_high, w_split)

        @block.vector
        def _(dve):
            ch = Chain(dve, ch_dve)

            def step(i):
                def normalize(n):
                    l = L[:, n % R, 0:(items[n][1] + 1) * P]
                    dve.wait_ge(exp_done, NI * i + n + 1)
                    ch.link(nc.vector.reciprocal(st[:, n, 2:3], st[:, n, 1:2]))
                    nc.vector.tensor_scalar(l, l, st[:, n, 2:3], None, ALU.mult).then_inc(p_ready, 1)
                for n, (a, t) in enumerate(items):
                    w = (t + 1) * P
                    dve.wait_ge(st_done, NI * i + n + 1)
                    if n >= R:
                        dve.wait_ge(turned, NI * i + n + 1 - R)
                    l = L[:, n % R, 0:w]
                    if fox:
                        b = k.fb[:, bass.ds(2 * i + a, 1), 0:w]
                        one = lambda x: x.rearrange("p (a t) -> p a t", a=1)
                        nc.vector.scalar_tensor_tensor(one(l), one(b_s[n % 2][:, 0:w]), DH ** -0.5, b, ALU.mult, ALU.add).then_inc(logits_ready, 1)
                        dve.wait_ge(logits_ready, NI * i + n + 1)
                        ch.link(nc.vector.tensor_tensor(l[:, w - P:w], l[:, w - P:w], k.c("causal"), ALU.add))
                    else:
                        nc.vector.scalar_tensor_tensor(l, b_s[n % 2][:, 0:w], DH ** -0.5, k.bias[:, OFF[t]:OFF[t + 1]], ALU.mult, ALU.add).then_inc(logits_ready, 1)
                        dve.wait_ge(logits_ready, NI * i + n + 1)
                    nc.vector.tensor_reduce(st[:, n, 0:1], l, AX, ALU.max, negate=True).then_inc(max_ready, 1)
                    if n:
                        normalize(n - 1)
                normalize(NI - 1)
                dve.wait_ge(pv_done, NI * i + NI)
                nc.vector.tensor_tensor(k.y[:, bass.ds(i + y0, 1), :], gate[:, :].rearrange("p (a t) -> p a t", a=1),
                                        b_o[:, :].rearrange("p (a t) -> p a t", a=1), ALU.mult).then_inc(y_ready, 1)
                dve.wait_ge(y_ready, i + 1)

            with dve.Fori(0, NP) as i:
                ch.loop(2 * NI if fox else NI, i)
                step(i)
            ch.end(NP)
    for s in range(4):
        k.loads[s] += NP
    del k.ws[2:]


def program(nc, a):
    k = Core(nc, a)
    gains = lambda layer, i: lambda m: k.p("gains", (4 * layer + i) * KD + m)
    tiles4 = lambda w: [w[s, :, :] for s in range(4)]
    rows2 = lambda w: [w[s * P:(s + 1) * P, :] for s in range(2)]
    load_inputs(k, a["ab_gate"][0, :, :])
    lower_bounds(k)
    norm_in(k, "in0", gains(0, 0))
    with ExitStack() as s:
        k.bcg = s.enter_context(nc.sbuf_tensor("delta_bc", [P, 2, HA, T], F32))
        k.cols = s.enter_context(nc.sbuf_tensor("gate_cols", [P, 6, HA, NT], F32))
        with nc.sbuf_tensor("mlstm_bc", [P, 2, HA, T], F32) as k.bcm:
            ab_gates(k, tiles4(a["m_in"])[:3])
            mlstm(k, a["m_in"], tiles4(a["g_in"]))
        delta(k, a["g_in"], rows2(a["ab_out"]))
    out_proj(k, "ab", k.y, KD, a["ab_out"], gains(0, 1), gains(0, 2), tiles4(a["ffn_up"][0]))
    ffn(k, "0", 0, gains(1, 0), tiles4(a["c_in"]))
    k.clear_semaphores()
    hgrn2(k, a["c_in"], rows2(a["c_out"]))
    out_proj(k, "c", k.y, KD, a["c_out"], gains(1, 1), gains(1, 2), tiles4(a["ffn_up"][1]))
    ffn(k, "1", 1, lambda m: k.p("norm2", m), tiles4(a["shared_in"]))
    with ExitStack() as s:
        k.fb = s.enter_context(nc.sbuf_tensor("forget_bc", [P, HF, T], F32))
        k.bias = s.enter_context(nc.sbuf_tensor("choice_bias", [P, OFF[4]], F32))
        shared_inputs(k, a["shared_in"], a["pool_w"], tiles4(a["fox_in"]))
        attention(k, "fox", a["fox_in"], 5, True, tiles4(a["dsa_in"]))
        attention(k, "dsa", a["dsa_in"], 2, False, rows2(a["out2"]))
    out_proj(k, "two", k.y, KD, a["out2"], None, lambda m: k.p("final2", m), None)


def constants():
    i = np.arange(P)
    s, l = i[:, None], i[None, :]
    parts = {
        "ident": s == l,
        "ones": np.ones((P, P)),
        "upper": s <= l,
        "causal": np.where(l <= s, 0.0, -BIG),
        "chunkdiag": np.where(l < (s // 64 + 1) * 64, 0.0, -BIG),
        "levels": np.concatenate([(s // (2 * b) == l // (2 * b)) & (s // b % 2 == 0) & (l // b % 2 == 1) for b in LEVELS], 1),
        "sel": np.repeat(s == np.arange(6)[None, :], P, 1),
        "reset": np.broadcast_to((np.arange(T) % P != 0).astype(np.float32), (P, T)),
        "rcount": np.concatenate([1.0 / np.minimum(np.arange(T)[None, :] + 1, np.where(i < 64, a, b)[:, None]) for a, b in ((2, 4), (8, 16))], 1),
    }
    return np.concatenate([np.asarray(parts[n], np.float32) for n, _ in _CST], 1)


def columns(d):
    def fold(v):
        v = v.reshape(-1, P)
        return v.T

    def head_rows(v):
        out = np.zeros((P, v.shape[1]), np.float32)
        out[:v.shape[0]] = v
        return out
    f = np.concatenate([d["ffn_conv_w"], d["ffn_conv_b"][:, None, :]], 1)
    f = f.reshape(2, 4, 2, KF, P).transpose(4, 0, 3, 2, 1)
    m = d["ab_conv_m"][0].reshape(4, 2, 4, 64).transpose(1, 3, 2, 0).reshape(P, 16)
    g = d["ab_conv_g"][0].reshape(4, 3, 4, P).transpose(3, 2, 1, 0)
    parts = {
        "gains": fold(d["norm_gains"]), "norm2": fold(d["norm_g_2"]), "final2": fold(d["final_g_2"]),
        "ffn": f.reshape(P, -1), "mconv": m, "gconv": g.reshape(P, -1),
        "mnorm": fold(d["ab_m_norm"]), "gnorm": fold(d["ab_g_norm"]), "cnorm": fold(d["c_norm"]),
        "lb": fold(d["c_lb_logits"]), "pscale": fold(d["pool_scale_2"]),
        "gbias": head_rows(d["ab_m_gate_bias"][0].T),
        "adt": head_rows(np.stack([d["ab_g_a_log"][0], d["ab_g_dt_bias"][0]], 1)),
        "foxb": head_rows(d["fox_bf_2"][0][:, None]),
    }
    return np.concatenate([parts[n] for n, _ in _COLS], 1)


def tiles(w):
    return w.reshape(KD, P, -1, P).transpose(2, 1, 0, 3).reshape(-1, P, D)


def layout_ffn(d):
    up = np.stack([tiles(w.reshape(D, 2, KF, P).transpose(0, 2, 1, 3).reshape(D, 2 * FF)) for w in d["ffn_w_up"]])
    return {"x": d["x"][0].T, "cst": constants(), "col": columns(d), "ffn_up": up, "ffn_down": d["ffn_w_down"]}


def layout_c(d):
    w = d["c_w_in"][0].reshape(D, 4, HC, P)[:, [0, 1, 3, 2]].transpose(0, 2, 1, 3).reshape(D, 4 * HC * P)
    return {"c_in": tiles(w), "c_out": d["c_w_out"][0]}


def layout_ab(d):
    w = d["ab_w_in"][0]
    cut = lambda lo, n: w[:, lo:lo + n]
    gate = np.zeros((D, P), np.float32)
    for i, lo in enumerate((1536, 1540, 3592, 3596)):
        gate[:, 32 * i:32 * i + 4] = cut(lo, 4)
    m = []
    for h in range(4):
        m += [cut(64 * h, 64), cut(256 + 64 * h, 64), cut(1024 + P * h, P), cut(512 + P * h, P)]
    g = []
    for h in range(4):
        g += [cut(1544 + 512 * i + P * h, P) for i in (0, 1, 2, 3)]
    return {"ab_gate": tiles(gate), "m_in": tiles(np.concatenate(m, 1)), "g_in": tiles(np.concatenate(g, 1)), "ab_out": d["ab_w_out"][0]}


def layout_2(d):
    w = d["w_in_2"][0]
    names = ("pv", 256), ("pg", 256), ("dq", 384), ("dk", 384), ("dv", 384), ("dg", 384), ("iq", 256), ("ik", 32), ("iw", 8), ("fq", 384), ("fk", 384), ("fv", 384), ("fg", 384), ("ff", 6)
    part, at = {}, 0
    for n, m in names:
        part[n] = w[:, at:at + m]
        at += m
    gate = np.zeros((D, P), np.float32)
    gate[:, 0:6], gate[:, 32:40] = part["ff"], part["iw"]
    shared = tiles(np.concatenate([gate] + [part["ik"]] * 4 + [part["iq"], part["pv"], part["pg"]], 1))
    pairs = lambda names: tiles(np.concatenate([part[n][:, P * i:P * i + P] for i in range(3) for n in names], 1))
    pw = np.zeros((P, 2, P), np.float32)
    for g in range(4):
        o = 64 * (g % 2)
        pw[o:o + 64, g // 2, o:o + 64] = d["pool_w_2"][0, g]
    return {"shared_in": shared, "pool_w": pw, "dsa_in": pairs(("dq", "dk", "dg", "dv")), "fox_in": pairs(("fq", "fk", "fg", "fv")), "out2": d["w_out_2"][0]}


def layout(d):
    return {**layout_ffn(d), **layout_ab(d), **layout_c(d), **layout_2(d)}


def kernel(**inputs):
    import concourse.bacc as _bacc
    from concourse.bass_utils import run_bass_kernel_spmd as _run

    d = {n: np.asarray(v) for n, v in inputs.items()}
    arrays = {n: np.ascontiguousarray(v) for n, v in layout(d).items()}
    nc = _bacc.Bacc("TRN2", target_bir_lowering=False, num_devices=1)
    aps = {n: nc.dram_tensor(n, v.shape, mybir.dt.from_np(v.dtype), kind="ExternalInput").ap() for n, v in arrays.items()}
    aps["out"] = nc.dram_tensor("out", (D, T), F32, kind="ExternalOutput").ap()
    program(nc, aps)
    r = _run(nc, [arrays], core_ids=[0])
    return r.results[0]["out"].T[None]
```

```python
from contextlib import ExitStack

import numpy as np
import concourse.bass as bass
from concourse import mybir
from concourse.alu_op_type import AluOpType as ALU

F32 = mybir.dt.float32
F32R = mybir.dt.float32r
U32 = mybir.dt.uint32
ACT = mybir.ActivationFunctionType
AX = mybir.AxisListType.X

P = 128
T = 512
NT = T // P
D = 1024
KD = D // P
FF = 2816
KF = FF // P
EPS = 1e-6
BIG = 1e30

LEVELS = [1 << n for n in range(7)]
_CST = [("ident", P), ("ones", P), ("upper", P), ("causal", P), ("chunkdiag", P), ("levels", P * len(LEVELS)),
        ("reset", T), ("rcount", 2 * T), ("sel", 6 * P)]
CST = {}
_at = 0
for _n, _w in _CST:
    CST[_n] = (_at, _w)
    _at += _w
NCST = _at

_COLS = [("gains", 8 * KD), ("norm2", KD), ("final2", KD), ("ffn", 2 * 2 * KF * 4), ("mconv", 4 * 4), ("gconv", 4 * 3 * 4),
         ("mnorm", 4), ("gnorm", 4), ("cnorm", 8), ("lb", 2 * 8), ("pscale", 2), ("gbias", 2), ("adt", 2), ("foxb", 1)]
COL = {}
_at = 0
for _n, _w in _COLS:
    COL[_n] = (_at, _w)
    _at += _w
NCOL = _at


LNEXP = "natural_log_exp_and_others"


class Chain:

    def __init__(self, eng, sem):
        self.eng, self.sem, self.base, self.n = eng, sem, 0, 0

    def link(self, ins):
        self.n += 1
        ins.then_inc(self.sem, 1)
        self.eng.wait_ge(self.sem, self.base + self.n)

    def loop(self, per_step, i):
        self.base, self.enter, self.n = self.base + self.n + i * per_step, (self.base + self.n, per_step), 0

    def end(self, steps):
        before, per_step = self.enter
        assert self.n == per_step, (self.n, per_step)
        self.base, self.n = before + per_step * steps, 0


def phase(f):
    def run(k, *args):
        with ExitStack() as k.stack:
            f(k, *args)
    return run


class Core:

    def __init__(self, nc, a):
        self.nc, self.a, self.sems = nc, a, []
        sb = nc.alloc_sbuf_tensor
        self.x = sb("x_res", [P, KD, T], F32)
        self.uh = sb("u_high", [P, KD, T], F32R)
        self.ul = sb("u_low", [P, KD, T], F32R)
        self.ws = [(sb(f"w{s}_high", [P, D], F32R), sb(f"w{s}_low", [P, D], F32R)) for s in range(4)]
        self.y = sb("y_mix", [P, KD, T], F32)
        self.w = sb("w_ring", [P, 4, D], F32)
        self.sq = sb("sq", [P, 2, T], F32)
        self.rstd = sb("rstd", [P, T], F32)
        self.cst = sb("cst_sb", [P, NCST], F32)
        self.col = sb("col_sb", [P, NCOL], F32)
        self.epsc = sb("eps_col", [P, 1], F32)
        self.lb = sb("lb_cols", [P, 2, KD], F32)
        self.w_loaded = [nc.alloc_semaphore(f"w_loaded{s}") for s in range(4)]
        self.w_high, self.w_split, self.proj_done = (nc.alloc_semaphore(s) for s in ("w_high", "w_split", "proj_done"))
        self.loads = [0] * 4
        self.base = self.products = 0
        self.ahead = self.split = self.projected = 0
        self.gain = None
        self.ps = [nc.alloc_psum_tensor(f"bank{i}", [P, T], F32) for i in range(8)]

    def sb(self, name, shape, dtype=F32):
        return self.stack.enter_context(self.nc.sbuf_tensor(name, shape, dtype))

    def sem(self, name):
        self.sems.append(self.nc.alloc_semaphore(name))
        return self.sems[-1]

    def load(self, sp, s, tile):
        sp.dma_start(self.w[:, s, :], tile).then_inc(self.w_loaded[s], 16)

    def load_ahead(self, sp, tiles, first=0, upto=0):
        for s, tile in enumerate(tiles):
            if s >= 4:
                self.wait_split(sp, upto + s - 4)
            self.load(sp, (first + s) % 4, tile)
        self.ahead = len(tiles)

    def first_loads(self, sp, tiles, first=0):
        for s in range(self.ahead, len(tiles)):
            self.load(sp, first + s, tiles[s])
        more, self.ahead = max(self.ahead - 4, 0), 0
        return more

    def loaded(self, s, i):
        return 16 * (self.loads[s] + i) + 16

    def split_high(self, act, s, i):
        act.wait_ge(self.w_loaded[s], self.loaded(s, i))
        self.nc.scalar.activation(self.ws[s][0][:, :], self.w[:, s, :], ACT.Copy).then_inc(self.w_high, 1)

    def split_low(self, eng, s, n, other=False):
        high, low = self.ws[s]
        if other:
            eng.wait_ge(self.w_split, self.base + n)
        eng.wait_ge(self.w_high, self.base + n + 1)
        eng.tensor_tensor(low[:, :], self.w[:, s, :], high[:, :].bitcast(F32), ALU.subtract).then_inc(self.w_split, 1)

    def wait_split(self, eng, n):
        eng.wait_ge(self.w_split, self.base + n + 1)

    def wait_product(self, eng, n):
        eng.wait_ge(self.proj_done, self.products + n + 1)

    def count(self, slots, split=0, projected=0, uncounted=0):
        for s, n in slots.items():
            self.loads[s] += n
        self.base += sum(slots.values())
        self.products += sum(slots.values()) - uncounted
        self.split, self.projected = split, projected

    def product(self, out, a, b, start=True, stop=True):
        nc = self.nc
        nc.tensor.matmul(out, a[0], b[0], start=start, stop=False)
        nc.tensor.matmul(out, a[0], b[1], start=False, stop=False)
        return nc.tensor.matmul(out, a[1], b[0], start=False, stop=stop)

    def project(self, out, j, ready=None, first=0, last=KD):
        for m in range(first, last):
            if ready:
                ready(m)
            s = slice(m * P, (m + 1) * P)
            ins = self.product(out, [x[:, s] for x in self.ws[j]], [x[:, m, :] for x in (self.uh, self.ul)], m == 0, m == KD - 1)
        return ins

    def turn(self, out, x):
        for c in range(NT):
            s = slice(c * P, (c + 1) * P)
            ins = self.nc.tensor.transpose(out[:, s], x[:, s], self.c("ident"))
        return ins

    def clear_semaphores(self):
        self.nc.clear_and_free_semaphores(self.sems)
        self.nc.all_engine_barrier()
        self.sems = []

    def c(self, name, lo=0, hi=None):
        at, w = CST[name]
        return self.cst[:, at + lo:at + (w if hi is None else hi)]

    def p(self, name, i, n=1):
        at, _ = COL[name]
        return self.col[:, bass.ds(at + i, n)]


class InputNorm:

    def __init__(self, k, tag):
        self.k, self.gain = k, k.gain
        self.rooted, self.normed, self.high, self.even, self.odd, self.ch = (
            k.sem(f"{s}_{tag}") for s in ("rooted", "normed", "u_high", "u_even", "u_odd", "ln_done"))

    def scalar(self, act):
        k, nc = self.k, self.k.nc
        Chain(act, self.ch).link(nc.scalar.activation(k.rstd[:, :], k.ps[1][:, :], ACT.Ln, bias=k.epsc[:, 0:1], scale=1.0 / D))
        nc.scalar.activation(k.rstd[:, :], k.rstd[:, :], ACT.Exp, scale=-0.5).then_inc(self.rooted, 1)
        for m in range(KD):
            act.wait_ge(self.normed, m + 1)
            nc.scalar.activation(k.uh[:, m, :], k.y[:, m, :], ACT.Copy).then_inc(self.high, 1)

    def low(self, eng, m):
        k = self.k
        eng.wait_ge(self.high, m + 1)
        eng.tensor_tensor(k.ul[:, m, :], k.y[:, m, :], k.uh[:, m, :].bitcast(F32), ALU.subtract).then_inc((self.even, self.odd)[m % 2], 1)

    def vector(self, dve):
        k, nc = self.k, self.k.nc
        dve.wait_ge(self.rooted, 1)
        for m in range(KD):
            nc.vector.scalar_tensor_tensor(k.y[:, m, :], k.x[:, m, :], self.gain(m), k.rstd[:, :], ALU.mult, ALU.mult).then_inc(self.normed, 1)
            if m % 2:
                self.low(dve, m - 1)

    def gpsimd(self, pool):
        for m in range(1, KD, 2):
            self.low(pool, m)

    def ready(self, pe):
        return lambda m: pe.wait_ge((self.even, self.odd)[m % 2], m // 2 + 1)


@phase
def load_inputs(k, gain, ahead):
    nc, a = k.nc, k.a
    x_loaded = [k.sem(f"x{i}_loaded") for i in range(4)]
    loaded, ones_loaded, eps_set, squared, summed = k.sem("inputs_loaded"), k.sem("ones_loaded"), k.sem("eps_set"), k.sem("squared_in"), k.sem("summed_in")
    k.gain = gain
    with nc.Block() as block:
        @block.sync
        def _(sp):
            x = a["x"].rearrange("(k p) t -> p k t", p=P)
            for i in range(4):
                sp.dma_start(k.x[:, 2 * i:2 * i + 2, :], x[:, 2 * i:2 * i + 2, :]).then_inc(x_loaded[i], 16)
                if i == 0:
                    sp.dma_start(k.cst[:, :], a["cst"]).then_inc(ones_loaded, 16)
            sp.dma_start(k.col[:, :], a["col"]).then_inc(loaded, 16)
            sp.dma_start(k.w[:, 3, :], ahead).then_inc(k.w_loaded[3], 16)
            sp.wait_ge(loaded, 16)

        @block.vector
        def _(dve):
            nc.vector.memset(k.epsc[:, :], EPS).then_inc(eps_set, 1)
            dve.wait_ge(eps_set, 1)

        @block.scalar
        def _(act):
            nc.scalar.preload_act_table_set(LNEXP)
            for m in range(KD):
                if m % 2 == 0:
                    act.wait_ge(x_loaded[m // 2], 16)
                if m >= 2:
                    act.wait_ge(summed, m - 1)
                nc.scalar.activation(k.sq[:, m % 2, :], k.x[:, m, :], ACT.Square).then_inc(squared, 1)
            k.split_high(act, 3, 0)

        @block.tensor
        def _(pe):
            pe.wait_ge(ones_loaded, 16)
            for m in range(KD):
                pe.wait_ge(squared, m + 1)
                nc.tensor.matmul(k.ps[1][:, :], k.c("ones"), k.sq[:, m % 2, :], start=m == 0, stop=m == KD - 1).then_inc(summed, 1)

        @block.gpsimd
        def _(pool):
            k.split_low(pool, 3, 0)
    k.count({}, split=1)


@phase
def out_proj(k, tag, src, tiles, weights, gain_post, gain_next, ahead):
    nc = k.nc
    final = not ahead
    names = ("src_high", "src_split", "mixed", "moved", "gathered", "squared", "summed", "rooted", "scaled", "added", "pool_added", "squared2",
             "summed2", "rooted2", "ln_done", "normed", "stored")
    src_high, src_split, mixed, moved, gathered, squared, summed, rooted, scaled, added, pool_added, squared2, summed2, rooted2, ln_done, normed, stored = (
        k.sem(f"{s}_{tag}") for s in names)
    pairs = tiles // 2
    mx = k.sb(f"mixed_sb_{tag}", [P, KD, T])
    sp2 = [(k.sb(f"src{s}_high_{tag}", [P, T], F32R), k.sb(f"src{s}_low_{tag}", [P, T], F32R)) for s in range(2)]
    on_pool = (2, 5) if gain_post else ()
    split = k.split

    def tile(n):
        return src[:, bass.ds(n, 1), :].rearrange("p a t -> p (a t)")

    def square(m):
        return k.sq[:, m, :] if m < 2 else mx[:, m, :]

    def wait_added(eng, m):
        if m in on_pool:
            eng.wait_ge(pool_added, on_pool.index(m) + 1)
        else:
            eng.wait_ge(added, m + 1 - sum(p < m for p in on_pool))

    with nc.Block() as block:
        @block.sync
        def _(sp):
            k.first_loads(sp, [weights[s * P:(s + 1) * P, :] for s in range(2)], 2)
            if ahead:
                k.load_ahead(sp, ahead[:2])
            with sp.Fori(1, pairs) as i:
                for s in range(2):
                    k.wait_split(sp, 2 * i - 2 + s)
                    k.load(sp, 2 + s, weights[bass.ds((2 * i + s) * P, P), :])
            if ahead:
                k.wait_split(sp, tiles - 1)
                k.load_ahead(sp, ahead[2:], 2)
                k.ahead = 4
            else:
                for m in range(KD):
                    sp.wait_ge(normed, m + 1)
                    sp.dma_start(k.a["out"][m * P:(m + 1) * P, :], mx[:, m, :]).then_inc(stored, 16)
                sp.wait_ge(stored, 16 * KD)

        @block.tensor
        def _(pe):
            def step(i, s, start, stop):
                k.wait_split(pe, 2 * i + s)
                pe.wait_ge(src_split, 2 * i + s + 1)
                for m in range(KD):
                    ins = k.product(k.ps[m][:, :], [x[:, m * P:(m + 1) * P] for x in k.ws[2 + s]], [x[:, :] for x in sp2[s]], start, stop)
                    if stop:
                        ins.then_inc(mixed, 1)
                if not stop:
                    ins.then_inc(k.proj_done, 1)
            step(0, 0, True, False)
            step(0, 1, False, False)
            with pe.Fori(1, pairs - 1) as i:
                step(i, 0, False, False)
                step(i, 1, False, False)
            step(pairs - 1, 0, False, False)
            step(pairs - 1, 1, False, True)
            if gain_post:
                pe.wait_ge(gathered, KD - 1)
                nc.tensor.matmul(k.ps[0][:, :], k.c("ones"), k.rstd[:, :], start=True, stop=True).then_inc(summed, 1)
            else:
                pe.wait_ge(added, 2)
            for m in range(KD):
                pe.wait_ge(squared2, m + 1)
                nc.tensor.matmul(k.ps[1][:, :], k.c("ones"), k.sq[:, m % 2, :], start=m == 0, stop=m == KD - 1).then_inc(summed2, 1)

        @block.scalar
        def _(act):
            ch = Chain(act, ln_done)

            def src_step(n, s):
                nc.scalar.activation(sp2[s][0][:, :], tile(n), ACT.Copy).then_inc(src_high, 1)

            def step(i, s):
                k.wait_product(act, 2 * i + s - 2)
                k.split_high(act, 2 + s, i)
                src_step(2 * i + s, s)

            def root(bank, done):
                ch.link(nc.scalar.activation(k.rstd[:, :], bank[:, :], ACT.Ln, bias=k.epsc[:, 0:1], scale=1.0 / D))
                nc.scalar.activation(k.rstd[:, :], k.rstd[:, :], ACT.Exp, scale=-0.5).then_inc(done, 1)

            for s in range(2):
                if s >= split:
                    k.split_high(act, 2 + s, 0)
                src_step(s, s)
            nc.scalar.preload_act_table_set(LNEXP)
            with act.Fori(1, pairs) as i:
                step(i, 0)
                step(i, 1)
            if not final:
                for s in range(2):
                    k.split_high(act, s, 0)
            if gain_post:
                for m in range(KD):
                    act.wait_ge(*((moved, m + 1) if m < 2 else (mixed, m + 1)))
                    nc.scalar.activation(square(m), (mx[:, m, :] if m < 2 else k.ps[m][:, :]), ACT.Square).then_inc(squared, 1)
                act.wait_ge(summed, 1)
                root(k.ps[0], rooted)
            for m in range(KD):
                wait_added(act, m)
                if m >= 2:
                    act.wait_ge(summed2, m - 1)
                nc.scalar.activation(k.sq[:, m % 2, :], k.x[:, m, :], ACT.Square).then_inc(squared2, 1)
            if final:
                act.wait_ge(summed2, KD)
                root(k.ps[1], rooted2)

        @block.vector
        def _(dve):
            def src_step(n, s):
                dve.wait_ge(src_high, n + 1)
                high_, low = sp2[s]
                one = lambda x: x.rearrange("p (a t) -> p a t", a=1)
                nc.vector.tensor_tensor(one(low[:, :]), src[:, bass.ds(n, 1), :], one(high_[:, :]).bitcast(F32), ALU.subtract).then_inc(src_split, 1)

            for s in range(2):
                if s >= split:
                    k.split_low(dve, 2 + s, s)
                src_step(s, s)
            with dve.Fori(1, pairs) as i:
                for s in range(2):
                    k.split_low(dve, 2 + s, 2 * i + s)
                    src_step(2 * i + s, s)

            def add(m):
                if gain_post:
                    dve.wait_ge(scaled, m + 1)
                else:
                    dve.wait_ge(mixed, m + 1)
                nc.vector.tensor_tensor(k.x[:, m, :], k.x[:, m, :], mx[:, m, :] if gain_post else k.ps[m][:, :], ALU.add).then_inc(added, 1)

            if gain_post:
                for m in range(2):
                    dve.wait_ge(mixed, m + 1)
                    nc.vector.tensor_copy(mx[:, m, :], k.ps[m][:, :]).then_inc(moved, 1)
                dve.wait_ge(moved, 2)
                for m in range(1, KD):
                    dve.wait_ge(squared, m + 1)
                    if m > 1:
                        dve.wait_ge(gathered, m - 1)
                    nc.vector.tensor_tensor(k.rstd[:, :], square(0) if m == 1 else k.rstd[:, :], square(m), ALU.add).then_inc(gathered, 1)
                dve.wait_ge(rooted, 1)
                for m in range(KD):
                    nc.vector.scalar_tensor_tensor(mx[:, m, :], mx[:, m, :] if m < 2 else k.ps[m][:, :], gain_post(m), k.rstd[:, :], ALU.mult, ALU.mult).then_inc(scaled, 1)
                    if m and m - 1 not in on_pool:
                        add(m - 1)
                add(KD - 1)
            else:
                for m in range(KD):
                    add(m)
            if final:
                dve.wait_ge(added, KD)
                dve.wait_ge(rooted2, 1)
                for m in range(KD):
                    nc.vector.scalar_tensor_tensor(mx[:, m, :], k.x[:, m, :], gain_next(m), k.rstd[:, :], ALU.mult, ALU.mult).then_inc(normed, 1)

        if not final:
            @block.gpsimd
            def _(pool):
                for s in range(2):
                    k.split_low(pool, s, tiles + s, other=s == 0)
                for m in on_pool:
                    pool.wait_ge(scaled, m + 1)
                    nc.gpsimd.tensor_tensor(k.x[:, m, :], k.x[:, m, :], mx[:, m, :], ALU.add).then_inc(pool_added, 1)
    k.count({2: pairs, 3: pairs}, split=2, uncounted=1)
    k.gain = gain_next


@phase
def ffn_up(k, tag, layer, weights, h, ahead):
    nc, sem = k.nc, k.sem
    tap_done, conv_done, silu_done, mul_done, chained = (sem(f"{s}_{tag}") for s in (
        "tap_done", "conv_done", "silu_done", "mul_done", "chained"))
    cg = k.sb(f"conv_{tag}", [P, 4, T])
    n = KF // 2
    norm = InputNorm(k, tag)

    def coef(tile, j):
        return k.p("ffn", (layer * 2 * KF + tile) * 4 + j)

    with nc.Block() as block:
        @block.sync
        def _(sp):
            k.first_loads(sp, [weights[s, :, :] for s in range(4)])
            with sp.Fori(1, n) as i:
                for s in range(4):
                    k.wait_split(sp, 4 * i - 4 + s)
                    k.load(sp, s, weights[bass.ds(4 * i + s, 1), :, :].rearrange("a p d -> p (a d)"))
            k.wait_split(sp, 4 * n - 1)
            k.load_ahead(sp, ahead, 2)

        @block.tensor
        def _(pe):
            def step(i, first):
                for s in range(4):
                    k.wait_split(pe, 4 * i + s)
                    if not first:
                        pe.wait_ge(conv_done, 4 * i - 3 + s)
                    k.project(k.ps[s][:, :], s, norm.ready(pe) if first and s == 0 else None).then_inc(k.proj_done, 1)
            step(0, True)
            with pe.Fori(1, n) as i:
                step(i, False)

        @block.scalar
        def _(act):
            def high(i, s, first):
                if not first:
                    k.wait_product(act, 4 * i + s - 4)
                k.split_high(act, s, i)

            def step(i, first, last):
                for s in range(4):
                    if s < 2:
                        high(i, s + 2, first)
                    elif not last:
                        high(i + 1, s - 2, False)
                    elif s == 3:
                        k.wait_product(act, 4 * n - 2)
                        k.split_high(act, 2, n)
                    k.wait_product(act, 4 * i + s)
                    if not first:
                        act.wait_ge(mul_done, 2 * i - 1 + s // 2)
                    nc.scalar.activation(cg[:, s, :], k.ps[s][:, :], ACT.Identity, bias=coef(4 * i + s, 3), scale=coef(4 * i + s, 2)).then_inc(tap_done, 1)
                    if s % 2:
                        act.wait_ge(conv_done, 4 * i + s)
                        nc.scalar.activation(cg[:, s - 1, :], cg[:, s - 1, :], ACT.Silu).then_inc(silu_done, 1)
            norm.scalar(act)
            step(0, True, False)
            with act.Fori(1, n - 1) as i:
                step(i, False, False)
            step(n - 1, False, True)

        @block.vector
        def _(dve):
            ch = Chain(dve, chained)

            def step(i, last):
                for s in range(4):
                    if not last or s < 2:
                        k.split_low(dve, (s + 2) % 4, 4 * i + s + 2)
                    elif s == 3:
                        k.split_low(dve, 2, 4 * n)
                    dve.wait_ge(tap_done, 4 * i + s + 1)
                    ch.link(nc.vector.scalar_tensor_tensor(cg[:, s, 1:T], k.ps[s][:, 0:T - 1], coef(4 * i + s, 1), cg[:, s, 1:T], ALU.mult, ALU.add))
                    nc.vector.scalar_tensor_tensor(cg[:, s, 2:T], k.ps[s][:, 0:T - 2], coef(4 * i + s, 0), cg[:, s, 2:T], ALU.mult, ALU.add).then_inc(conv_done, 1)

            norm.vector(dve)
            with dve.Fori(0, n - 1) as i:
                ch.loop(4, i)
                step(i, False)
            ch.end(n - 1)
            step(n - 1, True)

        @block.gpsimd
        def _(pool):
            norm.gpsimd(pool)
            with pool.Fori(0, n) as i:
                for s in (1, 3):
                    pool.wait_ge(conv_done, 4 * i + s + 1)
                    pool.wait_ge(silu_done, 2 * i + (s + 1) // 2)
                    nc.gpsimd.tensor_tensor(h[:, bass.ds(2 * i + s // 2, 1), :], cg[:, s - 1:s, :], cg[:, s:s + 1, :], ALU.mult).then_inc(mul_done, 1)
    k.count({s: n for s in range(4)}, split=1)


def ffn(k, tag, layer, gain_next, ahead):
    down = k.a["ffn_down"][layer]
    with k.nc.sbuf_tensor(f"hidden{tag}", [P, KF, T], F32) as hidden:
        ffn_up(k, f"up{tag}", layer, k.a["ffn_up"][layer], hidden, [down[s * P:(s + 1) * P, :] for s in range(2)])
        out_proj(k, f"down{tag}", hidden, KF, down, lambda m: k.p("gains", (4 * layer + 3) * KD + m), gain_next, ahead)


HC = 8


@phase
def lower_bounds(k):
    nc = k.nc
    t = k.sb("lb_tmp", [P, 5, HC], F32)
    maxed, powered, bounded = (k.sem(s) for s in ("lb_maxed", "lb_powered", "lb_bounded"))
    l0, l1 = k.p("lb", 0, HC), k.p("lb", HC, HC)
    with nc.Block() as block:
        @block.vector
        def _(dve):
            ch = Chain(dve, maxed)
            ch.link(nc.vector.tensor_tensor(t[:, 0, :], l0, l1, ALU.max))
            nc.vector.tensor_tensor(t[:, 1, :], l0, t[:, 0, :], ALU.subtract)
            ch.link(nc.vector.tensor_tensor(t[:, 2, :], l1, t[:, 0, :], ALU.subtract))
            dve.wait_ge(powered, 1)
            ch2 = Chain(dve, bounded)
            ch2.link(nc.vector.tensor_tensor(t[:, 0, :], t[:, 1, :], t[:, 2, :], ALU.add))
            ch2.link(nc.vector.reciprocal(t[:, 3, :], t[:, 0, :]))
            ch2.link(nc.vector.tensor_tensor(t[:, 1:3, :], t[:, 1:3, :], t[:, 3:4, :].to_broadcast([P, 2, HC]), ALU.mult))
            ch2.link(nc.vector.tensor_tensor(t[:, 4, :], t[:, 1, :], t[:, 2, :], ALU.add))
            ch2.link(nc.vector.tensor_tensor(k.lb[:, 0, :], t[:, 4, :], t[:, 1, :], ALU.subtract))
            ch2.link(nc.vector.tensor_scalar(k.lb[:, 1, :], k.lb[:, 0, :], -1.0, 1.0, ALU.mult, ALU.add))

        @block.scalar
        def _(act):
            act.wait_ge(maxed, 2)
            nc.scalar.activation(t[:, 1:3, :], t[:, 1:3, :], ACT.Exp).then_inc(powered, 1)


@phase
def hgrn2(k, weights, ahead):
    nc = k.nc
    sem = k.sem
    sb = k.sb
    H = HC
    scale = P ** -0.5
    q, kk, v, gate = (sb(f"c_{s}", [P, T], F32) for s in ("q", "k", "v", "gate"))
    vraw = sb("c_v_raw", [P, T], F32)
    fbuf, ef, sig, logf, G, E, kdf, qd, kd, kdt, at, osb = (
        sb(f"c_{s}", [P, T], F32) for s in ("f", "ef", "sig", "logf", "G", "E", "kdf", "qd", "kd", "kdt", "attn", "o"))
    dif = sb("c_dif", [P, 4, T], F32)
    tick = sb("c_tick", [P, 4], F32)
    X = sb("c_X", [P, 4, T], F32)
    S = sb("c_S", [P, NT - 1, P], F32)
    b_f, b_q, b_g, b_v, b_x0, b_x1, b_kv, b_o = k.ps
    b_x = [b_x0, b_x1]
    norm_in = InputNorm(k, "c_in")
    R = 4
    raw_ready, v_turned = sem("c_raw_ready"), sem("c_v_turned")
    (f_clamped, act_prep, sig_ready, ft_ready, logf_ready, g_ready, e_ready, kd_ready, tr_done, kdt_ready, kv_done,
     s_ready, diff_ready, lexp_ready, x_ready, lv_done, at_done, o_done, osb_ready, osq_ready, nrm_done, rs_ready, y_ready,
     ch_act, ch_dve) = (sem("c_" + s) for s in (
         "f_clamped act_prep sig_ready ft_ready logf_ready g_ready e_ready kd_ready tr_done kdt_ready kv_done "
         "s_ready diff_ready lexp_ready x_ready lv_done at_done o_done osb_ready osq_ready nrm_done rs_ready y_ready "
         "ch_act ch_dve").split())
    NL = len(LEVELS)

    def chunks(x):
        return x[:, :].rearrange("p (c l) -> p c l", l=P)

    def mask(name, lo):
        return k.c(name, lo, lo + P).rearrange("p (a l) -> p a l", a=1).to_broadcast([P, NT, P])

    def blocks(x, b):
        return x.rearrange("p (n e b) -> p n e b", e=2, b=b)

    with nc.Block() as block:
        @block.sync
        def _(sp):
            k.first_loads(sp, [weights[s, :, :] for s in range(4)])
            with sp.Fori(1, H) as h:
                for s in range(4):
                    k.wait_split(sp, 4 * h - 4 + s)
                    k.load(sp, s, weights[bass.ds(4 * h + s, 1), :, :].rearrange("a p d -> p (a d)"))
            k.wait_split(sp, 4 * H - 1)
            k.load_ahead(sp, ahead, 2)

        @block.tensor
        def _(pe):
            def project(h, s, first=0, last=KD):
                if first == 0:
                    k.wait_split(pe, 4 * h + s)
                    if not (isinstance(h, int) and h == 0):
                        if s == 0:
                            pe.wait_ge(f_clamped, h)
                        else:
                            pe.wait_ge(act_prep, 3 * h - 3 + s)
                ins = k.project(k.ps[s][:, :], s, norm_in.ready(pe) if isinstance(h, int) and h + s == 0 else None, first, last)
                if last == KD:
                    ins.then_inc(k.proj_done, 1)

            def level(h, l):
                pe.wait_ge(x_ready, NL * h + l + 1)
                if l >= 1:
                    pe.wait_ge(at_done, 8 * h + l)
                for c in range(NT):
                    xc = X[:, l % R, c * P:(c + 1) * P]
                    ins = nc.tensor.matmul(b_x[(l + 1) % 2][:, c * P:(c + 1) * P], xc, xc, start=True, stop=True)
                ins.then_inc(lv_done, 1)

            def core(h, nxt, first):
                if nxt:
                    project(h + 1, 0)
                pe.wait_ge(raw_ready, h + 1)
                k.turn(b_v, vraw).then_inc(v_turned, 1)
                if nxt:
                    project(h + 1, 1)
                pe.wait_ge(sig_ready, h + 1)
                pe.wait_ge(g_ready, h + 1)
                if not first:
                    pe.wait_ge(rs_ready, h)
                for c in range(NT):
                    ins = nc.tensor.matmul(b_x0[:, c * P:(c + 1) * P], kk[:, c * P:(c + 1) * P], q[:, c * P:(c + 1) * P], start=True, stop=True)
                ins.then_inc(lv_done, 1)
                if nxt:
                    project(h + 1, 2, 0, 3)
                for l in range(NL):
                    level(h, l)
                    if nxt and l < 5:
                        project(h + 1, 2, 3 + l, 4 + l)
                    elif nxt:
                        project(h + 1, 3, l - 5, l - 4)
                pe.wait_ge(kd_ready, h + 1)
                for c in range(NT - 1):
                    ins = nc.tensor.transpose(b_kv[:, c * P:(c + 1) * P], kd[:, c * P:(c + 1) * P], k.c("ident"))
                ins.then_inc(tr_done, 1)
                if nxt:
                    project(h + 1, 3, 2, 3)
                pe.wait_ge(kdt_ready, h + 1)
                pe.wait_ge(act_prep, 3 * h + 3)
                for c in range(NT - 1):
                    ins = nc.tensor.matmul(b_kv[:, c * P:(c + 1) * P], kdt[:, c * P:(c + 1) * P], v[:, c * P:(c + 1) * P], start=True, stop=True)
                ins.then_inc(kv_done, 1)
                if nxt:
                    project(h + 1, 3, 3, 4)
                pe.wait_ge(at_done, 8 * h + 8)
                for c in range(NT):
                    s = slice(c * P, (c + 1) * P)
                    ins = nc.tensor.matmul(b_o[:, s], v[:, s], at[:, s], start=True, stop=c == 0)
                    if c:
                        if c == 1:
                            pe.wait_ge(s_ready, h + 1)
                        ins = nc.tensor.matmul(b_o[:, s], S[:, c - 1, :], qd[:, s], start=False, stop=True)
                ins.then_inc(o_done, 1)
                if nxt:
                    project(h + 1, 3, 4, 7)
                pe.wait_ge(osq_ready, h + 1)
                nc.tensor.matmul(b_x0[:, :], k.c("ones"), k.sq[:, 0, :], start=True, stop=True).then_inc(nrm_done, 1)
                if nxt:
                    project(h + 1, 3, 7)

            for s in range(4):
                project(0, s)
            core(0, True, True)
            with pe.Fori(1, H - 1) as h:
                core(h, True, False)
            core(H - 1, False, False)

        @block.scalar
        def _(act):
            ch = Chain(act, ch_act)

            def high(h, s):
                k.wait_product(act, 4 * h + s - 4)
                k.split_high(act, s, h)

            def early(h):
                act.wait_ge(f_clamped, h + 1)
                ch.link(nc.scalar.activation(ef[:, :], fbuf[:, :], ACT.Exp, scale=-1.0))
                ch.link(nc.scalar.activation(sig[:, :], ef[:, :], ACT.Ln, bias=1.0))
                nc.scalar.activation(sig[:, :], sig[:, :], ACT.Exp, scale=-1.0).then_inc(sig_ready, 1)
                k.wait_product(act, 4 * h + 3)
                nc.scalar.activation(vraw[:, :], b_v[:, :], ACT.Copy).then_inc(raw_ready, 1)

            def step(h, nxt, nxt2):
                k.wait_product(act, 4 * h + 1)
                nc.scalar.activation(q[:, :], b_q[:, :], ACT.Silu).then_inc(act_prep, 1)
                k.wait_product(act, 4 * h + 2)
                nc.scalar.activation(gate[:, :], b_g[:, :], ACT.Silu).then_inc(act_prep, 1)
                nc.scalar.preload_act_table_set(LNEXP)
                act.wait_ge(v_turned, h + 1)
                nc.scalar.activation(v[:, :], b_v[:, :], ACT.Copy).then_inc(act_prep, 1)
                act.wait_ge(ft_ready, h + 1)
                nc.scalar.activation(logf[:, :], fbuf[:, :], ACT.Ln).then_inc(logf_ready, 1)
                act.wait_ge(g_ready, h + 1)
                nc.scalar.activation(E[:, :], G[:, :], ACT.Exp)
                nc.scalar.activation(kdf[:, :], kdf[:, :], ACT.Exp, scale=-1.0).then_inc(e_ready, 1)
                for l, b in enumerate(LEVELS):
                    act.wait_ge(diff_ready, NL * h + l + 1)
                    d = blocks(dif[:, l % R, :], b)
                    nc.scalar.activation(d[:, :, 0, :], d[:, :, 0, :], ACT.Exp, scale=-1.0)
                    nc.scalar.activation(d[:, :, 1, :], d[:, :, 1, :], ACT.Exp).then_inc(lexp_ready, 1)
                    if nxt and l == 0:
                        high(h + 1, 3)
                    if nxt2 and l == 4:
                        high(h + 2, 0)
                act.wait_ge(tr_done, h + 1)
                nc.scalar.activation(kdt[:, 0:T - P], b_kv[:, 0:T - P], ACT.Copy).then_inc(kdt_ready, 1)
                act.wait_ge(o_done, h + 1)
                nc.scalar.activation(osb[:, :], b_o[:, :], ACT.Copy, scale=scale).then_inc(osb_ready, 1)
                act.wait_ge(osb_ready, h + 1)
                nc.scalar.activation(k.sq[:, 0, :], osb[:, :], ACT.Square).then_inc(osq_ready, 1)
                if nxt2:
                    high(h + 2, 1)
                    high(h + 2, 2)
                act.wait_ge(nrm_done, h + 1)
                ch.link(nc.scalar.activation(k.rstd[:, :], b_x0[:, :], ACT.Ln, bias=k.epsc[:, 0:1], scale=1.0 / P))
                nc.scalar.activation(k.rstd[:, :], k.rstd[:, :], ACT.Exp, scale=-0.5).then_inc(rs_ready, 1)
                if nxt:
                    early(h + 1)
                act.wait_ge(y_ready, h + 1)

            norm_in.scalar(act)
            for s in range(2, 4):
                k.split_high(act, s, 0)
            high(1, 0)
            high(1, 1)
            high(1, 2)
            early(0)
            with act.Fori(0, H - 2) as h:
                ch.loop(3, h)
                step(h, True, True)
            ch.end(H - 2)
            step(H - 2, True, False)
            for s in range(2):
                k.wait_product(act, 4 * H - 2 + s)
                k.split_high(act, 2 + s, H)
            step(H - 1, False, False)

        @block.gpsimd
        def _(pool):
            def step(h):
                pool.wait_ge(e_ready, h + 1)
                nc.gpsimd.tensor_tensor(kd[:, :], kk[:, :], kdf[:, :], ALU.mult)
                nc.gpsimd.tensor_tensor(qd[:, :], q[:, :], E[:, :], ALU.mult).then_inc(kd_ready, 1)
                for l, b in enumerate(LEVELS):
                    pool.wait_ge(lexp_ready, NL * h + l + 1)
                    if l >= R:
                        pool.wait_ge(lv_done, 8 * h + l + 2 - R)
                    d, x = blocks(dif[:, l % R, :], b), blocks(X[:, l % R, :], b)
                    nc.gpsimd.tensor_tensor(x[:, :, 0, :], blocks(kk[:, :], b)[:, :, 0, :], d[:, :, 0, :], ALU.mult)
                    nc.gpsimd.tensor_tensor(x[:, :, 1, :], blocks(q[:, :], b)[:, :, 1, :], d[:, :, 1, :], ALU.mult).then_inc(x_ready, 1)

            norm_in.gpsimd(pool)
            with pool.Fori(0, H) as h:
                step(h)
            for s in range(2):
                k.split_low(pool, 2 + s, 4 * H + s, other=s == 0)

        @block.vector
        def _(dve):
            ch = Chain(dve, ch_dve)

            def diff(h, l):
                b = LEVELS[l]
                g = G[:, :].rearrange("p (n b) -> p n b", b=2 * b)
                ref = g[:, :, b - 1:b].to_broadcast([P, T // (2 * b), 2 * b])
                if l >= R:
                    dve.wait_ge(x_ready, NL * h + l + 1 - R)
                nc.vector.tensor_tensor(dif[:, l % R, :].rearrange("p (n b) -> p n b", b=2 * b), g, ref, ALU.subtract).then_inc(diff_ready, 1)

            def low(h, s):
                k.split_low(dve, s, 4 * h + s)

            def clamp(h):
                k.wait_product(dve, 4 * h)
                nc.vector.tensor_scalar(fbuf[:, :], b_f[:, :], -44.0, None, ALU.max).then_inc(f_clamped, 1)

            def step(h, nxt, nxt2):
                dve.wait_ge(sig_ready, h + 1)
                lb, omlb = k.lb[:, 0, bass.ds(h, 1)], k.lb[:, 1, bass.ds(h, 1)]
                ch.link(nc.vector.tensor_scalar(sig[:, :], sig[:, :], omlb, None, ALU.mult))
                nc.vector.tensor_scalar(fbuf[:, :], sig[:, :], lb, None, ALU.add).then_inc(ft_ready, 1)
                nc.vector.tensor_tensor(kk[:, :], ef[:, :], sig[:, :], ALU.mult)
                dve.wait_ge(logf_ready, h + 1)
                ch.link(nc.vector.tensor_tensor_scan(G[:, :], k.c("reset"), logf[:, :], 0.0, ALU.mult, ALU.add))
                nc.vector.tensor_tensor(chunks(kdf), chunks(G), chunks(G)[:, :, P - 1:P].to_broadcast([P, NT, P]), ALU.subtract).then_inc(g_ready, 1)
                for l in range(R):
                    diff(h, l)
                if nxt:
                    low(h + 1, 3)
                dve.wait_ge(lv_done, 8 * h + 1)
                nc.vector.tensor_tensor(chunks(at), chunks(b_x0), mask("ident", 0), ALU.mult).then_inc(at_done, 1)
                for l in range(NL):
                    dve.wait_ge(lv_done, 8 * h + l + 2)
                    dve.wait_ge(at_done, 8 * h + l + 1)
                    if l + R < NL:
                        diff(h, l + R)
                    elif nxt2 and l == 4:
                        low(h + 2, 0)
                    elif nxt and l == 5:
                        clamp(h + 1)
                    else:
                        nc.vector.memset(tick[:, l + R - NL:l + R + 1 - NL], 0.0)
                    nc.vector.copy_predicated(chunks(at), mask("levels", l * P).bitcast(U32), chunks(b_x[(l + 1) % 2])).then_inc(at_done, 1)
                dve.wait_ge(kv_done, h + 1)
                ch.link(nc.vector.tensor_copy(S[:, 0, :], b_kv[:, 0:P]))
                ch.link(nc.vector.scalar_tensor_tensor(S[:, 1, :], S[:, 0, :], E[:, 2 * P - 1:2 * P], b_kv[:, P:2 * P], ALU.mult, ALU.add))
                nc.vector.scalar_tensor_tensor(S[:, 2, :], S[:, 1, :], E[:, 3 * P - 1:3 * P], b_kv[:, 2 * P:3 * P], ALU.mult, ALU.add).then_inc(s_ready, 1)
                dve.wait_ge(osb_ready, h + 1)
                ch.link(nc.vector.tensor_tensor(gate[:, :], gate[:, :], osb[:, :], ALU.mult))
                if nxt2:
                    low(h + 2, 1)
                    low(h + 2, 2)
                dve.wait_ge(rs_ready, h + 1)
                nc.vector.scalar_tensor_tensor(k.y[:, bass.ds(h, 1), :].rearrange("p a t -> p (a t)"), gate[:, :], k.p("cnorm", h),
                                               k.rstd[:, :], ALU.mult, ALU.mult).then_inc(y_ready, 1)

            norm_in.vector(dve)
            for s in range(2, 4):
                low(0, s)
            clamp(0)
            low(1, 0)
            low(1, 1)
            low(1, 2)
            with dve.Fori(0, H - 2) as h:
                ch.loop(5, h)
                step(h, True, True)
            ch.end(H - 2)
            step(H - 2, True, False)
            step(H - 1, False, False)
    k.count({s: H for s in range(4)}, split=2)


HA = 4
CAP = 15.0


@phase
def ab_gates(k, ahead):
    nc = k.nc
    sem, sb = k.sem, k.sb
    R = sb("gate_rows", [HA, 12, T], F32)
    A = sb("decay_rate", [HA, 1], F32)
    r_i, r_f, r_a, r_b, r_sp, r_F, r_Aa, r_M, r_e, r_abs, r_G, r_t = (R[:, i, :] for i in range(12))
    norm_in = InputNorm(k, "ab_in")
    rows_taken, tanh_done, e1, l1, e2, rows_ready, spread, spread_used, turned, cols_ready, cexp, ch_d, ch_a = (
        sem("ab_" + s) for s in ("rows_taken tanh_done exp1 ln1 beta_ready rows_ready spread spread_used "
                                 "turned cols_ready cols_exp ch_dve ch_act").split())
    gb = lambda i: k.p("gbias", i)[0:HA]
    with nc.Block() as block:
        @block.sync
        def _(sp):
            k.load_ahead(sp, ahead[:3])
            for s in range(2):
                k.wait_split(sp, 1 + s)
                k.load(sp, s, ahead[3 + s])

        @block.tensor
        def _(pe):
            k.wait_split(pe, 0)
            k.project(k.ps[3][:, :], 3, norm_in.ready(pe)).then_inc(k.proj_done, 1)
            for s in range(3):
                k.wait_split(pe, 1 + s)
                k.project(k.ps[s][:, :], s).then_inc(k.proj_done, 1)
            pe.wait_ge(rows_ready, 1)
            pe.wait_ge(e2, 1)
            n = 0
            for kind, row in enumerate((r_M, r_e, r_G, r_b)):
                for h in range(HA):
                    if n >= 4:
                        pe.wait_ge(spread_used, n - 3)
                    nc.tensor.matmul(k.ps[4 + n % 4][:, :], k.c("sel", h * P, h * P + P)[0:HA, :], row, start=True, stop=True).then_inc(spread, 1)
                    n += 1
            for kind, row in enumerate((r_Aa, r_G, r_b)):
                for c in range(NT):
                    at = (kind * NT + c) * HA
                    ins = nc.tensor.transpose(k.ps[3][:, at:at + HA], row[:, c * P:(c + 1) * P], k.c("ident", 0, HA)[0:HA, :])
            ins.then_inc(turned, 1)

        @block.gpsimd
        def _(pool):
            norm_in.gpsimd(pool)
            for s in range(3):
                k.split_low(pool, s, 1 + s)

        @block.vector
        def _(dve):
            ch = Chain(dve, ch_d)
            norm_in.vector(dve)
            k.wait_product(dve, 0)
            nc.vector.tensor_scalar(r_i, k.ps[3][0:HA, :], gb(0), 1.0 / CAP, ALU.add, ALU.mult)
            ch.link(nc.vector.tensor_copy(r_f, k.ps[3][32:32 + HA, :]))
            nc.vector.tensor_scalar(r_f, r_f, gb(1), 1.0 / CAP, ALU.add, ALU.mult)
            ch.link(nc.vector.tensor_copy(r_a, k.ps[3][64:64 + HA, :]))
            ch.link(nc.vector.tensor_scalar(r_a, r_a, k.p("adt", 1)[0:HA], None, ALU.add))
            nc.vector.scalar_tensor_tensor(r_abs, r_a, -1.0, r_a, ALU.mult, ALU.max)
            ch.link(nc.vector.tensor_scalar(r_b, k.ps[3][96:96 + HA, :], -44.0, None, ALU.max))
            nc.vector.tensor_scalar(r_a, r_a, 0.0, None, ALU.max).then_inc(rows_taken, 1)
            dve.wait_ge(tanh_done, 1)
            nc.vector.tensor_scalar(r_i, r_i, CAP, None, ALU.mult)
            dve.wait_ge(l1, 1)
            dve.wait_ge(rows_taken, 1)
            ch.link(nc.vector.tensor_tensor_scan(r_F, r_sp, r_sp, 0.0, ALU.add, ALU.max))
            ch.link(nc.vector.tensor_tensor(r_Aa, r_i, r_F, ALU.add))
            ch.link(nc.vector.tensor_tensor_scan(r_M, r_Aa, r_Aa, 0.0, ALU.max, ALU.max))
            nc.vector.tensor_tensor(r_e, r_F, r_M, ALU.subtract)
            ch.link(nc.vector.tensor_tensor(r_t, r_a, r_abs, ALU.add))
            ch.link(nc.vector.tensor_scalar(r_t, r_t, A[:, 0:1], None, ALU.mult))
            nc.vector.tensor_tensor_scan(r_G, k.c("reset")[0:HA, :], r_t, 0.0, ALU.mult, ALU.add).then_inc(rows_ready, 1)
            for n in (0, 1, 2, 3, 8, 9, 10, 11, 12, 13, 14, 15):
                kind, h = divmod(n, HA)
                dve.wait_ge(spread, n + 1)
                if n == 8:
                    dve.wait_ge(spread_used, 8)
                nc.vector.tensor_copy((k.bcm, k.bcg)[kind // 2][:, kind % 2, h, :], k.ps[4 + n % 4][:, :]).then_inc(spread_used, 1)
            dve.wait_ge(turned, 1)
            dve.wait_ge(spread_used, 16)
            t = k.ps[3][:, 0:3 * NT * HA].rearrange("p (k c h) -> p k h c", k=3, c=NT)
            ch.link(nc.vector.tensor_copy(k.cols[:, 0:3, :, :], t))
            last = k.bcg[:, 0, :, :].rearrange("p h (c l) -> p h c l", l=P)[:, :, :, P - 1]
            nc.vector.tensor_copy(k.cols[:, 5, :, :], last)
            ch.link(nc.vector.tensor_tensor(k.cols[:, 3, :, :], k.cols[:, 1, :, :], last, ALU.subtract))
            nc.vector.tensor_copy(k.cols[:, 4, :, :], k.cols[:, 1, :, :]).then_inc(cols_ready, 1)
            dve.wait_ge(cexp, 1)
            ch.link(nc.vector.tensor_tensor(k.cols[:, 4, :, :], k.cols[:, 4, :, :], k.cols[:, 2, :, :], ALU.mult))

        @block.scalar
        def _(act):
            ch = Chain(act, ch_a)
            norm_in.scalar(act)
            for s in range(3):
                k.split_high(act, s, 0)
            act.wait_ge(rows_taken, 1)
            ch.link(nc.scalar.activation(R[:, 0:2, :], R[:, 0:2, :], ACT.Tanh))
            nc.scalar.activation(r_t, r_f, ACT.Copy, scale=CAP).then_inc(tanh_done, 1)
            nc.scalar.preload_act_table_set(LNEXP)
            act.wait_ge(tanh_done, 1)
            nc.scalar.activation(r_sp, r_t, ACT.Exp, scale=-1.0)
            nc.scalar.activation(r_abs, r_abs, ACT.Exp, scale=-1.0)
            nc.scalar.activation(A[:, 0:1], k.p("adt", 0)[0:HA], ACT.Exp)
            ch.link(nc.scalar.activation(r_b, r_b, ACT.Exp, scale=-1.0))
            nc.scalar.activation(r_sp, r_sp, ACT.Ln, bias=1.0)
            nc.scalar.activation(r_abs, r_abs, ACT.Ln, bias=1.0).then_inc(l1, 1)
            ch.link(nc.scalar.activation(r_b, r_b, ACT.Ln, bias=1.0))
            nc.scalar.activation(r_b, r_b, ACT.Exp, scale=-1.0).then_inc(e2, 1)
            for n in range(4, 8):
                act.wait_ge(spread, n + 1)
                act.wait_ge(spread_used, n)
                nc.scalar.activation(k.bcm[:, 1, n - 4, :], k.ps[4 + n % 4][:, :], ACT.Exp).then_inc(spread_used, 1)
            act.wait_ge(cols_ready, 1)
            nc.scalar.activation(k.cols[:, 3, :, :], k.cols[:, 3, :, :], ACT.Exp)
            nc.scalar.activation(k.cols[:, 4:6, :, :], k.cols[:, 4:6, :, :], ACT.Exp, scale=-1.0).then_inc(cexp, 1)
    k.count({3: 1}, split=3, projected=3)


@phase
def mlstm(k, weights, ahead):
    nc = k.nc
    sem, sb = k.sem, k.sb
    H = HA
    DK = 64
    acc, q, kk, v, vraw, og, osb, den = (sb(f"m_{s}", [n, T], F32) for s, n in
                                   (("acc", P), ("q", DK), ("k", DK), ("v", P), ("v_raw", P), ("og", P), ("o", P), ("den", P)))
    hc = sb("m_hc", [P, NT], F32)
    off = [0, 512, 896, 1152, 1280]
    W = sb("m_W", [P, off[4]], F32)
    b_qk, b_o, b_v, _, b_s0, b_s1, b_num, b_den = k.ps
    b_s = [b_s0, b_s1]
    raw_ready, v_turned = sem("m_raw_ready"), sem("m_v_turned")
    (tap_done, conv_done, act_prep, o_clamped, qk_ready, og_ready, arg_ready, d_ready, st_done, wt_ready, pv_done,
     osb_ready, osq_ready, nrm_done, rs_ready, y_ready, ch_act, ch_dve) = (sem("m_" + s) for s in (
         "tap_done conv_done act_prep o_clamped qk_ready og_ready arg_ready d_ready st_done wt_ready pv_done "
         "osb_ready osq_ready nrm_done rs_ready y_ready ch_act ch_dve").split())

    with nc.Block() as block:
        @block.sync
        def _(sp):
            k.first_loads(sp, [weights[s, :, :] for s in range(3)])
            k.wait_split(sp, 2)
            k.load(sp, 2, weights[5, :, :])
            with sp.Fori(2, H) as h:
                for s in range(3):
                    k.wait_split(sp, 3 * h - 3 + s)
                    k.load(sp, s, weights[bass.ds(3 * h + s, 1), :, :].rearrange("a p d -> p (a d)"))
            k.wait_split(sp, 3 * H - 1)
            k.load_ahead(sp, ahead, upto=3 * H)

        @block.tensor
        def _(pe):
            def project(h, s):
                k.wait_split(pe, 3 * h + s)
                if s < 3:
                    pe.wait_ge((conv_done, o_clamped, act_prep)[s], h)
                k.project(k.ps[s][:, :], s).then_inc(k.proj_done, 1)

            def score(h, j):
                if j >= 2:
                    pe.wait_ge(wt_ready, 4 * h + j - 1)
                nc.tensor.matmul(b_s[j % 2][:, 0:T - j * P], kk[:, j * P:(j + 1) * P], q[:, j * P:T], start=True, stop=True).then_inc(st_done, 1)

            def core(h, after, first=False):
                project(after, 0)
                pe.wait_ge(raw_ready, h + 1)
                k.turn(b_v, vraw).then_inc(v_turned, 1)
                pe.wait_ge(qk_ready, h + 1)
                if not first:
                    pe.wait_ge(rs_ready, h)
                score(h, 0)
                score(h, 1)
                project(after, 1)
                score(h, 2)
                score(h, 3)
                pe.wait_ge(act_prep, h + 1)
                for j in range(NT):
                    pe.wait_ge(wt_ready, 4 * h + j + 1)
                    w = W[:, off[j]:off[j + 1]]
                    nc.tensor.matmul(b_num[:, j * P:T], v[:, j * P:(j + 1) * P], w, start=j == 0, stop=j == NT - 1)
                    ins = nc.tensor.matmul(b_den[:, j * P:T], k.c("ones"), w, start=j == 0, stop=j == NT - 1)
                ins.then_inc(pv_done, 1)
                project(after, 2)
                pe.wait_ge(osq_ready, h + 1)
                nc.tensor.matmul(b_s0[:, :], k.c("ones"), k.sq[:, 0, :], start=True, stop=True).then_inc(nrm_done, 1)

            core(0, 1, first=True)
            with pe.Fori(1, H - 1) as h:
                core(h, h + 1)
            core(H - 1, H)
            project(H, 3)

        @block.scalar
        def _(act):
            ch = Chain(act, ch_act)

            def high(h, s):
                k.wait_product(act, 3 * h + s - 3)
                k.split_high(act, s, h)

            def tap(h):
                k.wait_product(act, 3 * h)
                nc.scalar.activation(acc[:, :], b_qk[:, :], ACT.Copy, scale=k.p("mconv", 4 * h + 3)).then_inc(tap_done, 1)

            def step(h, last=False):
                k.wait_product(act, 3 * h + 2)
                nc.scalar.activation(vraw[:, :], b_v[:, :], ACT.Copy).then_inc(raw_ready, 1)
                high(h + 1, 2)
                if last:
                    k.split_high(act, 3, 0)
                act.wait_ge(conv_done, h + 1)
                nc.scalar.activation(q[:, :], acc[0:DK, :], ACT.Silu)
                nc.scalar.activation(kk[:, :], acc[DK:P, :], ACT.Silu).then_inc(qk_ready, 1)
                nc.scalar.preload_act_table_set(LNEXP)
                act.wait_ge(arg_ready, h + 1)
                nc.scalar.activation(W[:, :], W[:, :], ACT.Exp, scale=-1.0).then_inc(d_ready, 1)
                act.wait_ge(v_turned, h + 1)
                nc.scalar.activation(v[:, :], b_v[:, :], ACT.Copy).then_inc(act_prep, 1)
                if not last:
                    high(h + 2, 0)
                act.wait_ge(o_clamped, h + 1)
                ch.link(nc.scalar.activation(og[:, :], og[:, :], ACT.Exp, scale=-1.0))
                ch.link(nc.scalar.activation(og[:, :], og[:, :], ACT.Ln, bias=1.0))
                nc.scalar.activation(og[:, :], og[:, :], ACT.Exp, scale=-1.0).then_inc(og_ready, 1)
                if not last:
                    tap(h + 1)
                act.wait_ge(osb_ready, h + 1)
                nc.scalar.activation(k.sq[:, 0, :], osb[:, :], ACT.Square).then_inc(osq_ready, 1)
                if not last:
                    high(h + 2, 1)
                act.wait_ge(nrm_done, h + 1)
                ch.link(nc.scalar.activation(k.rstd[:, :], b_s0[:, :], ACT.Ln, bias=k.epsc[:, 0:1], scale=1.0 / P))
                nc.scalar.activation(k.rstd[:, :], k.rstd[:, :], ACT.Exp, scale=-0.5).then_inc(rs_ready, 1)

            high(1, 0)
            tap(0)
            high(1, 1)
            with act.Fori(0, H - 1) as h:
                ch.loop(3, h)
                step(h)
            ch.end(H - 1)
            step(H - 1, last=True)

        @block.gpsimd
        def _(pool):
            k.split_low(pool, 0, 3)
            k.split_low(pool, 1, 4)
            with pool.Fori(1, H) as h:
                k.split_low(pool, 2, 3 * h + 2)
                k.split_low(pool, 0, 3 * h + 3)
                k.split_low(pool, 1, 3 * h + 4)
            k.split_low(pool, 2, 3 * H + 2)
            k.split_low(pool, 3, 3 * H + 3)

        @block.vector
        def _(dve):
            ch = Chain(dve, ch_dve)

            def convolve(h):
                dve.wait_ge(tap_done, h + 1)
                for tap in (2, 1, 0):
                    ins = nc.vector.scalar_tensor_tensor(acc[:, 3 - tap:T], b_qk[:, 0:T - 3 + tap], k.p("mconv", 4 * h + tap), acc[:, 3 - tap:T], ALU.mult, ALU.add)
                    if tap:
                        ch.link(ins)
                ins.then_inc(conv_done, 1)

            def step(h, last=False):
                ch.link(nc.vector.tensor_copy(hc[:, :].rearrange("p (a c) -> p a c", a=1), k.cols[:, 0, bass.ds(h, 1), :]))
                for j in range(NT):
                    ins = nc.vector.tensor_scalar(W[:, off[j]:off[j + 1]].rearrange("p (a t) -> p a t", a=1),
                                                  k.bcm[:, 0, bass.ds(h, 1), j * P:T], hc[:, j:j + 1], 0.0, ALU.subtract, ALU.max)
                ins.then_inc(arg_ready, 1)
                k.wait_product(dve, 3 * h + 1)
                nc.vector.tensor_scalar(og[:, :], b_o[:, :], -44.0, None, ALU.max).then_inc(o_clamped, 1)
                dve.wait_ge(d_ready, h + 1)
                for j in range(NT):
                    dve.wait_ge(st_done, 4 * h + j + 1)
                    w = W[:, off[j]:off[j + 1]]
                    ch.link(nc.vector.scalar_tensor_tensor(w, b_s[j % 2][:, 0:T - j * P], DK ** -0.5, w, ALU.mult, ALU.mult))
                    nc.vector.tensor_tensor(w[:, 0:P], w[:, 0:P], k.c("upper"), ALU.mult).then_inc(wt_ready, 1)
                if not last:
                    convolve(h + 1)
                dve.wait_ge(pv_done, h + 1)
                ch.link(nc.vector.scalar_tensor_tensor(den[:, :].rearrange("p (a t) -> p a t", a=1), b_den[:, :].rearrange("p (a t) -> p a t", a=1), -1.0,
                                                       k.bcm[:, 1, bass.ds(h, 1), :], ALU.mult, ALU.max))
                ch.link(nc.vector.tensor_tensor(den[:, :], den[:, :], b_den[:, :], ALU.max))
                ch.link(nc.vector.reciprocal(den[:, :], den[:, :]))
                nc.vector.tensor_tensor(osb[:, :], b_num[:, :], den[:, :], ALU.mult).then_inc(osb_ready, 1)
                dve.wait_ge(og_ready, h + 1)
                dve.wait_ge(osb_ready, h + 1)
                ch.link(nc.vector.tensor_tensor(og[:, :], og[:, :], osb[:, :], ALU.mult))
                dve.wait_ge(rs_ready, h + 1)
                nc.vector.scalar_tensor_tensor(k.y[:, bass.ds(h, 1), :].rearrange("p a t -> p (a t)"), og[:, :], k.p("mnorm", h),
                                               k.rstd[:, :], ALU.mult, ALU.mult).then_inc(y_ready, 1)
                dve.wait_ge(y_ready, h + 1)

            convolve(0)
            with dve.Fori(0, H - 1) as h:
                ch.loop(1 + 2 + NT + 4, h)
                step(h)
            ch.end(H - 1)
            step(H - 1, last=True)
    k.count({s: H for s in range(3)}, split=4, projected=4)


@phase
def delta(k, weights, ahead):
    nc = k.nc
    sem, sb = k.sem, k.sb
    H, NL = HA, len(LEVELS)
    scale = P ** -0.5
    q, kk, v, gate, rk, dec, db, at, At, EG, qd, kd, kb, vb, BT, Y, nwT, vn, osb = (sb("g_" + s, [P, T], F32) for s in (
        "q k v gate rk dec db attn At EG qd kd kb vb BT Y nwT vn o").split())
    HB = T // 2
    TB = sb("g_T", [P, 2, 2, HB], F32)
    S = sb("g_S", [P, NT - 1, P], F32)
    hc = sb("g_hc", [P, 6, NT], F32)
    b0, b1, b2, b3, b4, b5, b6, b7 = k.ps
    b_y, b_z = (b4, b7), (b5, b6)
    conv = ((b0, q), (b1, kk), (b2, v))
    (tap_done, conv_done, silu_done, gate_done, hc_ready, sq_ready, nrm_qk, rqk_ready, qk_ready, qk_turned, v_turned, kdb_ready,
     vb_ready, kk_done, arg_ready, dec_ready, eg_ready, masked, db_ready, t_ready, bt_ready, y_done, y_copied, z_done, w_done, nw_ready, vn_done, vn_ready,
     kv_done, s_ready, o_done, osb_ready, osq_ready, nrm_done, rs_ready, y_ready, qd_ready, ch_act, ch_dve, ch_pool) = (sem("g_" + s) for s in (
         "tap_done conv_done silu_done gate_done hc_ready sq_ready nrm_qk rqk_ready qk_ready qk_turned v_turned kdb_ready "
         "vb_ready kk_done arg_ready dec_ready eg_ready masked db_ready t_ready bt_ready y_done y_copied z_done w_done nw_ready vn_done vn_ready "
         "kv_done s_ready o_done osb_ready osq_ready nrm_done rs_ready y_ready qd_ready ch_act ch_dve ch_pool").split())

    TH = 1 + 2 * NL

    def cs(c):
        return slice(c * P, (c + 1) * P)

    def chunks(x):
        return x[:, :].rearrange("p (c l) -> p c l", l=P)

    def mask(name, lo=0, n=NT):
        return k.c(name, lo, lo + P).rearrange("p (a l) -> p a l", a=1).to_broadcast([P, n, P])

    def tm(c, kind=0):
        return TB[:, c // 2, kind, (c % 2) * P:(c % 2) * P + P]

    def half(x, a):
        return x[:, a * HB:(a + 1) * HB]

    def row(kind, h):
        return k.bcg[:, kind, bass.ds(h, 1), :]

    def one(x):
        return x.rearrange("p (a t) -> p a t", a=1)

    with nc.Block() as block:
        @block.sync
        def _(sp):
            more = k.first_loads(sp, [weights[s, :, :] for s in range(4)])
            for s in range(more, 4):
                k.wait_split(sp, s)
                k.load(sp, s, weights[4 + s, :, :])
            with sp.Fori(2, H) as h:
                for s in range(4):
                    k.wait_split(sp, 4 * h - 4 + s)
                    k.load(sp, s, weights[bass.ds(4 * h + s, 1), :, :].rearrange("a p d -> p (a d)"))
            k.wait_split(sp, 4 * H - 1)
            k.load_ahead(sp, ahead, 2)

        @block.tensor
        def _(pe):
            def project(h, lo, hi):
                for n in range(lo, hi):
                    s, m = divmod(n, KD)
                    if m == 0:
                        k.wait_split(pe, 4 * h + s)
                        if s < 3:
                            pe.wait_ge(conv_done, 3 * h - 2 + s)
                        else:
                            pe.wait_ge(gate_done, h)
                    ins = k.product(k.ps[s][:, :], [x[:, m * P:(m + 1) * P] for x in k.ws[s]], [x[:, m, :] for x in (k.uh, k.ul)],
                                    m == 0, m == KD - 1)
                    if m == KD - 1:
                        ins.then_inc(k.proj_done, 1)

            def four(bank, lhsT, rhs, cols=None):
                for c in range(NT):
                    ins = nc.tensor.matmul(bank[:, cs(c)], lhsT[:, cs(c)], rhs[:, cs(c)], start=True, stop=True)
                return ins

            def core(h, nxt, first):
                fill = (lambda lo, hi: project(h + 1, lo, hi)) if nxt else (lambda lo, hi: None)
                lead = 3 if first else 9
                fill(0, lead)
                if not first:
                    pe.wait_ge(rs_ready, h)
                pe.wait_ge(sq_ready, h + 1)
                nc.tensor.matmul(b4[:, :], k.c("ones"), k.sq[:, 0, :], start=True, stop=True)
                nc.tensor.matmul(b5[:, :], k.c("ones"), k.sq[:, 1, :], start=True, stop=True).then_inc(nrm_qk, 1)
                if not first:
                    pe.wait_ge(osb_ready, h)
                pe.wait_ge(silu_done, 3 * h + 3)
                for c in range(NT):
                    ins = nc.tensor.transpose(b7[:, cs(c)], v[:, cs(c)], k.c("ident"))
                ins.then_inc(v_turned, 1)
                fill(lead, 11)
                pe.wait_ge(qk_ready, h + 1)
                for c in range(NT):
                    ins = nc.tensor.transpose(b6[:, cs(c)], kk[:, cs(c)], k.c("ident"))
                ins.then_inc(qk_turned, 1)
                four(b4, kk, kk)
                four(b5, kk, q).then_inc(kk_done, 1)
                fill(11, 13)
                pe.wait_ge(vb_ready, h + 1)
                for l in range(NL):
                    for a in range(2):
                        pe.wait_ge(bt_ready, 2 * NL * h + 2 * l + a + 1)
                        pe.wait_ge(t_ready, TH * h + (2 * l + a if l else 1))
                        for c in (2 * a, 2 * a + 1):
                            ins = nc.tensor.matmul(b_y[a][:, cs(c)], BT[:, cs(c)], tm(c), start=True, stop=True)
                        ins.then_inc(y_done, 1)
                    fill(13 + 2 * l, 14 + 2 * l)
                    for a in range(2):
                        pe.wait_ge(y_copied, 2 * NL * h + 2 * l + a + 1)
                        if l == 0:
                            pe.wait_ge(kdb_ready, h + 1)
                        for c in (2 * a, 2 * a + 1):
                            at_ = (c % 2) * P
                            nc.tensor.matmul(b_z[a][:, at_:at_ + P], tm(c, 1), Y[:, cs(c)], start=True, stop=True)
                            ins = nc.tensor.matmul(b_z[a][:, HB + at_:HB + at_ + P], Y[:, cs(c)], tm(c, 1), start=True, stop=True)
                        ins.then_inc(z_done, 1)
                    fill(14 + 2 * l, 15 + 2 * l)
                pe.wait_ge(t_ready, TH * h + TH)
                for c in range(1, NT):
                    ins = nc.tensor.matmul(b4[:, cs(c)], kb[:, cs(c)], tm(c, 1), start=True, stop=True)
                ins.then_inc(w_done, 1)
                pe.wait_ge(qd_ready, h + 1)
                for c in range(NT):
                    if c == 1:
                        pe.wait_ge(nw_ready, h + 1)
                    ins = nc.tensor.matmul(b5[:, cs(c)], tm(c, 1), vb[:, cs(c)], start=True, stop=c == 0)
                    if c:
                        pe.wait_ge(s_ready, 3 * h + c)
                        ins = nc.tensor.matmul(b5[:, cs(c)], nwT[:, cs(c)], S[:, c - 1, :], start=False, stop=True)
                    ins.then_inc(vn_done, 1)
                    if c:
                        nc.tensor.matmul(b7[:, cs(c)], S[:, c - 1, :], qd[:, cs(c)], start=True, stop=False)
                    fill(27 + c, 28 + c)
                    pe.wait_ge(vn_ready, 4 * h + c + 1)
                    ins = nc.tensor.matmul(b7[:, cs(c)], vn[:, cs(c)], at[:, cs(c)], start=c == 0, stop=True)
                    if c == NT - 1:
                        ins.then_inc(o_done, 1)
                    else:
                        nc.tensor.matmul(b6[:, cs(c)], kd[:, cs(c)], vn[:, cs(c)], start=True, stop=True).then_inc(kv_done, 1)
                fill(31, 32)
                pe.wait_ge(osq_ready, h + 1)
                nc.tensor.matmul(b4[:, :], k.c("ones"), k.sq[:, 0, :], start=True, stop=True).then_inc(nrm_done, 1)

            core(0, True, True)
            with pe.Fori(1, H - 1) as h:
                core(h, True, False)
            core(H - 1, False, False)

        @block.scalar
        def _(act):
            ch = Chain(act, ch_act)

            def high(h, s):
                k.wait_product(act, 4 * h + s - 4)
                k.split_high(act, s, h)

            def tap(h, i):
                k.wait_product(act, 4 * h + i)
                nc.scalar.activation(conv[i][1][:, :], conv[i][0][:, :], ACT.Copy, scale=k.p("gconv", 12 * h + 4 * i + 3)).then_inc(tap_done, 1)

            def silu(h, i):
                act.wait_ge(conv_done, 3 * h + i + 1)
                x = conv[i][1]
                nc.scalar.activation(x[:, :], x[:, :], ACT.Silu).then_inc(silu_done, 1)

            def early(h):
                silu(h, 0)
                silu(h, 1)
                act.wait_ge(silu_done, 3 * h + 2)
                nc.scalar.activation(k.sq[:, 0, :], q[:, :], ACT.Square)
                nc.scalar.activation(k.sq[:, 1, :], kk[:, :], ACT.Square).then_inc(sq_ready, 1)
                silu(h, 2)

            def step(h, nxt, nxt2):
                k.wait_product(act, 4 * h + 3)
                nc.scalar.activation(gate[:, :], b3[:, :], ACT.Silu).then_inc(gate_done, 1)
                nc.scalar.preload_act_table_set(LNEXP)
                act.wait_ge(nrm_qk, h + 1)
                nc.scalar.activation(k.rstd[:, :], b4[:, :], ACT.Ln, bias=k.epsc[:, 0:1])
                ch.link(nc.scalar.activation(rk[:, :], b5[:, :], ACT.Ln, bias=k.epsc[:, 0:1]))
                nc.scalar.activation(k.rstd[:, :], k.rstd[:, :], ACT.Exp, scale=-0.5)
                nc.scalar.activation(rk[:, :], rk[:, :], ACT.Exp, scale=-0.5).then_inc(rqk_ready, 1)
                act.wait_ge(arg_ready, h + 1)
                nc.scalar.activation(dec[:, :], dec[:, :], ACT.Exp, scale=-1.0).then_inc(dec_ready, 1)
                act.wait_ge(v_turned, h + 1)
                act.wait_ge(hc_ready, h + 1)
                for c in range(NT):
                    ins = nc.scalar.activation(vb[:, cs(c)], b7[:, cs(c)], ACT.Copy, scale=hc[:, 2, c:c + 1])
                ins.then_inc(vb_ready, 1)
                nc.scalar.activation(one(EG[:, :]), row(0, h), ACT.Exp, scale=-1.0).then_inc(eg_ready, 1)
                for l in range(NL):
                    for a in range(2):
                        act.wait_ge(y_done, 2 * NL * h + 2 * l + a + 1)
                        nc.scalar.activation(half(Y, a), half(b_y[a], a), ACT.Copy).then_inc(y_copied, 1)
                    if nxt and l in (0, 3):
                        high(h + 1, 2 + l // 3)
                    if nxt and l in (0, 3, 6):
                        tap(h + 1, l // 3)
                    if nxt2 and l in (4, 5):
                        high(h + 2, l - 4)
                act.wait_ge(w_done, h + 1)
                nc.scalar.activation(nwT[:, P:T], b4[:, P:T], ACT.Copy, scale=-1.0).then_inc(nw_ready, 1)
                for c in range(NT):
                    act.wait_ge(vn_done, NT * h + c + 1)
                    nc.scalar.activation(vn[:, cs(c)], b5[:, cs(c)], ACT.Copy).then_inc(vn_ready, 1)
                act.wait_ge(o_done, h + 1)
                nc.scalar.activation(osb[:, :], b7[:, :], ACT.Copy, scale=scale).then_inc(osb_ready, 1)
                act.wait_ge(osb_ready, h + 1)
                nc.scalar.activation(k.sq[:, 0, :], osb[:, :], ACT.Square).then_inc(osq_ready, 1)
                act.wait_ge(nrm_done, h + 1)
                ch.link(nc.scalar.activation(k.rstd[:, :], b4[:, :], ACT.Ln, bias=k.epsc[:, 0:1], scale=1.0 / P))
                nc.scalar.activation(k.rstd[:, :], k.rstd[:, :], ACT.Exp, scale=-0.5).then_inc(rs_ready, 1)
                if nxt:
                    early(h + 1)
                act.wait_ge(y_ready, h + 1)

            tap(0, 0)
            high(1, 0)
            tap(0, 1)
            high(1, 1)
            tap(0, 2)
            early(0)
            with act.Fori(0, H - 2) as h:
                ch.loop(2, h)
                step(h, True, True)
            ch.end(H - 2)
            step(H - 2, True, False)
            for s in range(2):
                k.wait_product(act, 4 * H - 2 + s)
                k.split_high(act, 2 + s, H)
            step(H - 1, False, False)

        @block.gpsimd
        def _(pool):
            ch = Chain(pool, ch_pool)

            def low(h, s):
                k.split_low(pool, s, 4 * h + s)

            def step(h, nxt, nxt2):
                pool.wait_ge(dec_ready, h + 1)
                ch.link(nc.gpsimd.tensor_tensor(chunks(dec), chunks(dec), mask("upper"), ALU.mult))
                nc.gpsimd.tensor_tensor(one(db[:, :]), one(dec[:, :]), row(1, h), ALU.mult).then_inc(db_ready, 1)
                pool.wait_ge(eg_ready, h + 1)
                pool.wait_ge(qk_ready, h + 1)
                nc.gpsimd.tensor_tensor(qd[:, :], q[:, :], EG[:, :], ALU.mult).then_inc(qd_ready, 1)
                pool.wait_ge(masked, h + 1)
                for l in range(NL):
                    for a in range(2):
                        if l:
                            pool.wait_ge(y_done, 2 * NL * h + 2 * l + a - 1)
                        c = slice(2 * a, 2 * a + 2)
                        nc.gpsimd.tensor_tensor(chunks(BT)[:, c, :], chunks(At)[:, c, :], mask("levels", l * P, 2), ALU.mult).then_inc(bt_ready, 1)
                    if nxt and l in (0, 3):
                        low(h + 1, 2 + l // 3)
                    if nxt2 and l in (4, 5):
                        low(h + 2, l - 4)

            low(1, 0)
            low(1, 1)
            with pool.Fori(0, H - 2) as h:
                ch.loop(1, h)
                step(h, True, True)
            ch.end(H - 2)
            step(H - 2, True, False)
            step(H - 1, False, False)
            for s in range(2):
                k.split_low(pool, 2 + s, 4 * H + s)

        @block.vector
        def _(dve):
            ch = Chain(dve, ch_dve)

            def convolve(h, i):
                for tap in (2, 1, 0):
                    add_tap(h, i, tap)

            def add_tap(h, i, tap):
                bank, x = conv[i]
                if tap == 2:
                    dve.wait_ge(tap_done, 3 * h + i + 1)
                ins = nc.vector.scalar_tensor_tensor(x[:, 3 - tap:T], bank[:, 0:T - 3 + tap], k.p("gconv", 12 * h + 4 * i + tap), x[:, 3 - tap:T], ALU.mult, ALU.add)
                if tap:
                    ch.link(ins)
                else:
                    ins.then_inc(conv_done, 1)

            def step(h, nxt):
                nc.vector.tensor_copy(hc[:, :, :].rearrange("p k (a c) -> p k a c", a=1), k.cols[:, :, bass.ds(h, 1), :]).then_inc(hc_ready, 1)
                dve.wait_ge(hc_ready, h + 1)
                for c in range(NT):
                    g = k.bcg[:, 0, bass.ds(h, 1), cs(c)]
                    ins = nc.vector.tensor_scalar(one(dec[:, cs(c)]), g, hc[:, 1, c:c + 1], 0.0, ALU.subtract, ALU.max)
                ins.then_inc(arg_ready, 1)
                nc.vector.tensor_copy(TB[:, :, :, :].rearrange("p a k (c l) -> p (a k c) l", l=P), mask("ident", n=2 * NT)).then_inc(t_ready, 1)
                dve.wait_ge(rqk_ready, h + 1)
                nc.vector.tensor_tensor(kk[:, :], kk[:, :], rk[:, :], ALU.mult)
                nc.vector.tensor_tensor(q[:, :], q[:, :], k.rstd[:, :], ALU.mult).then_inc(qk_ready, 1)
                dve.wait_ge(kk_done, h + 1)
                dve.wait_ge(db_ready, h + 1)
                nc.vector.tensor_tensor(At[:, :], b4[:, :], db[:, :], ALU.mult).then_inc(masked, 1)
                nc.vector.tensor_tensor(at[:, :], b5[:, :], dec[:, :], ALU.mult)
                for c in range(NT):
                    nc.vector.tensor_scalar(kd[:, cs(c)], b6[:, cs(c)], hc[:, 3, c:c + 1], None, ALU.mult)
                    ins = nc.vector.tensor_scalar(kb[:, cs(c)], b6[:, cs(c)], hc[:, 4, c:c + 1], None, ALU.mult)
                ins.then_inc(kdb_ready, 1)
                for l in range(NL):
                    for a in range(2):
                        dve.wait_ge(z_done, 2 * NL * h + 2 * l + a + 1)
                        dve.wait_ge(t_ready, TH * h + (2 * l + a if l else 1))
                        t = TB[:, a, :, :].rearrange("p k n -> p (k n)")
                        nc.vector.tensor_tensor(t, t, b_z[a][:, :], ALU.subtract).then_inc(t_ready, 1)
                    if nxt and l in (1, 2, 3):
                        add_tap(h + 1, 0, 3 - l)
                    if nxt and l in (4, 5, 6):
                        add_tap(h + 1, 1, 6 - l)
                for c in range(NT - 1):
                    dve.wait_ge(kv_done, 3 * h + c + 1)
                    if c == 0:
                        nc.vector.tensor_copy(S[:, 0, :], b6[:, cs(0)]).then_inc(s_ready, 1)
                    else:
                        dve.wait_ge(s_ready, 3 * h + c)
                        nc.vector.scalar_tensor_tensor(S[:, c, :], S[:, c - 1, :], hc[:, 5, c:c + 1], b6[:, cs(c)], ALU.mult, ALU.add).then_inc(s_ready, 1)
                if nxt:
                    convolve(h + 1, 2)
                dve.wait_ge(osb_ready, h + 1)
                ch.link(nc.vector.tensor_tensor(gate[:, :], gate[:, :], osb[:, :], ALU.mult))
                dve.wait_ge(rs_ready, h + 1)
                nc.vector.scalar_tensor_tensor(k.y[:, bass.ds(HA + h, 1), :].rearrange("p a t -> p (a t)"), gate[:, :], k.p("gnorm", h),
                                               k.rstd[:, :], ALU.mult, ALU.mult).then_inc(y_ready, 1)
                dve.wait_ge(y_ready, h + 1)

            for i in range(3):
                convolve(0, i)
            with dve.Fori(0, H - 1) as h:
                ch.loop(7, h)
                step(h, True)
            ch.end(H - 1)
            step(H - 1, False)
    k.count({s: H for s in range(4)}, split=2)


HI, DI = 8, 32
HF = 6
DH = 64
TOPK = 128
NEG = -3e38
OFF = [0, P, 3 * P, 6 * P, 10 * P]


@phase
def shared_inputs(k, weights, pool_w, ahead):
    nc = k.nc
    sem, sb = k.sem, k.sb
    rows = sb("s_rows", [HI, 4, T], F32)
    iq = sb("s_iq", [P, 2, T], F32)
    ik = sb("s_ik", [P, T], F32)
    pv, pg, pp, pw = (sb("s_" + s, [P, 2, n], F32) for s, n in (("pv", T), ("pg", T), ("pp", T), ("pw", P)))
    s2 = sb("s_sum", [P, 2, T], F32)
    relu = sb("s_relu", [P, 2, T], F32)
    iw = sb("s_iw", [P, NT, HI], F32)
    sc = k.bias
    NW = 8
    norm_in = InputNorm(k, "two_in")
    (pw_loaded, pool_used, bank_free, rows_taken, ln_done, f_ready, spread, spread_used, turned, iw_ready, dots_done, relu_ready,
     relu_used, pool_ready, pool_done, ch_dve, ch_act) = (sem("s_" + s) for s in (
         "pw_loaded pool_used bank_free rows_taken ln_done f_ready spread spread_used turned iw_ready dots_done relu_ready "
         "relu_used pool_ready pool_done ch_dve ch_act").split())
    items = [(t, h) for t in range(1, NT) for h in range(HI)]
    r_f, r_n, r_F, r_w = (rows[:, i, :] for i in range(4))

    with nc.Block() as block:
        @block.sync
        def _(sp):
            k.first_loads(sp, [weights[s, :, :] for s in range(4)])
            for n in range(4, NW):
                k.wait_split(sp, n - 4)
                k.load(sp, n % 4, weights[n, :, :])
            sp.dma_start(pw[:, :, :], pool_w).then_inc(pw_loaded, 16)
            k.wait_split(sp, NW - 1)
            k.load_ahead(sp, ahead, upto=NW)

        @block.tensor
        def _(pe):
            def project(n):
                k.wait_split(pe, n)
                if n == 4:
                    pe.wait_ge(iw_ready, 1)
                if n > 4:
                    pe.wait_ge(bank_free, n - 4)
                k.project(k.ps[n % 4][:, :], n % 4, None if n else norm_in.ready(pe)).then_inc(k.proj_done, 1)
            for n in range(5):
                project(n)
            pe.wait_ge(iw_ready, 1)
            for t in range(NT):
                ins = nc.tensor.transpose(k.ps[4][:, t * HI:(t + 1) * HI], r_w[:, t * P:(t + 1) * P], k.c("ident", 0, HI)[0:HI, :])
            ins.then_inc(turned, 1)
            pe.wait_ge(bank_free, 3)
            pe.wait_ge(iw_ready, 2)
            for n, (t, h) in enumerate(items):
                if n >= 4:
                    pe.wait_ge(relu_ready, n - 3)
                r = slice(DI * (h % 4), DI * (h % 4) + DI)
                nc.tensor.matmul(k.ps[4 + n % 4][:, 0:(t + 1) * P], iq[r, h // 4, t * P:(t + 1) * P], ik[r, 0:(t + 1) * P],
                                 start=True, stop=True, tile_position=(DI * (h % 4), 0)).then_inc(dots_done, 1)
            for n in range(5, NW):
                project(n)
            pe.wait_ge(f_ready, 1)
            for h in range(HF):
                if h < 4:
                    pe.wait_ge(relu_ready, len(items))
                else:
                    pe.wait_ge(spread_used, h - 3)
                nc.tensor.matmul(k.ps[4 + h % 4][:, :], k.c("sel", h * P, h * P + P)[0:HF, :], r_F[0:HF, :], start=True, stop=True).then_inc(spread, 1)
            pe.wait_ge(pw_loaded, 16)
            pe.wait_ge(pool_ready, 2)
            pe.wait_ge(bank_free, 7)
            for i in range(2):
                nc.tensor.matmul(k.ps[i][:, :], pw[:, i, :], pp[:, i, :], start=True, stop=True).then_inc(pool_done, 1)
            for s in range(4):
                k.wait_split(pe, NW + s)
                if s < 2:
                    pe.wait_ge(pool_used, s + 1)
                k.project(k.ps[s][:, :], s).then_inc(k.proj_done, 1)

        @block.scalar
        def _(act):
            ch = Chain(act, ch_act)
            def high(n):
                if n >= 4:
                    k.wait_product(act, n - 4)
                k.split_high(act, n % 4, n // 4)
            norm_in.scalar(act)
            for n in range(2, 4):
                high(n)
            k.wait_product(act, 1)
            nc.scalar.activation(ik[:, :], k.ps[1][:, :], ACT.Copy).then_inc(bank_free, 1)
            high(4)
            high(5)
            for i in range(2):
                k.wait_product(act, 2 + i)
                nc.scalar.activation(iq[:, i, :], k.ps[2 + i][:, :], ACT.Copy).then_inc(bank_free, 1)
            high(6)
            high(7)
            nc.scalar.preload_act_table_set(LNEXP)
            act.wait_ge(rows_taken, 1)
            ch.link(nc.scalar.activation(r_n[0:HF], r_n[0:HF], ACT.Exp, scale=-1.0))
            nc.scalar.activation(r_n[0:HF], r_n[0:HF], ACT.Ln, bias=1.0).then_inc(ln_done, 1)
            for n, (t, h) in enumerate(items):
                act.wait_ge(dots_done, n + 1)
                if n >= 2:
                    act.wait_ge(relu_used, n - 1)
                nc.scalar.activation(relu[:, n % 2, 0:(t + 1) * P], k.ps[4 + n % 4][:, 0:(t + 1) * P], ACT.Relu).then_inc(relu_ready, 1)
                if n == 3:
                    k.wait_product(act, 4)
                    nc.scalar.activation(pv[:, 0, :], k.ps[0][:, :], ACT.Copy).then_inc(bank_free, 1)
            k.wait_product(act, 5)
            nc.scalar.activation(pv[:, 1, :], k.ps[1][:, :], ACT.Copy).then_inc(bank_free, 1)
            for i in range(2):
                k.wait_product(act, 6 + i)
                nc.scalar.activation(pg[:, i, :], k.ps[2 + i][:, :], ACT.Silu).then_inc(bank_free, 1)
            for n in range(NW, NW + 4):
                high(n)

        @block.gpsimd
        def _(pool):
            norm_in.gpsimd(pool)
            for n in range(2, NW + 4):
                k.split_low(pool, n % 4, n)

        @block.vector
        def _(dve):
            ch = Chain(dve, ch_dve)
            norm_in.vector(dve)
            k.wait_product(dve, 0)
            nc.vector.tensor_scalar(r_f[0:HF], k.ps[0][0:HF, :], k.p("foxb", 0)[0:HF], None, ALU.add)
            nc.vector.tensor_scalar(r_w, k.ps[0][32:32 + HI, :], HI ** -0.5, None, ALU.mult).then_inc(iw_ready, 1)
            dve.wait_ge(iw_ready, 1)
            ch.link(nc.vector.scalar_tensor_tensor(r_n[0:HF], r_f[0:HF], -1.0, r_f[0:HF], ALU.mult, ALU.max))
            nc.vector.tensor_scalar(r_f[0:HF], r_f[0:HF], -1.0, 0.0, ALU.mult, ALU.max).then_inc(rows_taken, 1)
            dve.wait_ge(rows_taken, 1)
            dve.wait_ge(ln_done, 1)
            ch.link(nc.vector.tensor_tensor(r_f[0:HF], r_f[0:HF], r_n[0:HF], ALU.add))
            nc.vector.tensor_tensor_scan(r_F[0:HF], r_f[0:HF], r_f[0:HF], 0.0, ALU.add, ALU.max).then_inc(f_ready, 1)
            dve.wait_ge(turned, 1)
            nc.vector.tensor_copy(iw[:, :, :], k.ps[4][:, 0:NT * HI].rearrange("p (t h) -> p t h", h=HI)).then_inc(iw_ready, 1)
            dve.wait_ge(iw_ready, 2)
            for n, (t, h) in enumerate(items):
                dve.wait_ge(relu_ready, n + 1)
                s, r, w = sc[:, OFF[t]:OFF[t + 1]], relu[:, n % 2, 0:(t + 1) * P], iw[:, t, h:h + 1]
                if h == 0:
                    nc.vector.tensor_scalar(s, r, w, None, ALU.mult).then_inc(relu_used, 1)
                else:
                    dve.wait_ge(relu_used, n)
                    nc.vector.scalar_tensor_tensor(s, r, w, s, ALU.mult, ALU.add).then_inc(relu_used, 1)
                if h == HI - 1:
                    dve.wait_ge(relu_used, n + 1)
                    ch.link(nc.vector.tensor_tensor(s[:, t * P:], s[:, t * P:], k.c("chunkdiag"), ALU.add))
            for i in range(2):
                dve.wait_ge(bank_free, 4 + i)
                src, wins = pv[:, i, :], 2 + 2 * i
                have, keep = src, {}
                for n in range(wins):
                    d, dst = 1 << n, s2[:, n % 2, :]
                    nc.vector.tensor_copy(dst[:, 0:d], have[:, 0:d])
                    ch.link(nc.vector.tensor_tensor(dst[:, d:], have[:, d:], have[:, 0:T - d], ALU.add))
                    have = dst
                rc = k.c("rcount", i * T, (i + 1) * T)
                for half in range(2):
                    r = slice(64 * half, 64 * half + 64)
                    ins = nc.vector.tensor_tensor(pp[r, i, :], s2[r, half, :], rc[r], ALU.mult)
                ch.link(ins)
                nc.vector.tensor_tensor(pp[:, i, :], pp[:, i, :], src, ALU.subtract).then_inc(pool_ready, 1)
            for h in range(HF):
                dve.wait_ge(spread, h + 1)
                nc.vector.tensor_copy(k.fb[:, h, :], k.ps[4 + h % 4][:, :]).then_inc(spread_used, 1)
            for i in range(2):
                dve.wait_ge(pool_done, i + 1)
                nc.vector.scalar_tensor_tensor(k.y[:, i, :], k.ps[i][:, :], k.p("pscale", i), pg[:, i, :], ALU.mult, ALU.mult).then_inc(pool_used, 1)
    k.count({s: NW // 4 for s in range(4)}, split=4, projected=4)


class Choice:

    def __init__(self, k, done):
        self.k, self.done, self.n = k, done, 0
        self.m8 = k.sb("choice_max8", [P, NT, 8], F32)
        self.steps = [(kind, t) for r in range(TOPK // 8) for kind in range(2) for t in range(1, NT)]

    def some(self, dve, n):
        nc = self.k.nc
        for kind, t in self.steps[self.n:self.n + n]:
            s, m = self.k.bias[:, OFF[t]:OFF[t + 1]], self.m8[:, t, :]
            if self.n >= NT - 1:
                dve.wait_ge(self.done, self.n - NT + 2)
            ins = nc.vector.match_replace(s, m, s, NEG) if kind else nc.vector.max(m, s)
            ins.then_inc(self.done, 1)
            self.n += 1

    def finish(self, dve):
        nc, bias = self.k.nc, self.k.bias
        self.some(dve, len(self.steps))
        dve.wait_ge(self.done, self.n)
        nc.vector.tensor_copy(bias[:, 0:P], self.k.c("chunkdiag"))
        nc.vector.tensor_scalar(bias[:, P:OFF[4]], bias[:, P:OFF[4]], NEG / 2, -BIG, ALU.is_gt, ALU.mult)


@phase
def attention(k, tag, weights, y0, fox, last, ahead):
    nc = k.nc
    sem, sb = k.sem, k.sb
    NP, NI = HF // 2, 2 * NT
    R = 4
    items = [(a, t) for a in range(2) for t in range(NT)]
    q, kk, v, vraw, gate = (sb(f"{tag}_{s}", [P, T], F32) for s in ("q", "k", "v", "v_raw", "gate"))
    L = sb(f"{tag}_logits", [P, R, T], F32)
    PT = sb(f"{tag}_probsT", [P, 2, T], F32)
    st = sb(f"{tag}_stats", [P, NI, 4], F32)
    slot = 2 if last else 0
    raw_ready, v_turned = sem(f"{tag}_raw_ready"), sem(f"{tag}_v_turned")
    (act_prep, st_done, logits_ready, max_ready, exp_done, p_ready, turned, pt_ready, pv_done, y_ready, ch_dve) = (
        sem(f"{tag}_{s}") for s in ("act_prep st_done logits_ready max_ready exp_done p_ready turned pt_ready pv_done y_ready ch_dve").split())
    choice = Choice(k, sem("choice_done")) if fox else None
    b_s, b_t, b_o = k.ps[4:6], k.ps[6], k.ps[7]

    with nc.Block() as block:
        @block.sync
        def _(sp):
            more = k.first_loads(sp, [weights[s, :, :] for s in range(4)])
            for s in range(more, 4):
                k.wait_split(sp, s)
                k.load(sp, s, weights[4 + s, :, :])
            with sp.Fori(2, NP) as i:
                for s in range(4):
                    k.wait_split(sp, 4 * i - 4 + s)
                    k.load(sp, s, weights[bass.ds(4 * i + s, 1), :, :].rearrange("a p d -> p (a d)"))
            k.wait_split(sp, 4 * NP - 1)
            k.load_ahead(sp, ahead, slot, 4 * NP)

        @block.tensor
        def _(pe):
            def project(i, lo, hi):
                for n in range(lo, hi):
                    s, m = divmod(n, KD)
                    if m == 0:
                        k.wait_split(pe, 4 * i + s)
                        pe.wait_ge(act_prep, 4 * i - 3 + s)
                    ins = k.project(k.ps[s][:, :], s, first=m, last=m + 1)
                    if m == KD - 1:
                        ins.then_inc(k.proj_done, 1)

            def score(i, n):
                a, t = items[n]
                if n >= 2:
                    pe.wait_ge(logits_ready, NI * i + n - 1)
                r = slice(DH * a, DH * a + DH)
                nc.tensor.matmul(b_s[n % 2][:, 0:(t + 1) * P], q[r, t * P:(t + 1) * P], kk[r, 0:(t + 1) * P], start=True, stop=True).then_inc(st_done, 1)

            def turn(i, n):
                pe.wait_ge(p_ready, NI * i + n + 1)
                if n:
                    pe.wait_ge(pt_ready, NI * i + n)
                for j in range(items[n][1] + 1):
                    ins = nc.tensor.transpose(b_t[:, j * P:(j + 1) * P], L[:, n % R, j * P:(j + 1) * P], k.c("ident"))
                ins.then_inc(turned, 1)

            def values(i, n):
                a, t = items[n]
                pe.wait_ge(pt_ready, NI * i + n + 1)
                for j in range(t + 1):
                    ins = nc.tensor.matmul(b_o[DH * a:DH * a + DH, t * P:(t + 1) * P], v[:, j * P + DH * a:j * P + DH * a + DH],
                                           PT[:, n % 2, j * P:(j + 1) * P], start=j == 0, stop=j == t)
                ins.then_inc(pv_done, 1)

            def core(i, nxt):
                pe.wait_ge(act_prep, 4 * i + 2)
                score(i, 0)
                score(i, 1)
                if nxt:
                    project(i + 1, 0, 8)
                pe.wait_ge(raw_ready, i + 1)
                k.turn(k.ps[3], vraw).then_inc(v_turned, 1)
                pe.wait_ge(act_prep, 4 * i + 4)
                score(i, 2)
                for n in range(NI):
                    if nxt:
                        project(i + 1, 8 + 3 * n, 11 + 3 * n)
                    turn(i, n)
                    if n + 3 < NI:
                        score(i, n + 3)
                    if n:
                        values(i, n - 1)
                values(i, NI - 1)

            core(0, True)
            with pe.Fori(1, NP - last) as i:
                core(i, True)
            if last:
                core(NP - 1, False)

        @block.scalar
        def _(act):
            def high(i, s):
                k.wait_product(act, 4 * i + s - 4)
                k.split_high(act, s, i)

            def take(i, s):
                k.wait_product(act, 4 * i + s)
                nc.scalar.activation((q, kk, gate)[s][:, :], k.ps[s][:, :], ACT.Silu if s == 2 else ACT.Copy).then_inc(act_prep, 1)

            def early(i):
                take(i, 0)
                take(i, 1)
                k.wait_product(act, 4 * i + 3)
                nc.scalar.activation(vraw[:, :], k.ps[3][:, :], ACT.Copy).then_inc(raw_ready, 1)

            def step(i, nxt, nxt2, more=True):
                take(i, 2)
                if nxt:
                    high(i + 1, 1)
                act.wait_ge(v_turned, i + 1)
                nc.scalar.activation(v[:, :], k.ps[3][:, :], ACT.Copy).then_inc(act_prep, 1)

                def turn(n):
                    t = items[n][1]
                    act.wait_ge(turned, NI * i + n + 1)
                    if n >= 2:
                        act.wait_ge(pv_done, NI * i + n - 1)
                    nc.scalar.activation(PT[:, n % 2, 0:(t + 1) * P], b_t[:, 0:(t + 1) * P], ACT.Copy).then_inc(pt_ready, 1)
                for n, (a, t) in enumerate(items):
                    act.wait_ge(max_ready, NI * i + n + 1)
                    l = L[:, n % R, 0:(t + 1) * P]
                    nc.scalar.activation(l, l, ACT.Exp, bias=st[:, n, 0:1], accum_out=st[:, n, 1:2]).then_inc(exp_done, 1)
                    if nxt and n in (1, 3):
                        high(i + 1, 2 + n // 2)
                    if nxt2 and n == 6:
                        high(i + 2, 0)
                    if n >= 2:
                        turn(n - 2)
                turn(NI - 2)
                turn(NI - 1)
                if more:
                    early(i + 1)
                act.wait_ge(y_ready, i + 1)

            early(0)
            high(1, 0)
            with act.Fori(0, NP - 1 - last) as i:
                step(i, True, True)
            if not last:
                step(NP - 1, True, False, more=False)
            else:
                step(NP - 2, True, False)
                for s in range(2):
                    k.wait_product(act, 4 * NP - 2 + s)
                    k.split_high(act, 2 + s, NP)
                step(NP - 1, False, False, more=False)

        @block.gpsimd
        def _(pool):
            with pool.Fori(1, NP + 1 - last) as i:
                for s in range(4):
                    k.split_low(pool, s, 4 * i + s)
            if last:
                for s in range(2):
                    k.split_low(pool, 2 + s, 4 * NP + s)

        @block.vector
        def _(dve):
            ch = Chain(dve, ch_dve)

            def step(i):
                def normalize(n):
                    l = L[:, n % R, 0:(items[n][1] + 1) * P]
                    dve.wait_ge(exp_done, NI * i + n + 1)
                    ch.link(nc.vector.reciprocal(st[:, n, 2:3], st[:, n, 1:2]))
                    nc.vector.tensor_scalar(l, l, st[:, n, 2:3], None, ALU.mult).then_inc(p_ready, 1)
                for n, (a, t) in enumerate(items):
                    w = (t + 1) * P
                    dve.wait_ge(st_done, NI * i + n + 1)
                    if n >= R:
                        dve.wait_ge(turned, NI * i + n + 1 - R)
                    l = L[:, n % R, 0:w]
                    if fox:
                        b = k.fb[:, bass.ds(2 * i + a, 1), 0:w]
                        one = lambda x: x.rearrange("p (a t) -> p a t", a=1)
                        nc.vector.scalar_tensor_tensor(one(l), one(b_s[n % 2][:, 0:w]), DH ** -0.5, b, ALU.mult, ALU.add).then_inc(logits_ready, 1)
                        dve.wait_ge(logits_ready, NI * i + n + 1)
                        ch.link(nc.vector.tensor_tensor(l[:, w - P:w], l[:, w - P:w], k.c("causal"), ALU.add))
                    else:
                        nc.vector.scalar_tensor_tensor(l, b_s[n % 2][:, 0:w], DH ** -0.5, k.bias[:, OFF[t]:OFF[t + 1]], ALU.mult, ALU.add).then_inc(logits_ready, 1)
                        dve.wait_ge(logits_ready, NI * i + n + 1)
                    nc.vector.tensor_reduce(st[:, n, 0:1], l, AX, ALU.max, negate=True).then_inc(max_ready, 1)
                    if choice:
                        choice.some(dve, 2)
                    if n:
                        normalize(n - 1)
                    if choice:
                        choice.some(dve, 2)
                normalize(NI - 1)
                dve.wait_ge(pv_done, NI * i + NI)
                nc.vector.tensor_tensor(k.y[:, bass.ds(i + y0, 1), :], gate[:, :].rearrange("p (a t) -> p a t", a=1),
                                        b_o[:, :].rearrange("p (a t) -> p a t", a=1), ALU.mult).then_inc(y_ready, 1)
                dve.wait_ge(y_ready, i + 1)

            if choice:
                for i in range(NP):
                    step(i)
                choice.finish(dve)
            else:
                with dve.Fori(0, NP) as i:
                    ch.loop(NI, i)
                    step(i)
                ch.end(NP)
    k.count({s: NP for s in range(4)}, split=2 if last else 4, projected=0 if last else 4)


def program(nc, a):
    k = Core(nc, a)
    gains = lambda layer, i: lambda m: k.p("gains", (4 * layer + i) * KD + m)
    tiles4 = lambda w: [w[s, :, :] for s in range(4)]
    tiles6 = lambda w: [w[s, :, :] for s in range(6)]
    rows2 = lambda w: [w[s * P:(s + 1) * P, :] for s in range(2)]
    load_inputs(k, gains(0, 0), a["ab_gate"][0, :, :])
    lower_bounds(k)
    with ExitStack() as s:
        k.bcg = s.enter_context(nc.sbuf_tensor("delta_bc", [P, 2, HA, T], F32))
        k.cols = s.enter_context(nc.sbuf_tensor("gate_cols", [P, 6, HA, NT], F32))
        with nc.sbuf_tensor("mlstm_bc", [P, 2, HA, T], F32) as k.bcm:
            ab_gates(k, tiles6(a["m_in"]))
            mlstm(k, a["m_in"], tiles6(a["g_in"]))
        delta(k, a["g_in"], rows2(a["ab_out"]))
    out_proj(k, "ab", k.y, KD, a["ab_out"], gains(0, 1), gains(0, 2), tiles4(a["ffn_up"][0]))
    ffn(k, "0", 0, gains(1, 0), tiles4(a["c_in"]))
    k.clear_semaphores()
    hgrn2(k, a["c_in"], rows2(a["c_out"]))
    out_proj(k, "c", k.y, KD, a["c_out"], gains(1, 1), gains(1, 2), tiles4(a["ffn_up"][1]))
    ffn(k, "1", 1, lambda m: k.p("norm2", m), tiles4(a["shared_in"]))
    with ExitStack() as s:
        k.fb = s.enter_context(nc.sbuf_tensor("forget_bc", [P, HF, T], F32))
        k.bias = s.enter_context(nc.sbuf_tensor("choice_bias", [P, OFF[4]], F32))
        shared_inputs(k, a["shared_in"], a["pool_w"], tiles6(a["fox_in"]))
        attention(k, "fox", a["fox_in"], 5, True, 0, tiles6(a["dsa_in"]))
        attention(k, "dsa", a["dsa_in"], 2, False, 1, rows2(a["out2"]))
    out_proj(k, "two", k.y, KD, a["out2"], None, lambda m: k.p("final2", m), None)


def constants():
    i = np.arange(P)
    s, l = i[:, None], i[None, :]
    parts = {
        "ident": s == l,
        "ones": np.ones((P, P)),
        "upper": s <= l,
        "causal": np.where(l <= s, 0.0, -BIG),
        "chunkdiag": np.where(l < (s // 64 + 1) * 64, 0.0, -BIG),
        "levels": np.concatenate([(s // (2 * b) == l // (2 * b)) & (s // b % 2 == 0) & (l // b % 2 == 1) for b in LEVELS], 1),
        "sel": np.repeat(s == np.arange(6)[None, :], P, 1),
        "reset": np.broadcast_to((np.arange(T) % P != 0).astype(np.float32), (P, T)),
        "rcount": np.concatenate([1.0 / np.minimum(np.arange(T)[None, :] + 1, np.where(i < 64, a, b)[:, None]) for a, b in ((2, 4), (8, 16))], 1),
    }
    return np.concatenate([np.asarray(parts[n], np.float32) for n, _ in _CST], 1)


def columns(d):
    def fold(v):
        v = v.reshape(-1, P)
        return v.T

    def head_rows(v):
        out = np.zeros((P, v.shape[1]), np.float32)
        out[:v.shape[0]] = v
        return out
    f = np.concatenate([d["ffn_conv_w"], d["ffn_conv_b"][:, None, :]], 1)
    f = f.reshape(2, 4, 2, KF, P).transpose(4, 0, 3, 2, 1)
    m = d["ab_conv_m"][0].reshape(4, 2, 4, 64).transpose(1, 3, 2, 0).reshape(P, 16)
    g = d["ab_conv_g"][0].reshape(4, 3, 4, P).transpose(3, 2, 1, 0)
    parts = {
        "gains": fold(d["norm_gains"]), "norm2": fold(d["norm_g_2"]), "final2": fold(d["final_g_2"]),
        "ffn": f.reshape(P, -1), "mconv": m, "gconv": g.reshape(P, -1),
        "mnorm": fold(d["ab_m_norm"]), "gnorm": fold(d["ab_g_norm"]), "cnorm": fold(d["c_norm"]),
        "lb": fold(d["c_lb_logits"]), "pscale": fold(d["pool_scale_2"]),
        "gbias": head_rows(d["ab_m_gate_bias"][0].T),
        "adt": head_rows(np.stack([d["ab_g_a_log"][0], d["ab_g_dt_bias"][0]], 1)),
        "foxb": head_rows(d["fox_bf_2"][0][:, None]),
    }
    return np.concatenate([parts[n] for n, _ in _COLS], 1)


def tiles(w):
    return w.reshape(KD, P, -1, P).transpose(2, 1, 0, 3).reshape(-1, P, D)


def layout_ffn(d):
    up = np.stack([tiles(w.reshape(D, 2, KF, P).transpose(0, 2, 1, 3).reshape(D, 2 * FF)) for w in d["ffn_w_up"]])
    return {"x": d["x"][0].T, "cst": constants(), "col": columns(d), "ffn_up": up, "ffn_down": d["ffn_w_down"]}


def layout_c(d):
    w = d["c_w_in"][0].reshape(D, 4, HC, P)[:, [1, 0, 3, 2]].transpose(0, 2, 1, 3).reshape(D, 4 * HC * P)
    return {"c_in": tiles(w), "c_out": d["c_w_out"][0]}


def layout_ab(d):
    w = d["ab_w_in"][0]
    cut = lambda lo, n: w[:, lo:lo + n]
    gate = np.zeros((D, P), np.float32)
    for i, lo in enumerate((1536, 1540, 3592, 3596)):
        gate[:, 32 * i:32 * i + 4] = cut(lo, 4)
    m = []
    for h in range(4):
        m += [cut(64 * h, 64), cut(256 + 64 * h, 64), cut(1024 + P * h, P), cut(512 + P * h, P)]
    g = []
    for h in range(4):
        g += [cut(1544 + 512 * i + P * h, P) for i in (0, 1, 2, 3)]
    return {"ab_gate": tiles(gate), "m_in": tiles(np.concatenate(m, 1)), "g_in": tiles(np.concatenate(g, 1)), "ab_out": d["ab_w_out"][0]}


def layout_2(d):
    w = d["w_in_2"][0]
    names = ("pv", 256), ("pg", 256), ("dq", 384), ("dk", 384), ("dv", 384), ("dg", 384), ("iq", 256), ("ik", 32), ("iw", 8), ("fq", 384), ("fk", 384), ("fv", 384), ("fg", 384), ("ff", 6)
    part, at = {}, 0
    for n, m in names:
        part[n] = w[:, at:at + m]
        at += m
    gate = np.zeros((D, P), np.float32)
    gate[:, 0:6], gate[:, 32:40] = part["ff"], part["iw"]
    shared = tiles(np.concatenate([gate] + [part["ik"]] * 4 + [part["iq"], part["pv"], part["pg"]], 1))
    pairs = lambda names: tiles(np.concatenate([part[n][:, P * i:P * i + P] for i in range(3) for n in names], 1))
    pw = np.zeros((P, 2, P), np.float32)
    for g in range(4):
        o = 64 * (g % 2)
        pw[o:o + 64, g // 2, o:o + 64] = d["pool_w_2"][0, g]
    return {"shared_in": shared, "pool_w": pw, "dsa_in": pairs(("dq", "dk", "dg", "dv")), "fox_in": pairs(("fq", "fk", "fg", "fv")), "out2": d["w_out_2"][0]}


def layout(d):
    return {**layout_ffn(d), **layout_ab(d), **layout_c(d), **layout_2(d)}


def kernel(**inputs):
    import concourse.bacc as _bacc
    from concourse.bass_utils import run_bass_kernel_spmd as _run

    d = {n: np.asarray(v) for n, v in inputs.items()}
    arrays = {n: np.ascontiguousarray(v) for n, v in layout(d).items()}
    nc = _bacc.Bacc("TRN2", target_bir_lowering=False, num_devices=1)
    aps = {n: nc.dram_tensor(n, v.shape, mybir.dt.from_np(v.dtype), kind="ExternalInput").ap() for n, v in arrays.items()}
    aps["out"] = nc.dram_tensor("out", (D, T), F32, kind="ExternalOutput").ap()
    program(nc, aps)
    r = _run(nc, [arrays], core_ids=[0])
    return r.results[0]["out"].T[None]
```
